# Optimizing a Trainium2 kernel written in Bass

```python
import jax, jax.numpy as jnp
from jax import lax
import numpy as np

D_MODEL = 1024
BATCH = 1
SEQ = 512
DEPTH = 1
DEC_BATCH = 8
DEC_SEQ = 1
PAST_LEN = 4096
PAGE_SIZE = 128

N_META = 16
MLA_HEADS = 8
Q_LORA = 384
KV_LORA = 256
NOPE_DIM = 64
ROPE_DIM = 32
V_DIM = 64
ROPE_THETA = 10000.0
Q_BLOCK = 128
RET_HEADS = 4
RET_DK = 128
RET_DV = 128
RET_CHUNK = 128
D_FF = 2816
CONV_W = 3
LN_EPS = 1e-5
RMS_EPS = 1e-6
ALPHA = (2 * DEPTH) ** 0.25
BETA = (8 * DEPTH) ** -0.25
IN_SIZES = (Q_LORA, KV_LORA, ROPE_DIM, RET_HEADS * RET_DK, RET_HEADS * RET_DK, RET_HEADS * RET_DV, RET_HEADS * RET_DV, D_MODEL, D_MODEL)
N_IN = Q_LORA + KV_LORA + ROPE_DIM + 2 * RET_HEADS * RET_DK + 2 * RET_HEADS * RET_DV + 2 * D_MODEL

kernel_name = 'mla_retention_convffn_hybrid_step'

def layer_norm(x, g, b):
    xf = x.astype(jnp.float32)
    mu = jnp.mean(xf, -1, keepdims=True)
    var = jnp.mean(jnp.square(xf - mu), -1, keepdims=True)
    return ((xf - mu) * lax.rsqrt(var + LN_EPS) * g.astype(jnp.float32) + b.astype(jnp.float32)).astype(x.dtype)

def rms_norm(x, g):
    xf = x.astype(jnp.float32)
    return (xf * lax.rsqrt(jnp.mean(jnp.square(xf), -1, keepdims=True) + RMS_EPS) * g.astype(jnp.float32)).astype(x.dtype)

def rope(x, pos):
    half = x.shape[-1] // 2
    inv = ROPE_THETA ** (-jnp.arange(half, dtype=jnp.float32) / half)
    ang = pos[:, None] * inv[None, :]
    cos = jnp.cos(ang)[:, None, :]
    sin = jnp.sin(ang)[:, None, :]
    xf = x.astype(jnp.float32)
    x1, x2 = xf[..., :half], xf[..., half:]
    return jnp.concatenate([x1 * cos - x2 * sin, x2 * cos + x1 * sin], -1).astype(x.dtype)

def mixer_inputs(xn, pos, w_in, q_norm_g, kv_norm_g, w_uq):
    b, t, _ = xn.shape
    h = xn @ w_in
    q_lat, c_raw, kr_raw, rq, rk, rv, rg, ga, gb = jnp.split(h, np.cumsum(IN_SIZES)[:-1].tolist(), axis=-1)
    q = jnp.einsum('btl,lhd->bthd', rms_norm(q_lat, q_norm_g), w_uq)
    q_nope = q[..., :NOPE_DIM]
    q_rope = rope(q[..., NOPE_DIM:], pos)
    c = rms_norm(c_raw, kv_norm_g)
    k_rope = rope(kr_raw[:, :, None, :], pos)[:, :, 0]
    rq = rope(rq.reshape(b, t, RET_HEADS, RET_DK), pos)
    rk = rope(rk.reshape(b, t, RET_HEADS, RET_DK), pos) * (RET_DK ** -0.5)
    rv = rv.reshape(b, t, RET_HEADS, RET_DV)
    return q_nope, q_rope, c, k_rope, rq, rk, rv, rg, ga, gb

def mla_prompt(q_nope, q_rope, c, k_rope, w_uk, w_uv):
    b, l = c.shape[:2]
    k_nope = jnp.einsum('blc,chn->blhn', c, w_uk)
    v = jnp.einsum('blc,chv->blhv', c, w_uv)
    n_blk = -(-l // Q_BLOCK)
    lq = n_blk * Q_BLOCK

    def blocks(q):
        q = jnp.pad(q, ((0, 0), (0, lq - l), (0, 0), (0, 0)))
        return jnp.swapaxes(q.reshape(b, n_blk, Q_BLOCK, q.shape[2], q.shape[3]), 0, 1)

    q_pos = jnp.arange(lq).reshape(n_blk, Q_BLOCK)
    k_pos = jnp.arange(l)
    scale = (NOPE_DIM + ROPE_DIM) ** -0.5

    def attend(args):
        qn, qr, qp = args
        s = jnp.einsum('bqhn,bkhn->bhqk', qn, k_nope) + jnp.einsum('bqhr,bkr->bhqk', qr, k_rope)
        s = jnp.where(k_pos[None, :] <= qp[:, None], s.astype(jnp.float32) * scale, -jnp.inf)
        p = jax.nn.softmax(s, axis=-1).astype(v.dtype)
        return jnp.einsum('bhqk,bkhv->bqhv', p, v)

    o = lax.map(attend, (blocks(q_nope), blocks(q_rope), q_pos))
    return jnp.swapaxes(o, 0, 1).reshape(b, lq, MLA_HEADS * V_DIM)[:, :l]

def mla_sample(q_nope, q_rope, c_new, kr_new, c_past, kr_past, w_uk, w_uv):
    b, t = c_new.shape[:2]
    past = c_past.shape[1]
    scale = (NOPE_DIM + ROPE_DIM) ** -0.5
    q_abs = jnp.einsum('bthn,chn->bthc', q_nope, w_uk)
    s_past = jnp.einsum('bthc,bsc->bhts', q_abs, c_past) + jnp.einsum('bthr,bsr->bhts', q_rope, kr_past)
    s_new = jnp.einsum('bthc,buc->bhtu', q_abs, c_new) + jnp.einsum('bthr,bur->bhtu', q_rope, kr_new)
    causal = jnp.arange(t)[None, :] <= jnp.arange(t)[:, None]
    s_new = jnp.where(causal, s_new.astype(jnp.float32), -jnp.inf)
    s = jnp.concatenate([s_past.astype(jnp.float32), s_new], -1) * scale
    p = jax.nn.softmax(s, axis=-1).astype(c_new.dtype)
    o_lat = jnp.einsum('bhts,bsc->bthc', p[..., :past], c_past) + jnp.einsum('bhtu,buc->bthc', p[..., past:], c_new)
    return jnp.einsum('bthc,chv->bthv', o_lat, w_uv).reshape(b, t, MLA_HEADS * V_DIM)

def ret_log_decay():
    return jnp.log(1.0 - 2.0 ** (-5.0 - jnp.arange(RET_HEADS, dtype=jnp.float32)))

def retention_chunk(state, q, k, v, log_g):
    c = q.shape[2]
    idx = jnp.arange(c, dtype=jnp.float32)
    lg = log_g[:, None, None]
    diff = idx[:, None] - idx[None, :]
    decay = jnp.where(diff >= 0, jnp.exp(jnp.maximum(diff, 0.0) * lg), 0.0)
    inner = jnp.einsum('bhik,bhjk->bhij', q, k) * decay
    o = jnp.einsum('bhij,bhjv->bhiv', inner, v) + jnp.einsum('bhik,bhkv->bhiv', q * jnp.exp((idx[:, None] + 1.0) * lg), state)
    k_dec = k * jnp.exp((c - 1.0 - idx[:, None]) * lg)
    new_state = jnp.exp(c * log_g)[:, None, None] * state + jnp.einsum('bhjk,bhjv->bhkv', k_dec, v)
    return new_state, o

def retention_prompt(rq, rk, rv, log_g):
    b, l = rq.shape[:2]
    pad = (-l) % RET_CHUNK
    n = (l + pad) // RET_CHUNK

    def chunks(x):
        x = jnp.pad(jnp.swapaxes(x.astype(jnp.float32), 1, 2), ((0, 0), (0, 0), (pad, 0), (0, 0)))
        return jnp.moveaxis(x.reshape(b, RET_HEADS, n, RET_CHUNK, x.shape[-1]), 2, 0)

    state0 = jnp.zeros((b, RET_HEADS, RET_DK, RET_DV), jnp.float32)
    state, o = lax.scan(lambda s, xs: retention_chunk(s, xs[0], xs[1], xs[2], log_g), state0, (chunks(rq), chunks(rk), chunks(rv)))
    o = jnp.moveaxis(o, 0, 2).reshape(b, RET_HEADS, n * RET_CHUNK, RET_DV)[:, :, pad:]
    return jnp.swapaxes(o, 1, 2), state

def retention_sample(rq, rk, rv, state, log_g):
    tr = lambda x: jnp.swapaxes(x.astype(jnp.float32), 1, 2)
    new_state, o = retention_chunk(state.astype(jnp.float32), tr(rq), tr(rk), tr(rv), log_g)
    return jnp.swapaxes(o, 1, 2), new_state

def retention_readout(o, rg, gn_g):
    b, t = o.shape[:2]
    mu = jnp.mean(o, -1, keepdims=True)
    var = jnp.mean(jnp.square(o - mu), -1, keepdims=True)
    on = ((o - mu) * lax.rsqrt(var + LN_EPS)).reshape(b, t, RET_HEADS * RET_DV) * gn_g.astype(jnp.float32)
    return (on * jax.nn.silu(rg.astype(jnp.float32))).astype(rg.dtype)

def mixer_merge(attn_o, ret_o, ga, gb, w_attn_out, w_ret_out, w_o):
    m = jax.nn.sigmoid(ga) * (attn_o @ w_attn_out) + jax.nn.sigmoid(gb) * (ret_o @ w_ret_out)
    return m @ w_o

def conv_ffn(x, prev, w_ffn_in, conv_w, conv_b, w_ffn_out):
    t = x.shape[1]
    a, g = jnp.split(x @ w_ffn_in, 2, axis=-1)
    ap = jnp.concatenate([prev.astype(a.dtype), a], axis=1)
    acc = conv_b
    for j in range(CONV_W):
        acc = acc + conv_w[j] * ap[:, j:j + t]
    h = jax.nn.gelu(acc) * g
    return h @ w_ffn_out, ap[:, -(CONV_W - 1):]

def setup_inputs(seed: int = 0) -> dict:
    key = jax.random.key(seed)
    ks = jax.random.split(key, 32)
    n_pages = PAST_LEN // PAGE_SIZE
    n_used = DEC_BATCH * n_pages
    n_phys = n_used + max(1, n_used // 4)
    nrm = lambda k, shape, s: jax.random.normal(k, shape, jnp.float32) * s
    gain = lambda k, shape: 1.0 + nrm(k, shape, 0.02)
    page_table = jax.random.permutation(ks[0], n_phys)[:n_used].reshape(DEC_BATCH, n_pages).astype(jnp.int32)
    hv = MLA_HEADS * V_DIM
    rdv = RET_HEADS * RET_DV
    return {
        'x_prompt': nrm(ks[1], (BATCH, SEQ, D_MODEL), 1.0),
        'x_sample': nrm(ks[2], (DEC_BATCH, DEC_SEQ, D_MODEL), 1.0),
        'cache_kv_latent': nrm(ks[3], (DEPTH, n_phys, PAGE_SIZE, KV_LORA), 1.0),
        'cache_k_rope': nrm(ks[4], (DEPTH, n_phys, PAGE_SIZE, ROPE_DIM), 1.0),
        'state_retention': nrm(ks[5], (DEPTH, DEC_BATCH, RET_HEADS, RET_DK, RET_DV), 0.5),
        'state_ffn_conv': nrm(ks[6], (DEPTH, DEC_BATCH, CONV_W - 1, D_FF), 1.0),
        'page_table': page_table,
        'meta_tokens': nrm(ks[7], (N_META, D_MODEL), 1.0),
        'ln0_g': gain(ks[8], (D_MODEL,)),
        'ln0_b': nrm(ks[9], (D_MODEL,), 0.02),
        'w_in': nrm(ks[10], (DEPTH, D_MODEL, N_IN), D_MODEL ** -0.5),
        'q_norm_g': gain(ks[11], (DEPTH, Q_LORA)),
        'kv_norm_g': gain(ks[12], (DEPTH, KV_LORA)),
        'w_uq': nrm(ks[13], (DEPTH, Q_LORA, MLA_HEADS, NOPE_DIM + ROPE_DIM), Q_LORA ** -0.5),
        'w_uk': nrm(ks[14], (DEPTH, KV_LORA, MLA_HEADS, NOPE_DIM), KV_LORA ** -0.5),
        'w_uv': nrm(ks[15], (DEPTH, KV_LORA, MLA_HEADS, V_DIM), KV_LORA ** -0.5),
        'ret_gn_g': gain(ks[16], (DEPTH, rdv)),
        'w_attn_out': nrm(ks[17], (DEPTH, hv, D_MODEL), hv ** -0.5),
        'w_ret_out': nrm(ks[18], (DEPTH, rdv, D_MODEL), rdv ** -0.5),
        'w_o': nrm(ks[19], (DEPTH, D_MODEL, D_MODEL), BETA * D_MODEL ** -0.5),
        'ln1_g': gain(ks[20], (DEPTH, D_MODEL)),
        'ln1_b': nrm(ks[21], (DEPTH, D_MODEL), 0.02),
        'w_ffn_in': nrm(ks[22], (DEPTH, D_MODEL, 2 * D_FF), D_MODEL ** -0.5),
        'conv_w': nrm(ks[23], (DEPTH, CONV_W, D_FF), CONV_W ** -0.5),
        'conv_b': nrm(ks[24], (DEPTH, D_FF), 0.02),
        'w_ffn_out': nrm(ks[25], (DEPTH, D_FF, D_MODEL), BETA * D_FF ** -0.5),
        'ln2_g': gain(ks[26], (DEPTH, D_MODEL)),
        'ln2_b': nrm(ks[27], (DEPTH, D_MODEL), 0.02),
    }

def reference(x_prompt, x_sample, cache_kv_latent, cache_k_rope, state_retention, state_ffn_conv, page_table, meta_tokens, ln0_g, ln0_b, w_in, q_norm_g, kv_norm_g, w_uq, w_uk, w_uv, ret_gn_g, w_attn_out, w_ret_out, w_o, ln1_g, ln1_b, w_ffn_in, conv_w, conv_b, w_ffn_out, ln2_g, ln2_b):
    b = x_prompt.shape[0]
    db, t = x_sample.shape[:2]
    past = page_table.shape[1] * PAGE_SIZE
    meta = jnp.broadcast_to(meta_tokens.astype(x_prompt.dtype)[None], (b, N_META, D_MODEL))
    xp = layer_norm(jnp.concatenate([meta, x_prompt], axis=1), ln0_g, ln0_b)
    xs = layer_norm(x_sample, ln0_g, ln0_b)
    pos_p = jnp.arange(xp.shape[1], dtype=jnp.float32)
    pos_s = past + jnp.arange(t, dtype=jnp.float32)
    log_g = ret_log_decay()
    conv0 = jnp.zeros((b, CONV_W - 1, D_FF), xp.dtype)
    kv_p, kr_p, rs_p, cs_p = [], [], [], []
    kv_s, kr_s, rs_s, cs_s = [], [], [], []
    for i in range(DEPTH):
        qn, qr, c, kr, rq, rk, rv, rg, ga, gb = mixer_inputs(xp, pos_p, w_in[i], q_norm_g[i], kv_norm_g[i], w_uq[i])
        a_o = mla_prompt(qn, qr, c, kr, w_uk[i], w_uv[i])
        r_o, r_state = retention_prompt(rq, rk, rv, log_g)
        mix = mixer_merge(a_o, retention_readout(r_o, rg, ret_gn_g[i]), ga, gb, w_attn_out[i], w_ret_out[i], w_o[i])
        xp = layer_norm(ALPHA * xp + mix, ln1_g[i], ln1_b[i])
        f, c_state = conv_ffn(xp, conv0, w_ffn_in[i], conv_w[i], conv_b[i], w_ffn_out[i])
        xp = layer_norm(ALPHA * xp + f, ln2_g[i], ln2_b[i])
        kv_p.append(c)
        kr_p.append(kr)
        rs_p.append(r_state.astype(state_retention.dtype))
        cs_p.append(c_state)
        qn, qr, c, kr, rq, rk, rv, rg, ga, gb = mixer_inputs(xs, pos_s, w_in[i], q_norm_g[i], kv_norm_g[i], w_uq[i])
        c_past = cache_kv_latent[i][page_table].reshape(db, past, KV_LORA).astype(c.dtype)
        kr_past = cache_k_rope[i][page_table].reshape(db, past, ROPE_DIM).astype(kr.dtype)
        a_o = mla_sample(qn, qr, c, kr, c_past, kr_past, w_uk[i], w_uv[i])
        r_o, r_state = retention_sample(rq, rk, rv, state_retention[i], log_g)
        mix = mixer_merge(a_o, retention_readout(r_o, rg, ret_gn_g[i]), ga, gb, w_attn_out[i], w_ret_out[i], w_o[i])
        xs = layer_norm(ALPHA * xs + mix, ln1_g[i], ln1_b[i])
        f, c_state = conv_ffn(xs, state_ffn_conv[i], w_ffn_in[i], conv_w[i], conv_b[i], w_ffn_out[i])
        xs = layer_norm(ALPHA * xs + f, ln2_g[i], ln2_b[i])
        kv_s.append(c)
        kr_s.append(kr)
        rs_s.append(r_state.astype(state_retention.dtype))
        cs_s.append(c_state.astype(state_ffn_conv.dtype))
    y_prompt = xp[:, N_META:]
    y_sample = xs
    return (y_prompt, y_sample, jnp.stack(kv_p), jnp.stack(kr_p), jnp.stack(rs_p), jnp.stack(cs_p), jnp.stack(kv_s), jnp.stack(kr_s), jnp.stack(rs_s), jnp.stack(cs_s))


_drawn_inputs = setup_inputs


def setup_inputs(seed=0):
    import zlib

    import numpy as np

    out = dict(_drawn_inputs(seed))
    spreads = {}
    factors = {'cache_kv_latent': 7.974,
     'cache_k_rope': 8.0,
     'q_norm_g': 8.0,
     'kv_norm_g': 2.955,
     'ret_gn_g': 25.202,
     'ln1_g': 2.807,
     'conv_b': 8.0,
     'ln2_g': 7.838,
     'ln2_b': 8.728,
     'ln1_b': 6.154}
    for name, (base, spread) in spreads.items():
        noise = np.random.default_rng([zlib.crc32(name.encode()), seed]).standard_normal(out[name].shape)
        drawn = base * np.exp(spread * noise) if base else spread * noise
        out[name] = __import__('jax').numpy.asarray(drawn.astype(out[name].dtype))
    for name, factor in factors.items():
        out[name] = (out[name] * factor).astype(out[name].dtype)
    return out
```

```python
from contextlib import ExitStack, contextmanager

import numpy as np
import concourse.bass as bass
from concourse import mybir

ALU = mybir.AluOpType
ACT = mybir.ActivationFunctionType
F32 = mybir.dt.float32
F32R = mybir.dt.float32r
I32 = mybir.dt.int32
AX = mybir.AxisListType.X

P = 128
D = 1024
KT = D // P
SEQ, META, DEC = 512, 16, 8
COLS = DEC + META + SEQ
HALF = COLS // 2
T0 = DEC + META
NT = 5
HEADS, NOPE, ROPE, VD = 8, 64, 32, 64
QD_ = NOPE + ROPE
QL, KVL = 384, 256
RH, RD = 4, 128
DFF = 2816
FT = DFF // P
PAGE, NPAGES = 128, 32
PAST = PAGE * NPAGES
NCH = 8
ALPHA = 2.0 ** 0.25
LN_EPS, RMS_EPS = 1e-5, 1e-6
SCALE = float(QD_) ** -0.5
NEG = -1e30
OFF_Q, OFF_C, OFF_KR, OFF_RQ = 0, 384, 640, 672
OFF_RK, OFF_RV, OFF_RG = 1184, 1696, 2208
OFF_GA, OFF_GB = 2720, 3744
SLOT_W = 256
FFN_TILES = (12, 10)


def tile_cols(t):
    return (0, T0) if t == 0 else (T0 + P * (t - 1), P)


def shape_constants():
    f32 = np.float32
    pos = np.concatenate([np.full(DEC, PAST, f32), np.arange(META + SEQ, dtype=f32)])

    def rope_rows(half):
        inv = (10000.0 ** (-np.arange(half, dtype=np.float64) / half)).astype(f32)
        ang = (pos[None, :] * inv[:, None]).astype(f32).astype(np.float64)
        c, s = np.cos(ang), np.sin(ang)
        return np.concatenate([c, c]).astype(f32), np.concatenate([-s, s]).astype(f32)

    rc, rs = rope_rows(RD // 2)
    mc, ms = rope_rows(ROPE // 2)
    c = {"ret_rope": np.stack([rc, rs], 1), "mla_rope": np.concatenate([mc, ms], 0)}
    lg = np.log(1.0 - 2.0 ** (-5.0 - np.arange(RH)))
    i = np.arange(P)
    head = np.zeros((P, RH, 2 * P + T0 + 8), f32)
    for h in range(RH):
        d = i[None, :] - i[:, None]
        head[:, h, 0:P] = np.where(d >= 0, np.exp(np.maximum(d, 0) * lg[h]), 0.0)
        head[:, h, P:2 * P] = np.exp((i[None, :] + 1.0) * lg[h])
        m = head[:, h, 2 * P:2 * P + T0]
        m[DEC:T0, DEC:T0] = head[0:META, h, 0:META]
        head[:, h, 2 * P + T0] = np.exp((P - 1.0 - i) * lg[h])
        head[DEC:T0, h, 2 * P + T0 + 1] = np.exp((META - 1.0 - np.arange(META)) * lg[h])
        head[:, h, 2 * P + T0 + 2] = np.exp(lg[h])
        head[:, h, 2 * P + T0 + 3] = np.exp(P * lg[h])
    c["ret_head"] = head
    sq = np.zeros((P, 5, P), f32)
    sq[:, 0] = np.eye(P)
    sq[:, 1] = 1.0
    sq[:, 2] = 1.0 / P
    sq[:, 3] = np.eye(P) - 1.0 / P
    sq[:, 4] = np.where(i[None, :] <= i[:, None], 0.0, NEG)
    c["square"] = sq
    m = np.zeros((P, 58), f32)
    jj = np.arange(META)
    m[DEC:T0, 0:META] = np.where(jj[None, :] <= jj[:, None], 0.0, NEG)
    m[0:DEC, 16:24] = np.where(np.eye(DEC) > 0, 0.0, NEG)
    m[:, 24] = i % 4
    m[:, 25] = 8 * (i % 4)
    for g in range(4):
        for j in range(2 * HEADS):
            m[32 * g + j, 26 + HEADS * g + j % HEADS] = 1.0
    c["small"] = m
    return c


class Count:

    def __init__(self, sem, step=1, start=0):
        self.sem, self.step, self.n, self.term, self.inside = sem, step, start, 0, False

    def add(self, k=1):
        assert not k or not Count.looping or self.inside, f"not declared in the loop: {self.sem}"
        self.n += k

    def after(self, k=1):
        self.add(k)
        assert self.n > 0, f"a wait against zero: {self.sem}"
        return self.term + self.n * self.step

    looping = False


@contextmanager
def loop(eng, count, per):
    with eng.Fori(0, count) as i:
        begun = {}
        for c, k in per.items():
            begun[c], c.term, c.inside = c.n, i * (k * c.step), True
        Count.looping = True
        yield i
        Count.looping = False
        bad = {str(c.sem): (c.n - begun[c], k) for c, k in per.items() if c.n - begun[c] != k}
        assert not bad, f"counts per iteration differ (found, declared): {bad}"
    for c, k in per.items():
        c.n += (count - 1) * k
        c.term, c.inside = 0, False


def build(nc, ins, outs):
    ctx = ExitStack()
    with ctx:
        consts = {k: nc.inline_tensor(v, name=k + "_const") for k, v in shape_constants().items()}
        sems = {}

        def sem(name):
            sems[name] = ctx.enter_context(nc.semaphore(name))
            return sems[name]

        base = -(-nc.sbuf_base // 32) * 32
        top = [0]

        def fixed(name, shape, dt=F32):
            n = int(np.prod(shape[1:])) * 4
            t = nc.alloc_sbuf_tensor_at(name, shape, dt, offset=base + top[0])
            top[0] += -(-n // 32) * 32
            return t

        XH = fixed("x_hi", [P, KT, COLS], F32R)
        XL = fixed("x_lo", [P, KT, COLS], F32R)
        RAW = fixed("w_raw", [P, 2, 8, SLOT_W])
        WH = fixed("w_hi", [P, 2, 8, SLOT_W], F32R)
        WL = fixed("w_lo", [P, 2, 8, SLOT_W], F32R)
        ab_off = top[0]
        AT = fixed("attn_T", [P, 4, COLS])
        BT = fixed("ret_T", [P, 4, COLS])
        TT = nc.alloc_sbuf_tensor_at("sum_T", [P, KT, COLS], F32, offset=base + ab_off)
        SQ = fixed("square_consts", [P, 5, P])
        SMALL = fixed("small_consts", [P, 58])
        VT = fixed("vectors_T", [P, 41])
        CV = fixed("conv_T", [P, 88])
        PV = fixed("conv_prev_T", [P, FT, 2 * DEC])
        CSP = fixed("conv_last_T", [P, FT, 2])
        CSS = fixed("conv_new_T", [P, 2, FT, 4])
        QS = fixed("q_sample", [P, HEADS, DEC])
        EPS = fixed("eps", [P, 2])
        STAT = fixed("stats", [P, NT, 2, 6])
        MV = fixed("mean_var", [P, NT, 2])
        SDV = fixed("std", [P, NT])
        RSV = fixed("rstd", [P, NT])
        SMX = fixed("softmax_small", [P, 32])
        PTI = fixed("page_table_rows", [P, DEC], I32)
        IDX = fixed("page_rows", [P, DEC, NCH + 1], I32)
        IDB = fixed("page_rows_now", [P, 2, NCH + 1], I32)
        CN8 = fixed("latent_new_T", [P, 2, DEC])
        KR8 = fixed("rope_new_T", [P, DEC])
        arena = top[0]

        def at(name, off, shape, dt=F32):
            n = int(np.prod(shape[1:])) * 4
            assert arena + off + n <= nc.sbuf_usable_end - base, (name, arena + off + n, nc.sbuf_usable_end - base)
            assert off % 32 == 0, name
            return nc.alloc_sbuf_tensor_at(name, shape, dt, offset=base + arena + off)

        def plan(start, *items):
            got, off = [], start
            for name, shape, *dt in items:
                got.append(at(name, off, shape, *dt))
                off += -(-int(np.prod(shape[1:])) * 4 // 32) * 32
            return got, off

        IDENT, ONES, MEAN, CENTRE, CAUSAL = (SQ[:, j, :] for j in range(5))
        (XK, XF, GB0), e0 = plan(0, ("x_tok", [P, NT, D]), ("x_feat", [P, KT, COLS]), ("ln0_gb", [P, 2, D]))
        (VR, CN), _ = plan(e0 + 21760, ("vec_rows", [P, 2, P]), ("conv_rows", [16, 2, 1408]))
        (RR, HC, RQ, RK, RV, RG, SW, TP, RQD, KDEC, VTOK, KTOK0, VBLK, INT, IN0, RS, ST, OT, OC, OSQ,
         ORS), e1 = plan(
            e0, ("ret_rope", [P, 2, COLS]), ("ret_head", [P, RH, 2 * P + T0 + 8]), ("rq", [P, COLS]),
            ("rk", [P, COLS]), ("rv", [P, COLS]), ("rg", [P, COLS]), ("rot_swap", [P, COLS]),
            ("rot_tmp", [P, COLS]), ("rq_dec", [P, 4, P]), ("k_dec", [P, NT, P]), ("v_tok", [P, NT, P]),
            ("k_tok0", [P, P]), ("v_blocks", [P, DEC, P]), ("inner", [P, 4, P]), ("inner0", [P, T0]),
            ("states", [P, NT, P]), ("state_s", [P, DEC, P]), ("o_T", [P, COLS]), ("o_cent", [P, COLS]),
            ("o_sq", [P, COLS]), ("o_rstd", [P, COLS]))
        (CTOK, QN, CNT, MR, KRT, KRO, UQ, UK, TQ, QT, KTB, VB, UKT, SG), e2 = plan(
            32768, ("c_tok", [P, NT, KVL]), ("q_lat", [P, 3, COLS]), ("c_lat", [P, 2, COLS]),
            ("mla_rope", [P, COLS]), ("k_rope_T", [P, COLS]), ("k_rope_tok", [P, NT, ROPE]),
            ("w_uq", [P, 3, 2, P]), ("w_uk", [P, 2, P]), ("rope_tmp", [P, 2, COLS]), ("q_heads", [P, 2, COLS]),
            ("k_heads", [P, 2, COLS]), ("v_pair", [P, NT, P]), ("w_uk_T", [P, 2, 2, P]),
            ("gate_out", [P, 2, 2, COLS]))
        (QSQ, RIN), _ = plan(e2, ("lat_sq", [P, 3, COLS]), ("lat_rms", [P, COLS]))
        (EX, SD, PTS), e3 = plan(e2, ("probs", [P, 2, 528]), ("diag", [P, 2, P]), ("probs_T", [P, 2, NT, P]))
        (PGC,), _ = plan(0, ("pages_c", [P, 2, NPAGES, KVL]))
        (CTX, QAB, UV), _ = plan(e3, ("c_tok0", [T0, KVL]), ("q_abs", [P, 2, DEC, HEADS]), ("w_uv", [P, 2, 512]))
        assert PGC.shape[2] * KVL * 4 == 32768
        (PGR, RTT, SCB, PB, PHL, QRB, SSM, OL, SPART, OPART, QB), e4 = plan(
            65536, ("pages_r", [P, 2, NPAGES, ROPE]), ("rope_T", [P, NCH, P]),
            ("scores", [P, 2, 33, HEADS]), ("p_sample", [P, 2, 33, HEADS]), ("p_parts", [P, 32, 2 * HEADS], F32R),
            ("q_rope_blocks", [P, DEC, 4, HEADS]), ("sm", [P, 2, 40]), ("o_lat", [P, 2, HEADS, DEC]),
            ("score_parts", [P, 2, 512]), ("out_parts", [2 * HEADS, KVL]), ("q_parts", [P, 2, 224], F32R))
        CTH, CTL, PGH, PGL = (nc.alloc_sbuf_tensor_at(name, [P, 2, 4, KVL], F32R, offset=base + j * 2 * 4 * KVL * 4)
                              for j, name in enumerate(("pages_T_hi", "pages_T_lo", "pages_hi", "pages_lo")))
        assert 4 * 2 * 4 * KVL * 4 <= 2 * KT * COLS * 4
        PHI = [PGH[:, 0], PGH[:, 1], WH[:, 0, 4:8, :], WH[:, 1, 4:8, :]]
        PLO = [PGL[:, 0], PGL[:, 1], WL[:, 0, 4:8, :], WL[:, 1, 4:8, :]]
        assert e4 <= e3
        (MH, ML, AH, AL, BH, BL, GG), e5 = plan(
            0, ("m_hi", [P, KT, COLS], F32R), ("m_lo", [P, KT, COLS], F32R), ("attn_hi", [P, 4, COLS], F32R),
            ("attn_lo", [P, 4, COLS], F32R), ("ret_hi", [P, 4, COLS], F32R), ("ret_lo", [P, 4, COLS], F32R),
            ("gates", [P, 2, 2, COLS]))
        YK = at("y_tok", 84000, [P, NT, D])
        assert e5 <= 84000
        XF1 = at("x1_feat", 0, [P, KT, COLS])
        GB1 = at("ln1_gb", 68608, [P, 2, D])
        NH = FFN_TILES[0]
        (FH, FL, AB, ACC, GL, HF), e6 = plan(
            0, ("ffn_hi", [P, NH, COLS], F32R), ("ffn_lo", [P, NH, COLS], F32R), ("a_rows", [P, 2, 2 + META + SEQ]),
            ("conv_acc", [P, 2, COLS]), ("gelu", [P, 2, COLS]), ("h_f32", [P, 2, COLS]))
        (GB2, CST), e7 = plan(e6, ("ln2_gb", [P, 2, D]), ("conv_out", [P, 3, P]))
        assert e7 <= 84000, e7
        assert KT * COLS * 4 == 2 * 4 * COLS * 4

        PS = ctx.enter_context(nc.psum_tensor("PS", [P, 8, 512], F32))

        def pair(p, lo=0, hi=P):
            return PS[lo:hi, 2 * p:2 * p + 2, 0:HALF]

        def two(ap):
            return ap.rearrange("p (a b) -> p a b", a=2)

        x_scr = nc.dram_tensor("x_tok_scratch", (NT, P, D), F32, kind="Internal").ap()
        g_scr = nc.dram_tensor("gate_scratch", (2, KT, P, COLS), F32, kind="Internal").ap()

        s_free = [sem(f"psum_free{p}") for p in range(4)]
        s_fa = [sem(f"psum_full_for_act{p}") for p in range(4)]
        s_fd = [sem(f"psum_full_for_dve{p}") for p in range(4)]
        s_act, s_dve, s_pool = sem("act_own_order"), sem("dve_own_order"), sem("pool_own_order")
        s_win = [sem(f"weights_landed{j}") for j in range(2)]
        s_whi, s_wsplit, s_done = sem("weights_hi"), sem("weights_split"), sem("slot_done")
        s_x = [sem(f"x_landed{t}") for t in range(NT)]
        names = ("consts_landed consts2_landed vectors_T_ready stats_ready std_ready x_normed ln_turned x_hi_ready "
                 "x_split x_tok_ready x_tok_stored swap_ready k_feat q_feat g_ready head_done sn_ready "
                 "state_landed state_stored inner_ready tok_ready ot_ready sq_ready sd_ready final_state_stored "
                 "lat_copied lat_sq lat_sd lat_normed tok_out_ready out_stored head_w_landed proj_done q_heads_ready "
                 "v_ready uk_T_ready qabs_ready scores_full nmax_ready exp_ready probs_ready probs_turned "
                 "pt_act pt_dve attn_done gate_full gate_sig gate_stored0 gate_stored1 kr_landed idx_in gate_free0 gate_free1 idx_ready idx_now "
                 "rope_pages0 rope_pages1 rope_turned rope_back chunk_turned ct_act ct_dve chunk_scored q_parts parts_back page_hi page_split p_hi p_split o_parts lat_turned s_full s_bank_free mx_ready mx_turned "
                 "dg_ready mx_spread shifted exp_s sum_ready sum_spread rs_ready pv_chunk pv_full olat_ready a_s_full "
                 "a_done ab_hi ab_split gates_back gates_used m_added m_hi m_split y_back back_turned back_taken gb_landed "
                 "y_scaled conv_first conv_acc gelu_done h_ready h_hi h_split f_taken cst_ready cst_turned y_out "
                 "go_on rows_zeroed qrb_ready").split()
        for n in names:
            sem(n)
        s_pg = [[sem(f"pages_landed{j}_{c}") for c in range(NCH)] for j in range(2)]
        S = sems

        w_in = ins["w_in"][0].rearrange("(k p) n -> p k n", p=P)
        w_ga = w_in
        w_ffi = ins["w_ffn_in"][0].rearrange("(k p) n -> p k n", p=P)
        w_ffo = ins["w_ffn_out"][0].rearrange("(k p) n -> p k n", p=P)
        w_ao = ins["w_attn_out"][0].rearrange("(k p) n -> p k n", p=P)
        w_ro = ins["w_ret_out"][0].rearrange("(k p) n -> p k n", p=P)
        w_o = ins["w_o"][0].rearrange("(k p) n -> p k n", p=P)
        w_uq = ins["w_uq"][0].rearrange("(k p) h n -> p k h n", p=P)
        w_uk = ins["w_uk"][0].rearrange("(k p) h n -> p k (h n)", p=P)
        w_uv = ins["w_uv"][0].rearrange("(k p) h n -> p k (h n)", p=P)

        N_RET = 0
        N_LAT = N_RET + 2 * RH
        N_GATE = N_LAT + 3
        N_MERGE = N_GATE + 8
        N_O = N_MERGE + 8
        N_F1 = N_O + 4
        N_F1O = N_F1 + FFN_TILES[0]
        N_F2 = N_F1O + 8
        N_F2O = N_F2 + FFN_TILES[1]
        N_END = N_F2O + 8


        def evac_cols(t):
            c0, r = tile_cols(t)
            return slice(c0, c0 + r), r

        def css(f):
            return CSS[:, :, bass.ds(f, 1), :].rearrange("p k f r -> p k (f r)")

        block = ctx.enter_context(nc.Block())

        @block.sync
        def _(sp):
            raw_free = Count(S["weights_split"])
            state_stored, sn, inner = Count(S["state_stored"], 16), Count(S["sn_ready"]), Count(S["inner_ready"])
            final_stored = Count(S["final_state_stored"], 16)
            out_stored = Count(S["out_stored"], 16)

            def slot(par, parts, first=False):
                if not first:
                    sp.wait_ge(raw_free.sem, raw_free.after())
                for dst, src in parts:
                    sp.dma_start(dst, src).then_inc(s_win[par], 16)

            def cols_slot(n, w, c0, c1, nk=8, k0=0, first=False):
                par = n % 2
                slot(par, [(RAW[:, par, 0:nk, 0:P], w[:, k0:k0 + nk, bass.ds(c0, P)]),
                           (RAW[:, par, 0:nk, P:2 * P], w[:, k0:k0 + nk, bass.ds(c1, P)])], first)

            sp.dma_start(XK[0:DEC, 0, :], ins["x_sample"][:, 0, :]).then_inc(s_x[0], 16)
            sp.dma_start(XK[DEC:T0, 0, :], ins["meta_tokens"]).then_inc(s_x[0], 16)
            for t in range(1, NT):
                sp.dma_start(XK[:, t, :], ins["x_prompt"][0, P * (t - 1):P * t, :]).then_inc(s_x[t], 16)
            sp.dma_start(SQ[:], consts["square"].ap()).then_inc(S["consts_landed"], 16)
            row = 0
            for name, k in (("ln0_g", 8), ("ln0_b", 8), ("ln1_g", 8), ("ln1_b", 8), ("q_norm_g", 3),
                            ("kv_norm_g", 2), ("ret_gn_g", 4)):
                v = ins[name] if name.startswith("ln0") else ins[name][0]
                sp.dma_start(VR[row:row + k, 0, :], v.rearrange("(k p) -> k p", p=P)).then_inc(S["consts_landed"], 16)
                row += k
            for j in range(3):
                sp.dma_start(VR[j * FT:(j + 1) * FT, 1, :],
                             ins["conv_w"][0, j].rearrange("(k p) -> k p", p=P)).then_inc(S["consts_landed"], 16)
            sp.dma_start(VR[3 * FT:4 * FT, 1, :],
                         ins["conv_b"][0].rearrange("(k p) -> k p", p=P)).then_inc(S["consts_landed"], 16)
            cols_slot(0, w_in, OFF_RK, OFF_RV, first=True)
            cols_slot(1, w_in, OFF_RQ, OFF_RG, first=True)
            c2 = S["consts2_landed"]
            sp.dma_start(RR[:], consts["ret_rope"].ap()).then_inc(c2, 16)
            sp.dma_start(HC[:], consts["ret_head"].ap()).then_inc(c2, 16)
            sp.dma_start(SMALL[:], consts["small"].ap()).then_inc(c2, 16)
            sp.dma_start(CN[:].rearrange("p a b -> p (a b)"),
                         ins["state_ffn_conv"][0].rearrange("b j f -> (b j) f")).then_inc(c2, 16)
            for j, name in enumerate(("ln0_g", "ln0_b")):
                sp.dma_start(GB0[:, j, :], ins[name].partition_broadcast(P)).then_inc(c2, 16)
            for q in range(4):
                sp.dma_start(PTI[q:P:4, :], ins["page_table"].rearrange("b j -> j b"),
                             allow_slow_non_contiguous=True).then_inc(c2, 16)
            st_dram = ins["state_retention"][0].rearrange("b h k v -> k b h v")
            sto_dram = outs[8][0].rearrange("b h k v -> k b h v")

            def state_load(h):
                sp.dma_start(ST[:], st_dram[:, :, bass.ds(h, 1), :].rearrange("k b h v -> k b (h v)")
                             ).then_inc(S["state_landed"], 16)

            def state_store(h):
                sp.wait_ge(inner.sem, inner.after())
                sp.dma_start(outs[4][0, 0, bass.ds(h, 1)].rearrange("h k v -> k (h v)"), RS[:, NT - 1, :]
                             ).then_inc(S["final_state_stored"], 16)
                sp.wait_ge(sn.sem, sn.after())
                sp.dma_start(sto_dram[:, :, bass.ds(h, 1), :].rearrange("k b h v -> k b (h v)"), ST[:]
                             ).then_inc(S["state_stored"], 16)
                sp.wait_ge(state_stored.sem, state_stored.after())

            state_load(0)
            ot = Count(S["ot_ready"])
            with loop(sp, RH - 1, {raw_free: 2, ot: 1, inner: 1, sn: 1, state_stored: 1}) as i:
                cols_slot(0, w_in, i * P + (OFF_RK + P), i * P + (OFF_RV + P))
                cols_slot(1, w_in, i * P + (OFF_RQ + P), i * P + (OFF_RG + P))
                state_store(i)
                sp.wait_ge(ot.sem, ot.after())
                state_load(i + 1)
            cols_slot(N_LAT, w_in, OFF_Q, OFF_Q + P)
            par = (N_LAT + 1) % 2
            slot(par, [(RAW[:, par, :, 0:P], w_in[:, :, OFF_Q + 2 * P:OFF_Q + 3 * P]),
                       (RAW[:, par, :, P:P + 96], w_in[:, :, OFF_KR - 64:OFF_KR + ROPE])])
            sp.dma_start(RAW[:, par, :, P + 96:P + 112], w_in[:, :, OFF_KR + 16:OFF_KR + 32]).then_inc(S["kr_landed"], 16)
            sp.dma_start(RAW[:, par, :, P + 112:P + 128], w_in[:, :, OFF_KR:OFF_KR + 16]).then_inc(S["kr_landed"], 16)
            state_store(RH - 1)
            sp.wait_ge(final_stored.sem, final_stored.after(RH))
            cols_slot(N_LAT + 2, w_in, OFF_C, OFF_C + P)
            head_done = Count(S["head_done"])
            sp.wait_ge(head_done.sem, head_done.after(RH))
            sp.dma_start(MR[64:P, :], consts["mla_rope"].ap()).then_inc(S["idx_in"], 16)
            sp.dma_start(UV[:], w_uv).then_inc(S["idx_in"], 16)

            def head_weights(p):
                hw = S["head_w_landed"]
                for hh in range(2):
                    src = w_uq[:, :, bass.ds(p * 2 + hh, 1), :].rearrange("p k h n -> p k (h n)")
                    sp.dma_start(UQ[:, :, hh, 0:QD_], src[:, :, 0:QD_]).then_inc(hw, 16)
                    sp.dma_start(UQ[:, :, hh, QD_:QD_ + 16], src[:, :, QD_ - 16:QD_]).then_inc(hw, 16)
                    sp.dma_start(UQ[:, :, hh, QD_ + 16:P], src[:, :, NOPE:NOPE + 16]).then_inc(hw, 16)
                sp.dma_start(UK[:], w_uk[:, :, bass.ds(p * P, P)]).then_inc(hw, 16)

            head_weights(0)
            tok_out = Count(S["tok_out_ready"])

            def store(dst, src):
                sp.dma_start(dst, src).then_inc(S["out_stored"], 16)

            proj_done = Count(S["proj_done"])
            cols_slot(N_GATE, w_in, OFF_GA, OFF_GA + P)
            cols_slot(N_GATE + 1, w_in, OFF_GB, OFF_GB + P)
            sp.wait_ge(tok_out.sem, tok_out.after())
            store(outs[2][0, 0, 0:META, :], CTX[DEC:T0, :])
            store(outs[2][0, 0, META:, :].rearrange("(t p) c -> p t c", p=P), CTOK[:, 1:NT, :])
            store(outs[6][0, :, 0, :], CTX[0:DEC, :])
            store(outs[3][0, 0, 0:META, :], KRO[DEC:T0, 0, :])
            store(outs[3][0, 0, META:, :].rearrange("(t p) c -> p t c", p=P), KRO[:, 1:NT, :])
            store(outs[7][0, :, 0, :], KRO[0:DEC, 0, :])
            store(outs[9][0, :, 0, :], ins["state_ffn_conv"][0, :, 1, :])
            with loop(sp, 3, {raw_free: 2, proj_done: 1}) as i:
                sp.wait_ge(proj_done.sem, proj_done.after())
                head_weights(i + 1)
                cols_slot(N_GATE, w_in, i * 2 * P + (OFF_GA + 2 * P), i * 2 * P + (OFF_GA + 3 * P))
                cols_slot(N_GATE + 1, w_in, i * 2 * P + (OFF_GB + 2 * P), i * 2 * P + (OFF_GB + 3 * P))
            sp.wait_ge(out_stored.sem, out_stored.after(7))
            cols_slot(N_MERGE, w_ao, 0, P, 4)
            cols_slot(N_MERGE + 1, w_ro, 0, P, 4)
            a_done = Count(S["a_done"])
            sp.wait_ge(a_done.sem, a_done.after())
            m_split = Count(S["m_split"])

            def gates_back(jj):
                for s in range(2):
                    sp.dma_start(GG[:, s, :, :], g_scr[s, bass.ds(jj * 2, 2)].rearrange("m p c -> p m c")
                                 ).then_inc(S["gates_back"], 16)

            for j in range(2):
                sp.wait_ge(S[f"gate_stored{j}"], 16 * (1 + 4))
            x_stored = Count(S["x_tok_stored"], 16)
            sp.wait_ge(x_stored.sem, x_stored.after(NT))
            gates_back(0)
            sp.dma_start(YK[:, 1:NT, :], x_scr[1:NT].rearrange("t p d -> p t d")).then_inc(S["y_back"], 16)
            sp.dma_start(YK[0:T0, 0, :], x_scr[0, 0:T0, :]).then_inc(S["y_back"], 16)
            with loop(sp, 3, {raw_free: 2, m_split: 1}) as i:
                cols_slot(N_MERGE, w_ao, i * 2 * P + 2 * P, i * 2 * P + 3 * P, 4)
                cols_slot(N_MERGE + 1, w_ro, i * 2 * P + 2 * P, i * 2 * P + 3 * P, 4)
                sp.wait_ge(m_split.sem, m_split.after())
                gates_back(i + 1)
            with loop(sp, 2, {raw_free: 2}) as i:
                cols_slot(N_O, w_o, i * 4 * P, i * 4 * P + P)
                cols_slot(N_O + 1, w_o, i * 4 * P + 2 * P, i * 4 * P + 3 * P)
            sp.wait_ge(m_split.sem, m_split.after())
            for j, name in enumerate(("ln1_g", "ln1_b")):
                sp.dma_start(GB1[:, j, :], ins[name][0].partition_broadcast(P)).then_inc(S["gb_landed"], 16)
            f0 = 0
            for part, nf in enumerate(FFN_TILES):
                na = (N_F1, N_F2)[part]
                with loop(sp, nf // 2, {raw_free: 2}) as i:
                    cols_slot(na, w_ffi, i * 2 * P + f0 * P, i * 2 * P + (f0 + 1) * P)
                    cols_slot(na + 1, w_ffi, i * 2 * P + (DFF + f0 * P), i * 2 * P + (DFF + (f0 + 1) * P))
                no = (N_F1O, N_F2O)[part]
                hk = nf // 2
                with loop(sp, 4, {raw_free: 2}) as i:
                    cols_slot(no, w_ffo, i * 2 * P, i * 2 * P + P, hk, f0)
                    cols_slot(no + 1, w_ffo, i * 2 * P, i * 2 * P + P, hk, f0 + hk)
                if part == 0:
                    sp.wait_ge(S["x_tok_ready"], NT)
                    for j, name in enumerate(("ln2_g", "ln2_b")):
                        sp.dma_start(GB2[:, j, :], ins[name][0].partition_broadcast(P)).then_inc(S["gb_landed"], 16)
                f0 += nf
            cst = Count(S["cst_ready"])
            sp.wait_ge(cst.sem, cst.after(3))
            for j in range(2):
                store(outs[5][0, 0, j].rearrange("(f p) -> f p", p=P), CST[j:2 * FT:2, 0, :])
            for b in range(DEC):
                k, r = divmod(b, 4)
                store(outs[9][0, b, 1].rearrange("(f p) -> f p", p=P), CST[r:4 * FT:4, 1 + k, :])
            y_out = Count(S["y_out"])
            sp.wait_ge(y_out.sem, y_out.after())
            store(outs[1][:, 0, :], YK[0:DEC, 0, :])
            for t in range(1, NT):
                sp.wait_ge(y_out.sem, y_out.after())
                store(outs[0][0, P * (t - 1):P * t, :], YK[:, t, :])
            sp.wait_ge(out_stored.sem, out_stored.after(2 + DEC + NT))
            assert out_stored.n == 7 + 2 + DEC + NT

        @block.gpsimd
        def _(pool):
            chain = Count(S["pool_own_order"])
            c2 = Count(S["consts2_landed"], 16)
            turned = Count(S["ln_turned"])
            split = Count(S["x_split"])
            pool.wait_ge(c2.sem, c2.after(10))
            for t in range(NT):
                r = tile_cols(t)[1]
                pool.wait_ge(turned.sem, turned.after())
                nc.gpsimd.tensor_tensor(XK[0:r, t, :], XK[0:r, t, :], GB0[0:r, 0, :], ALU.mult).then_inc(chain.sem, 1)
                pool.wait_ge(chain.sem, chain.after())
                nc.gpsimd.tensor_tensor(XK[0:r, t, :], XK[0:r, t, :], GB0[0:r, 1, :], ALU.add).then_inc(chain.sem, 1)
                pool.wait_ge(chain.sem, chain.after())
                pool.dma_start(x_scr[t, 0:r, :], XK[0:r, t, :]).then_inc(S["x_tok_stored"], 16)
            stored = Count(S["x_tok_stored"], 16)
            pool.wait_ge(stored.sem, stored.after(NT))
            pool.wait_ge(split.sem, split.after(NT))
            lat_rows = ins["cache_kv_latent"][0].rearrange("n (q r) c -> (n q) (r c)", q=32)
            rope_rows = ins["cache_k_rope"][0].rearrange("n (q r) c -> (n q) (r c)", q=4)

            def rows_of(par, b):
                nc.gpsimd.tensor_copy(
                    IDB[:, par, :], IDX[:, bass.ds(b, 1), :].rearrange("p b c -> p (b c)")).then_inc(chain.sem, 1)
                pool.wait_ge(chain.sem, chain.after())

            def chunk(par, c):
                nc.gpsimd.indirect_dma_start(
                    out=PGC[:, par, 4 * c:4 * c + 4, :].rearrange("p r c -> p (r c)"), out_offset=None,
                    in_=lat_rows, in_offset=bass.IndirectOffsetOnAxis(ap=IDB[:, par, c:c + 1], axis=0)
                ).then_inc(s_pg[par][c], 16)

            def rope_page(par):
                nc.gpsimd.indirect_dma_start(
                    out=PGR[:, par, :, :].rearrange("p r c -> p (r c)"), out_offset=None, in_=rope_rows,
                    in_offset=bass.IndirectOffsetOnAxis(ap=IDB[:, par, NCH:NCH + 1], axis=0)
                ).then_inc(S[f"rope_pages{par}"], 16)

            idx = Count(S["idx_ready"])
            pool.wait_ge(idx.sem, idx.after())
            rows_of(0, 0)
            for c in range(NCH):
                chunk(0, c)
            attn_done = Count(S["attn_done"])
            pool.wait_ge(attn_done.sem, attn_done.after(4))
            for j in range(2):
                pool.wait_ge(S[f"gate_stored{j}"], 16 * (1 + 4))
            rope_page(0)
            rows_of(1, 1)
            rope_page(1)
            for c in range(NCH):
                chunk(1, c)
            s_full, page_split = Count(S["s_full"]), Count(S["page_split"])
            with loop(pool, 3, {chain: 2, s_full: 2, page_split: 2 * NCH}) as i:
                for par in range(2):
                    pool.wait_ge(s_full.sem, s_full.after())
                    rows_of(par, i * 2 + (2 + par))
                    pool.sem_inc(S["go_on"])
                    rope_page(par)
                    for c in range(NCH):
                        pool.wait_ge(page_split.sem, page_split.after())
                        pool.sem_inc(S["go_on"])
                        chunk(par, c)

            gb = Count(S["gb_landed"], 16)
            pool.wait_ge(gb.sem, gb.after(2))
            for t in range(NT):
                r = tile_cols(t)[1]
                pool.wait_ge(turned.sem, turned.after())
                nc.gpsimd.tensor_tensor(YK[0:r, t, :], YK[0:r, t, :], GB1[0:r, 0, :], ALU.mult).then_inc(chain.sem, 1)
                pool.wait_ge(chain.sem, chain.after())
                nc.gpsimd.tensor_tensor(YK[0:r, t, :], YK[0:r, t, :], GB1[0:r, 1, :], ALU.add
                                        ).then_inc(S["x_tok_ready"], 1)
            pool.wait_ge(gb.sem, gb.after(2))
            scaled = Count(S["y_scaled"])
            for t in range(NT):
                r = tile_cols(t)[1]
                pool.wait_ge(scaled.sem, scaled.after())
                nc.gpsimd.tensor_tensor(YK[0:r, t, :], YK[0:r, t, :], GB2[0:r, 1, :], ALU.add
                                        ).then_inc(S["y_out"], 1)

        @block.scalar
        def _(act):
            chain = Count(S["act_own_order"])
            landed = [Count(s_win[j], 16) for j in range(2)]
            reuse = Count(s_done)
            done = Count(s_done)
            fa = [Count(s_fa[p]) for p in range(4)]

            def hi(n, nk=8, first=False):
                par = n % 2
                act.wait_ge(landed[par].sem, landed[par].after(2))
                if not first:
                    act.wait_ge(reuse.sem, reuse.after())
                nc.scalar.activation(WH[:, par, 0:nk], RAW[:, par, 0:nk], ACT.Copy).then_inc(s_whi, 1)

            def to_features(dst, g0, b0, early_hi=None):
                for t in range(NT):
                    act.wait_ge(turned.sem, turned.after())
                    cols, r = evac_cols(t)
                    bank = 4 + 2 * (t % 2)
                    for k in range(KT):
                        ins_ = nc.scalar.activation(
                            dst[:, k, cols], PS[:, bank + k // 4, (k % 4) * P:(k % 4) * P + r], ACT.Identity,
                            scale=VT[:, g0 + k:g0 + k + 1], bias=VT[:, b0 + k:b0 + k + 1])
                    ins_.then_inc(chain.sem, 1)
                    act.wait_ge(chain.sem, chain.after())
                    nc.scalar.activation(XH[:, :, cols], dst[:, :, cols], ACT.Copy).then_inc(S["x_hi_ready"], 1)
                    if early_hi:
                        early_hi(t)

            stats = Count(S["stats_ready"])
            turned = Count(S["ln_turned"])
            vt = Count(S["vectors_T_ready"])
            act.wait_ge(stats.sem, stats.after())
            nc.scalar.activation(SDV[:], MV[:, :, 1], ACT.Sqrt, bias=EPS[:, 0:1]).then_inc(S["std_ready"], 1)
            act.wait_ge(vt.sem, vt.after())
            to_features(XF, 0, 8, lambda t: hi(0, first=True) if t == 1 else hi(1, first=True) if t == 4 else None)

            k_feat, q_feat, head_done = Count(S["k_feat"]), Count(S["q_feat"]), Count(S["head_done"])

            def swap(scale):
                for lo in (0, 64):
                    ins_ = nc.scalar.activation(two(SW[lo:lo + 64, :]), pair(0, 64 - lo, 128 - lo), ACT.Copy,
                                                scale=scale)
                ins_.then_inc(S["swap_ready"], 1)

            def centred():
                act.wait_ge(fa[2].sem, fa[2].after())
                nc.scalar.activation(two(OC[:]), pair(2), ACT.Copy)
                nc.scalar.activation(two(OSQ[:]), pair(2), ACT.Square).then_inc(S["sq_ready"], 1)

            def deviation():
                act.wait_ge(fa[3].sem, fa[3].after())
                nc.scalar.activation(two(ORS[:]), pair(3), ACT.Sqrt, bias=EPS[:, 0:1]).then_inc(S["sd_ready"], 1)

            def ret_head(prev, n_next):
                if prev:
                    hi(1)
                act.wait_ge(fa[0].sem, fa[0].after())
                if prev:
                    act.wait_ge(q_feat.sem, q_feat.after())
                swap(RD ** -0.5)
                act.wait_ge(done.sem, done.after())
                nc.scalar.activation(two(RV[:]), pair(1), ACT.Copy).then_inc(s_free[1], 1)
                if prev:
                    centred()
                act.wait_ge(fa[0].sem, fa[0].after())
                act.wait_ge(k_feat.sem, k_feat.after())
                swap(1.0)
                if prev:
                    deviation()
                hi(n_next)
                act.wait_ge(done.sem, done.after())
                if prev:
                    act.wait_ge(head_done.sem, head_done.after())
                nc.scalar.activation(two(RG[:]), pair(1), ACT.Silu).then_inc(S["g_ready"], 1)

            ret_head(False, 2)
            with loop(act, RH - 1, {landed[0]: 2, landed[1]: 2, reuse: 2, done: 2, fa[0]: 2, fa[2]: 1, fa[3]: 1,
                                    q_feat: 1, k_feat: 1, head_done: 1}):
                ret_head(True, 2)
            centred()
            deviation()

            kr = Count(S["kr_landed"], 16)
            act.wait_ge(kr.sem, kr.after(2))
            hi(N_LAT + 1)
            act.wait_ge(head_done.sem, head_done.after())
            act.wait_ge(S["x_tok_stored"], 16 * NT)
            act.wait_ge(S["state_stored"], 16 * RH)
            act.wait_ge(S["final_state_stored"], 16 * RH)
            act.wait_ge(fa[0].sem, fa[0].after())
            nc.scalar.activation(two(QN[:, 0, :]), pair(0), ACT.Copy).then_inc(s_free[0], 1)
            act.wait_ge(done.sem, done.after())
            nc.scalar.activation(two(QN[:, 1, :]), pair(1), ACT.Copy).then_inc(s_free[1], 1)
            act.wait_ge(fa[0].sem, fa[0].after())
            nc.scalar.activation(two(QN[:, 2, :]), pair(0), ACT.Copy).then_inc(chain.sem, 1)
            chain.add()
            act.wait_ge(chain.sem, chain.after(0))
            nc.scalar.activation(QSQ[:], QN[:], ACT.Square).then_inc(S["lat_sq"], 1)
            hi(N_LAT + 2)
            act.wait_ge(fa[2].sem, fa[2].after())
            nc.scalar.activation(two(RIN[:]), pair(2), ACT.Sqrt, bias=EPS[:, 1:2], scale=1.0 / QL
                                 ).then_inc(S["lat_sd"], 1)
            act.wait_ge(done.sem, done.after())
            act.wait_ge(fa[0].sem, fa[0].after())
            nc.scalar.activation(two(CNT[:, 0, :]), pair(0), ACT.Copy).then_inc(s_free[0], 1)
            act.wait_ge(done.sem, done.after())
            nc.scalar.activation(two(CNT[:, 1, :]), pair(1), ACT.Copy).then_inc(chain.sem, 1)
            act.wait_ge(chain.sem, chain.after())
            nc.scalar.activation(QSQ[:, 0:2, :], CNT[:], ACT.Square).then_inc(S["lat_sq"], 1)
            hi(N_GATE)
            act.wait_ge(fa[3].sem, fa[3].after())
            nc.scalar.activation(two(QSQ[:, 2, :]), pair(3), ACT.Sqrt, bias=EPS[:, 1:2], scale=1.0 / KVL
                                 ).then_inc(S["lat_sd"], 1)

            gate_full = Count(S["gate_full"])
            stored = [Count(S[f"gate_stored{j}"], 16) for j in range(2)]
            nmax, probs_turned = Count(S["nmax_ready"]), Count(S["probs_turned"])
            act.sem_inc(S["gate_stored0"], 16)
            act.sem_inc(S["gate_stored1"], 16)

            def gate(g, p):
                s, m, half = g // 4, (g // 2) % 2, g % 2
                if g % 4 == 3:
                    act.wait_ge(done.sem, done.after())
                else:
                    act.wait_ge(gate_full.sem, gate_full.after())
                if g % 4 == 0:
                    act.wait_ge(stored[s].sem, stored[s].after())
                ins_ = nc.scalar.activation(SG[:, s, m, half * HALF:(half + 1) * HALF], PS[:, half, 0:HALF],
                                            ACT.Tanh, scale=0.5)
                ins_.then_inc(S[f"gate_free{half}"], 1)
                if g % 4 == 3:
                    act.wait_ge(turn_free.sem, turn_free.after(2))
                    act.dma_start(g_scr[s, bass.ds(p * 2, 2)].rearrange("m p c -> p m c"), SG[:, s]
                                  ).then_inc(S[f"gate_stored{s}"], 16)

            def exps(t):
                act.wait_ge(nmax.sem, nmax.after())
                r = tile_cols(t)[1]
                n = META + P * (t - 1)
                for hh in range(2):
                    bias = SMX[0:r, 4 + hh:5 + hh]
                    if t:
                        nc.scalar.activation(EX[:, hh, 0:n], PS[:, 4 + hh, 0:n], ACT.Exp, bias=bias, scale=SCALE,
                                             accum_out=SMX[:, 8 + 2 * hh:9 + 2 * hh])
                        ins_ = nc.scalar.activation(EX[:, hh, n:n + P], SD[:, hh, :], ACT.Exp, bias=bias,
                                                    scale=SCALE, accum_out=SMX[:, 9 + 2 * hh:10 + 2 * hh])
                    else:
                        ins_ = nc.scalar.activation(EX[0:r, hh, 0:META], SD[0:r, hh, 0:META], ACT.Exp, bias=bias,
                                                    scale=SCALE, accum_out=SMX[0:r, 8 + hh:9 + hh])
                ins_.then_inc(S["exp_ready"], 1)

            def probs_back(t):
                act.wait_ge(probs_turned.sem, probs_turned.after())
                r = tile_cols(t)[1]
                if t:
                    k = min(t, 3)
                    nc.scalar.activation(PTS[:, 0, 1:k + 1, :], PS[:, 4, P:(k + 1) * P].rearrange(
                        "p (k c) -> p k c", k=k), ACT.Copy)
                nc.scalar.activation(PTS[0:META, 0, 0, 0:r], PS[0:META, 4, 0:r], ACT.Copy).then_inc(S["pt_act"], 1)

            turn_free = Count(S["gate_free1"], start=1)

            def gate_pair(p):
                hi(N_GATE + 1)
                for g in range(3):
                    gate(g, p)
                for t in range(NT):
                    exps(t)
                    if t:
                        gate(2 + t, p)
                    if t == 1:
                        hi(N_GATE)
                    probs_back(t)
                gate(7, p)

            with loop(act, 4, {landed[0]: 2, landed[1]: 2, reuse: 2, done: 2, gate_full: 6, stored[0]: 1,
                               stored[1]: 1, nmax: NT, probs_turned: NT, turn_free: 4}) as p:
                gate_pair(p)

            for j in range(2):
                act.wait_ge(stored[j].sem, stored[j].after(1))
            hi(N_MERGE + 1, 4)
            ct, scored, shifted = Count(S["chunk_turned"]), Count(S["chunk_scored"]), Count(S["shifted"])
            rope_t, exp_s, pv = Count(S["rope_turned"]), Count(S["exp_s"]), Count(S["pv_chunk"])

            def chunk_hi(c):
                act.wait_ge(ct.sem, ct.after())
                if c >= 2:
                    act.wait_ge(scored.sem, scored.after())
                j = c % 2
                nc.scalar.activation(CTH[:, j].rearrange("p a b -> p (a b)"),
                                     PS[:, 2 * j:2 * j + 2, :].rearrange("p a b -> p (a b)"), ACT.Copy
                                     ).then_inc(S["ct_act"], 1)

            def exp_sample(par):
                act.wait_ge(shifted.sem, shifted.after())
                nc.scalar.activation(PB[:, par], SCB[:, par], ACT.Exp, scale=SCALE).then_inc(S["exp_s"], 1)

            def probs_hi(par):
                act.wait_ge(exp_s.sem, exp_s.after())
                nc.scalar.activation(PHL[:, :, 0:HEADS], PB[:, par, 0:NPAGES], ACT.Copy).then_inc(S["p_hi"], 1)

            def page_hi(par, c):
                if c >= 4:
                    act.wait_ge(pv.sem, pv.after())
                nc.scalar.activation(PHI[c % 4], PGC[:, par, 4 * c:4 * c + 4, :], ACT.Copy
                                     ).then_inc(S["page_hi"], 1)

            def parts_back(a):
                nc.scalar.activation(SPART[:, a, :], PS[:, 4 + a, :], ACT.Copy).then_inc(S["parts_back"], 1)

            def rope_back():
                act.wait_ge(rope_t.sem, rope_t.after())
                nc.scalar.activation(RTT[:].rearrange("p c s -> p (c s)"),
                                     PS[:, 2:4, :].rearrange("p a b -> p (a b)"), ACT.Copy
                                     ).then_inc(S["rope_back"], 1)

            def sample_act(prev, more=True):
                for c in range(2, NCH):
                    chunk_hi(c)
                    if prev is not None:
                        if c % 2 == 0:
                            page_hi(prev, c // 2 - 1)
                        if c == 6:
                            exp_sample(prev)
                    if c == 5:
                        parts_back(0)
                if prev is not None:
                    probs_hi(prev)
                act.wait_ge(scored.sem, scored.after(2))
                parts_back(1)
                if more:
                    chunk_hi(0)
                    rope_back()
                if prev is not None:
                    for c in range(3, NCH):
                        if c == 7 and more:
                            chunk_hi(1)
                        page_hi(prev, c)
                    act.wait_ge(pv.sem, pv.after(4))
                else:
                    chunk_hi(1)

            chunk_hi(0)
            rope_back()
            chunk_hi(1)
            sample_act(None)
            with loop(act, 3, {ct: 2 * NCH, scored: 2 * NCH, shifted: 2, rope_t: 2, exp_s: 2, pv: 2 * NCH}):
                for par in range(2):
                    sample_act(par)
            sample_act(0, False)
            exp_sample(1)
            probs_hi(1)
            for c in range(NCH):
                page_hi(1, c)

            a_done = Count(S["a_done"])
            act.wait_ge(a_done.sem, a_done.after())
            nc.scalar.activation(AH[:], AT[:], ACT.Copy).then_inc(S["ab_hi"], 1)
            nc.scalar.activation(BH[:], BT[:], ACT.Copy).then_inc(S["ab_hi"], 1)
            m_added = Count(S["m_added"])

            def merge(jj, nk_next0, nk_next1):
                act.wait_ge(done.sem, done.after())
                hi(N_MERGE + 2, nk_next0)
                act.wait_ge(done.sem, done.after())
                hi(N_MERGE + 3, nk_next1)
                act.wait_ge(m_added.sem, m_added.after())
                nc.scalar.activation(MH[:, bass.ds(jj * 2, 2), :], GG[:, 0], ACT.Copy, scale=0.5
                                     ).then_inc(S["m_hi"], 1)

            with loop(act, 3, {landed[0]: 2, landed[1]: 2, reuse: 2, done: 2, m_added: 1}) as jj:
                merge(jj, 4, 4)
            merge(3, 8, 8)

            def out_pair(jj, more):
                act.wait_ge(fa[0].sem, fa[0].after())
                nc.scalar.activation(two(TT[:, bass.ds(jj * 4, 1), :].rearrange("p a c -> p (a c)")), pair(0),
                                     ACT.Copy).then_inc(s_free[0], 1)
                act.wait_ge(done.sem, done.after())
                nc.scalar.activation(two(TT[:, bass.ds(jj * 4 + 1, 1), :].rearrange("p a c -> p (a c)")), pair(1),
                                     ACT.Copy).then_inc(s_free[1], 1)
                hi(N_O)
                act.wait_ge(fa[2].sem, fa[2].after())
                nc.scalar.activation(two(TT[:, bass.ds(jj * 4 + 2, 1), :].rearrange("p a c -> p (a c)")), pair(2),
                                     ACT.Copy).then_inc(s_free[2], 1)
                act.wait_ge(done.sem, done.after())
                nc.scalar.activation(two(TT[:, bass.ds(jj * 4 + 3, 1), :].rearrange("p a c -> p (a c)")), pair(3),
                                     ACT.Copy).then_inc(s_free[3], 1)
                hi(N_O + 1)

            with loop(act, 2, {landed[0]: 2, landed[1]: 2, reuse: 2, done: 2, fa[0]: 1, fa[2]: 1}) as jj:
                out_pair(jj, True)

            act.wait_ge(stats.sem, stats.after())
            nc.scalar.activation(SDV[:], MV[:, :, 1], ACT.Sqrt, bias=EPS[:, 0:1]).then_inc(S["std_ready"], 1)
            to_features(XF1, 16, 24)

            conv_acc, h_ready = Count(S["conv_acc"]), Count(S["h_ready"])
            act.wait_ge(S["rows_zeroed"], 1)

            def conv_start(m, f):
                if m:
                    act.wait_ge(done.sem, done.after())
                else:
                    act.wait_ge(fa[0].sem, fa[0].after())
                nc.scalar.activation(AB[:, m, 2:2 + HALF - DEC], PS[:, 2 * m, DEC:HALF], ACT.Copy)
                nc.scalar.activation(AB[:, m, 2 + HALF - DEC:], PS[:, 2 * m + 1, 0:HALF], ACT.Copy).then_inc(chain.sem, 1)
                chain.add()
                nc.scalar.activation(CSP[:, bass.ds(f, 1), :].rearrange("p a c -> p (a c)"),
                                     PS[:, 2 * m + 1, HALF - 2:HALF], ACT.Copy)
                nc.scalar.activation(css(f), PS[:, 2 * m, 0:DEC].rearrange("p (k r) -> p k r", k=2),
                                     ACT.Copy).then_inc(s_free[m], 1)
                act.wait_ge(chain.sem, chain.after(0))
                nc.scalar.activation(ACC[:, m, DEC:], AB[:, m, 0:META + SEQ], ACT.Identity,
                                     scale=CV[:, bass.ds(f, 1)], bias=CV[:, bass.ds(f + 3 * FT, 1)])
                nc.scalar.activation(ACC[:, m, 0:DEC], PV[:, bass.ds(f, 1), 0:2 * DEC:2].rearrange("p a c -> p (a c)"),
                                     ACT.Identity, scale=CV[:, bass.ds(f, 1)], bias=CV[:, bass.ds(f + 3 * FT, 1)]
                                     ).then_inc(S["conv_first"], 1)

            for part, nf in enumerate(FFN_TILES):
                f0 = sum(FFN_TILES[:part])

                def ffn_in_pair(i, next_a, next_b):
                    for m in range(2):
                        conv_start(m, i * 2 + (f0 + m))
                    next_a()
                    for m in range(2):
                        act.wait_ge(conv_acc.sem, conv_acc.after())
                        nc.scalar.activation(GL[:, m], ACC[:, m], ACT.Gelu_apprx_tanh).then_inc(S["gelu_done"], 1)
                    for m in range(2):
                        act.wait_ge(h_ready.sem, h_ready.after())
                        nc.scalar.activation(FH[:, bass.ds(i * 2 + m, 1), :].rearrange("p a c -> p (a c)"), HF[:, m],
                                             ACT.Copy).then_inc(S["h_hi"], 1)
                    act.wait_ge(done.sem, done.after())
                    next_b()

                na = (N_F1, N_F2)[part]
                no = (N_F1O, N_F2O)[part]
                hk = nf // 2
                with loop(act, nf // 2 - 1, {landed[0]: 2, landed[1]: 2, reuse: 2, done: 2, fa[0]: 1, chain: 2,
                                             conv_acc: 2, h_ready: 2}) as i:
                    ffn_in_pair(i, lambda: hi(na), lambda: hi(na + 1))
                ffn_in_pair(nf // 2 - 1, lambda: hi(no, hk), lambda: hi(no + 1, hk))
                last = part == 1

                def out_cols(jj, hi_a, hi_b):
                    act.wait_ge(done.sem, done.after())
                    hi_a()
                    if not last:
                        act.wait_ge(fa[0].sem, fa[0].after())
                        nc.scalar.activation(two(TT[:, bass.ds(jj * 2, 1), :].rearrange("p a c -> p (a c)")), pair(0),
                                             ACT.Copy).then_inc(s_free[0], 1)
                    act.wait_ge(done.sem, done.after())
                    if not last:
                        nc.scalar.activation(two(TT[:, bass.ds(jj * 2 + 1, 1), :].rearrange("p a c -> p (a c)")),
                                             pair(1), ACT.Copy).then_inc(s_free[1], 1)
                    hi_b()

                per = {landed[0]: 2, landed[1]: 2, reuse: 2, done: 2}
                if not last:
                    per[fa[0]] = 1
                with loop(act, 3, per) as jj:
                    out_cols(jj, lambda: hi(no, hk), lambda: hi(no + 1, hk))
                if last:
                    out_cols(3, lambda: None, lambda: None)
                else:
                    out_cols(3, lambda: hi(N_F2), lambda: hi(N_F2 + 1))

            act.wait_ge(stats.sem, stats.after())
            nc.scalar.activation(SDV[:], MV[:, :, 1], ACT.Sqrt, bias=EPS[:, 0:1]).then_inc(S["std_ready"], 1)

        @block.vector
        def _(dve):
            chain = Count(S["dve_own_order"])
            whi = Count(s_whi)
            fd = [Count(s_fd[p]) for p in range(4)]
            done = Count(s_done)
            V = nc.vector

            def lo(n, nk=8):
                par = n % 2
                dve.wait_ge(whi.sem, whi.after())
                V.tensor_tensor(WL[:, par, 0:nk], RAW[:, par, 0:nk], WH[:, par, 0:nk].bitcast(F32), ALU.subtract
                                ).then_inc(s_wsplit, 1)

            def norm_tiles(x):
                for t in range(NT):
                    r = tile_cols(t)[1]
                    if x is XK:
                        dve.wait_ge(s_x[t], 32 if t == 0 else 16)
                    for j in range(2):
                        V.bn_stats(STAT[0:r, t, j, :], x[0:r, t, 512 * j:512 * j + 512]).then_inc(chain.sem, 1)
                        chain.add()
                dve.wait_ge(chain.sem, chain.after(0))
                for t in range(NT):
                    r = tile_cols(t)[1]
                    last = V.bn_aggr(MV[0:r, t, :], STAT[0:r, t, :, :].rearrange("p a b -> p (a b)"))
                last.then_inc(S["stats_ready"], 1)
                dve.wait_ge(std.sem, std.after())
                V.reciprocal(RSV[:], SDV[:]).then_inc(chain.sem, 1)
                dve.wait_ge(chain.sem, chain.after())
                for t in range(NT):
                    r = tile_cols(t)[1]
                    V.tensor_scalar(x[0:r, t, :], x[0:r, t, :], MV[0:r, t, 0:1], RSV[0:r, t:t + 1], ALU.subtract,
                                    ALU.mult).then_inc(S["x_normed"], 1)

            def split_x(src, early_lo=None):
                for t in range(NT):
                    c, r = evac_cols(t)
                    dve.wait_ge(x_hi.sem, x_hi.after())
                    V.tensor_tensor(XL[:, :, c], src[:, :, c], XH[:, :, c].bitcast(F32), ALU.subtract
                                    ).then_inc(S["x_split"], 1)
                    if early_lo:
                        early_lo(t)

            std, x_hi = Count(S["std_ready"]), Count(S["x_hi_ready"])
            V.memset(EPS[:, 0:1], LN_EPS)
            V.memset(EPS[:, 1:2], RMS_EPS)
            V.memset(MV[:], 1.0).then_inc(chain.sem, 1)
            dve.wait_ge(chain.sem, chain.after())
            norm_tiles(XK)
            dve.wait_ge(fd[0].sem, fd[0].after())
            V.tensor_copy(CV[:], PS[:, 1, 0:4 * FT])
            V.tensor_copy(VT[:], PS[:, 0, 0:41]).then_inc(S["vectors_T_ready"], 1)
            split_x(XF, lambda t: lo(0) if t == 1 else lo(1) if t == 4 else None)
            vt = Count(S["vectors_T_ready"])
            dve.wait_ge(vt.sem, vt.after())
            dve.wait_ge(fd[1].sem, fd[1].after())
            V.tensor_copy(PV[:].rearrange("p f c -> p (f c)"), PS[:, 2, 0:2 * DEC * FT]).then_inc(s_free[1], 1)

            swap_ready, q_feat = Count(S["swap_ready"]), Count(S["q_feat"])
            state_landed, sd_ready, g_ready = Count(S["state_landed"], 16), Count(S["sd_ready"]), Count(S["g_ready"])
            final_stored = Count(S["final_state_stored"], 16)
            c2 = Count(S["consts2_landed"], 16)
            dve.wait_ge(c2.sem, c2.after(10))

            def rotate(dst, scale, s_out):
                dve.wait_ge(swap_ready.sem, swap_ready.after())
                V.tensor_tensor(TP[:], SW[:], RR[:, 1, :], ALU.mult)
                V.scalar_tensor_tensor(two(dst), pair(0), scale, two(RR[:, 0, :]), ALU.mult, ALU.mult).then_inc(chain.sem, 1)
                dve.wait_ge(chain.sem, chain.after())
                V.tensor_tensor(dst, dst, TP[:], ALU.add).then_inc(s_out, 1)

            def head_const(h, c0, n):
                return HC[:, bass.ds(h, 1), c0:c0 + n].rearrange("p a c -> p (a c)")

            C_KD, C_KD0, C_G1, C_GP = (2 * P + T0 + j for j in range(4))

            def outputs_back(h):
                dve.wait_ge(fd[3].sem, fd[3].after())
                V.tensor_copy(OT[:, DEC:T0], PS[:, 7, DEC:T0])
                V.tensor_copy(OT[:, T0:], PS[:, 6, :])
                dve.wait_ge(fd[2].sem, fd[2].after())
                dve.wait_ge(state_landed.sem, state_landed.after())
                V.scalar_tensor_tensor(ST[:].rearrange("p (a b) v -> p a (b v)", a=2),
                                       ST[:].rearrange("p (a b) v -> p a (b v)", a=2), head_const(h, C_G1, 1),
                                       PS[:, 4:6, :], ALU.mult, ALU.add).then_inc(S["sn_ready"], 1)

            def sample_back():
                dve.wait_ge(fd[3].sem, fd[3].after())
                V.tensor_copy(OT[:, 0:DEC], PS[:, 6, 0:DEC]).then_inc(S["ot_ready"], 1)

            def readout(h):
                dve.wait_ge(sd_ready.sem, sd_ready.after())
                dve.wait_ge(g_ready.sem, g_ready.after())
                V.reciprocal(ORS[:], ORS[:]).then_inc(chain.sem, 1)
                dve.wait_ge(chain.sem, chain.after())
                V.tensor_tensor(OC[:], OC[:], ORS[:], ALU.mult).then_inc(chain.sem, 1)
                dve.wait_ge(chain.sem, chain.after())
                V.scalar_tensor_tensor(BT[:, bass.ds(h, 1), :].rearrange("p a c -> p (a c)"), OC[:],
                                       VT[:, bass.ds(h + 37, 1)], RG[:], ALU.mult, ALU.mult
                                       ).then_inc(S["head_done"], 1)

            def ret_head(h, prev):
                if prev:
                    lo(1)
                rotate(RK[:], RD ** -0.5, S["k_feat"])
                if prev:
                    outputs_back(h - 1)
                    sample_back()
                rotate(RQ[:], 1.0, S["q_feat"])
                dve.wait_ge(q_feat.sem, q_feat.after())
                V.tensor_tensor(RQD[:], RQ[:, T0:].rearrange("p (t c) -> p t c", t=4),
                                head_const(h, P, P).unsqueeze(1).to_broadcast([P, 4, P]), ALU.mult)
                dve.wait_ge(fd[2].sem, fd[2].after())
                V.tensor_scalar(KDEC[:, 1:NT, :], PS[:, 4, :].rearrange("p (t c) -> p t c", t=4),
                                head_const(h, C_KD, 1), None, ALU.mult)
                V.tensor_copy(VTOK[:, 1:NT, :], PS[:, 5, :].rearrange("p (t c) -> p t c", t=4))
                dve.wait_ge(fd[3].sem, fd[3].after())
                V.tensor_copy(KTOK0[0:T0, :], PS[0:T0, 6, 0:P])
                V.tensor_scalar(KDEC[0:T0, 0, :], PS[0:T0, 6, 0:P], head_const(h, C_KD0, 1)[0:T0], None, ALU.mult)
                V.tensor_copy(VTOK[0:T0, 0, :], PS[0:T0, 6, P:2 * P]).then_inc(chain.sem, 1)
                dve.wait_ge(chain.sem, chain.after())
                for b in range(DEC):
                    last = V.tensor_scalar(VBLK[0:DEC, b, :], VTOK[0:DEC, 0, :], IDENT[0:DEC, b:b + 1], None, ALU.mult)
                last.then_inc(S["tok_ready"], 1)
                if prev:
                    readout(h - 1)
                lo(0)
                dve.wait_ge(fd[2].sem, fd[2].after())
                dve.wait_ge(fd[3].sem, fd[3].after())
                if prev:
                    dve.wait_ge(final_stored.sem, final_stored.after())
                V.tensor_tensor(INT[:], PS[:, 4, :].rearrange("p (t c) -> p t c", t=4),
                                head_const(h, 0, P).unsqueeze(1).to_broadcast([P, 4, P]), ALU.mult)
                V.tensor_tensor(IN0[0:T0, :], PS[0:T0, 6, 0:T0], head_const(h, 2 * P, T0)[0:T0], ALU.mult)
                V.tensor_copy(RS[:, 0, :], PS[:, 6, P:2 * P]).then_inc(chain.sem, 1)
                dve.wait_ge(chain.sem, chain.after())
                for t in range(1, NT):
                    ins_ = V.scalar_tensor_tensor(RS[:, t, :], RS[:, t - 1, :], head_const(h, C_GP, 1),
                                                  PS[:, 5, P * (t - 1):P * t], ALU.mult, ALU.add)
                    if t < NT - 1:
                        ins_.then_inc(chain.sem, 1)
                        dve.wait_ge(chain.sem, chain.after())
                ins_.then_inc(S["inner_ready"], 1)

            ret_head(0, False)
            with loop(dve, RH - 1, {whi: 2, chain: 9, swap_ready: 2, q_feat: 1, fd[2]: 3, fd[3]: 4, state_landed: 1,
                                    sd_ready: 1, g_ready: 1, final_stored: 1}) as i:
                ret_head(i + 1, True)
            outputs_back(RH - 1)
            sample_back()
            for c in range(NCH):
                V.tensor_scalar(IDX[:, :, c], PTI[:], 32.0, SMALL[:, 25:26], ALU.mult, ALU.add)
            V.tensor_scalar(IDX[:, :, NCH], PTI[:], 4.0, SMALL[:, 24:25], ALU.mult, ALU.add).then_inc(chain.sem, 1)
            dve.wait_ge(chain.sem, chain.after())
            for c in range(1, NCH):
                last = V.tensor_scalar(IDX[:, :, c], IDX[:, :, c], float(c), None, ALU.add)
            last.then_inc(S["idx_ready"], 1)
            readout(RH - 1)

            lo(N_LAT + 1)
            dve.wait_ge(done.sem, done.after(N_LAT + 2))
            mr = Count(S["idx_in"], 16)
            dve.wait_ge(mr.sem, mr.after(2))
            hd = Count(S["head_done"])
            dve.wait_ge(hd.sem, hd.after(RH))
            R0, R1 = slice(64, 96), slice(96, 128)

            def rotated(p, j):
                dve.wait_ge(chain.sem, chain.after(0))
                V.tensor_tensor(two(TQ[R0, 0, :]), pair(p, 96, 128), two(MR[R1, :]), ALU.mult)
                V.tensor_tensor(two(TQ[R0, 1, :]), pair(p, 64, 96), two(MR[R0, :]), ALU.mult).then_inc(chain.sem, 1)
                dve.wait_ge(chain.sem, chain.after())

            rotated(1, 0)
            for j in range(2):
                V.tensor_tensor(KTB[R0, j, :], TQ[R0, 0, :], TQ[R0, 1, :], ALU.add)
            V.tensor_tensor(KRT[0:32, :], TQ[R0, 0, :], TQ[R0, 1, :], ALU.add).then_inc(s_free[1], 1)
            lo(N_LAT + 2)
            lat_sd = Count(S["lat_sd"])
            dve.wait_ge(lat_sd.sem, lat_sd.after())
            V.reciprocal(RIN[:], RIN[:]).then_inc(chain.sem, 1)
            dve.wait_ge(chain.sem, chain.after())
            for j in range(3):
                last = V.scalar_tensor_tensor(QN[:, j, :], QN[:, j, :], VT[:, 32 + j:33 + j], RIN[:], ALU.mult, ALU.mult)
            last.then_inc(S["lat_normed"], 1)
            lo(N_GATE)
            dve.wait_ge(lat_sd.sem, lat_sd.after())
            V.reciprocal(QSQ[:, 2, :], QSQ[:, 2, :]).then_inc(chain.sem, 1)
            dve.wait_ge(chain.sem, chain.after())
            for j in range(2):
                last = V.scalar_tensor_tensor(CNT[:, j, :], CNT[:, j, :], VT[:, 35 + j:36 + j], QSQ[:, 2, :],
                                              ALU.mult, ALU.mult)
            V.memset(KR8[:], 0.0).then_inc(chain.sem, 1)
            dve.wait_ge(chain.sem, chain.after())
            last2 = V.tensor_copy(KR8[0:32, :], KRT[0:32, 0:DEC])
            last2.then_inc(chain.sem, 1)
            dve.wait_ge(chain.sem, chain.after())
            V.tensor_copy(CN8[:], CNT[:, :, 0:DEC]).then_inc(S["lat_normed"], 1)
            dve.wait_ge(fd[2].sem, fd[2].after())
            V.tensor_copy(CTOK[:, 1:NT, :].rearrange("p (a b) c -> p a (b c)", a=2), PS[:, 4:6, :]
                          ).then_inc(s_free[2], 1)
            dve.wait_ge(fd[3].sem, fd[3].after())
            V.tensor_copy(CTX[:], PS[0:T0, 6, 0:KVL])
            V.tensor_copy(KRO[0:T0, 0, :], PS[0:T0, 7, P:P + ROPE])
            V.tensor_copy(KRO[:, 1:NT, :], PS[:, 7, 0:P].rearrange("p (t c) -> p t c", t=4)
                          ).then_inc(S["tok_out_ready"], 1)

            proj, scores = Count(S["proj_done"]), Count(S["scores_full"])
            expd, turned = Count(S["exp_ready"]), Count(S["probs_turned"])

            def softmax(t):
                dve.wait_ge(scores.sem, scores.after())
                r = tile_cols(t)[1]
                n = META + P * (t - 1)
                diag = PS[0:r, 6, 0:2 * P].rearrange("p (h c) -> p h c", h=2)
                if t:
                    V.tensor_tensor(SD[:], diag, CAUSAL.unsqueeze(1).to_broadcast([P, 2, P]), ALU.add).then_inc(chain.sem, 1)
                    chain.add()
                    V.reduce_max(SMX[:, 0:2], PS[:, 4:6, 0:n], AX).then_inc(chain.sem, 1)
                    dve.wait_ge(chain.sem, chain.after())
                    V.reduce_max(SMX[:, 2:4], SD[:], AX).then_inc(chain.sem, 1)
                    dve.wait_ge(chain.sem, chain.after())
                    V.tensor_tensor(SMX[:, 6:8], SMX[:, 0:2], SMX[:, 2:4], ALU.max).then_inc(chain.sem, 1)
                    dve.wait_ge(chain.sem, chain.after())
                else:
                    V.tensor_tensor(SD[0:r, :, 0:META], diag[:, :, 0:META],
                                    SMALL[0:r, 0:META].unsqueeze(1).to_broadcast([r, 2, META]), ALU.add).then_inc(chain.sem, 1)
                    dve.wait_ge(chain.sem, chain.after())
                    V.reduce_max(SMX[0:r, 6:8], SD[0:r, :, 0:META], AX).then_inc(chain.sem, 1)
                    dve.wait_ge(chain.sem, chain.after())
                V.tensor_scalar(SMX[0:r, 4:6], SMX[0:r, 6:8], -SCALE, None, ALU.mult).then_inc(S["nmax_ready"], 1)
                dve.wait_ge(expd.sem, expd.after())
                if t:
                    V.reduce_sum(SMX[:, 12:14], SMX[:, 8:12].rearrange("p (h c) -> p h c", h=2), AX).then_inc(chain.sem, 1)
                    dve.wait_ge(chain.sem, chain.after())
                    src = SMX[:, 12:14]
                else:
                    src = SMX[0:r, 8:10]
                V.reciprocal(SMX[0:r, 14:16], src).then_inc(chain.sem, 1)
                dve.wait_ge(chain.sem, chain.after())
                w = n + P if t else META
                for hh in range(2):
                    last = V.tensor_scalar(EX[0:r, hh, 0:w], EX[0:r, hh, 0:w], SMX[0:r, 14 + hh:15 + hh], None, ALU.mult)
                last.then_inc(S["probs_ready"], 1)

            def probs_back(t):
                dve.wait_ge(turned.sem, turned.after())
                r = tile_cols(t)[1]
                if t:
                    k = min(t, 3)
                    V.tensor_copy(PTS[:, 1, 1:k + 1, :], PS[:, 5, P:(k + 1) * P].rearrange("p (k c) -> p k c", k=k))
                if t == NT - 1:
                    V.tensor_copy(PTS[:, :, NT - 1, :], PS[:, 6, 0:2 * P].rearrange("p (h c) -> p h c", h=2))
                V.tensor_copy(PTS[0:META, 1, 0, 0:r], PS[0:META, 5, 0:r]).then_inc(S["pt_dve"], 1)

            def attn_pair(p):
                lo(N_GATE + 1)
                for hh in range(2):
                    dve.wait_ge(fd[2 + hh].sem, fd[2 + hh].after())
                    rotated(2 + hh, hh)
                    V.tensor_copy(two(QT[0:64, hh, :]), pair(2 + hh, 0, 64)).then_inc(s_free[2 + hh], 1)
                    V.tensor_tensor(QT[R0, hh, :], TQ[R0, 0, :], TQ[R0, 1, :], ALU.add).then_inc(chain.sem, 1)
                    chain.add()
                dve.wait_ge(fd[1].sem, fd[1].after())
                V.tensor_copy(two(KTB[0:64, 0, :]), pair(1, 0, 64))
                V.tensor_copy(two(KTB[0:64, 1, :]), pair(1, 64, 128))
                dve.wait_ge(chain.sem, chain.after(0))
                V.tensor_copy(QS[R0, bass.ds(p * 2, 2), :], QT[R0, :, 0:DEC]).then_inc(S["q_heads_ready"], 1)
                dve.wait_ge(fd[2].sem, fd[2].after())
                V.tensor_copy(VB[0:META, 0, :], PS[0:META, 5, 0:P])
                V.tensor_copy(VB[:, 1:NT, :], PS[:, 4, :].rearrange("p (t c) -> p t c", t=4)).then_inc(s_free[2], 1)
                dve.wait_ge(proj.sem, proj.after())
                V.tensor_copy(UKT[0:64].rearrange("p a b c -> p (a b c)"), PS[0:64, 6, :]).then_inc(S["uk_T_ready"], 1)
                dve.wait_ge(fd[3].sem, fd[3].after())
                for ct in range(2):
                    last = V.tensor_copy(QAB[:, ct, :, bass.ds(p * 2, 2)].rearrange("p b h -> p h b"),
                                         PS[:, 6, 16 * ct:16 * ct + 16].rearrange("p (h b) -> p h b", h=2))
                last.then_inc(s_free[3], 1)
                for t in range(NT):
                    softmax(t)
                    probs_back(t)
                    if t == 2:
                        lo(N_GATE)
                dve.wait_ge(fd[1].sem, fd[1].after())
                at_p = AT[:, bass.ds(p, 1), :].rearrange("p a c -> p (a c)")
                V.tensor_copy(at_p[:, DEC:T0], PS[:, 3, DEC:T0])
                V.tensor_copy(at_p[:, T0:], PS[:, 2, :]).then_inc(S["attn_done"], 1)

            with loop(dve, 4, {whi: 2, chain: 4 + 3 + 4 * 6, fd[1]: 2, fd[2]: 2, fd[3]: 2, proj: 1,
                               scores: NT, expd: NT, turned: NT}) as p:
                attn_pair(p)

            lo(N_MERGE + 1, 4)
            attn_done = Count(S["attn_done"])
            dve.wait_ge(attn_done.sem, attn_done.after(4))
            V.memset(QRB[:], 0.0).then_inc(chain.sem, 1)
            dve.wait_ge(chain.sem, chain.after())
            for g in range(4):
                V.tensor_copy(QRB[32 * g:32 * g + 32, :, g, :],
                              QS[R0, :, :].rearrange("p h b -> p b h")).then_inc(chain.sem, 1)
                chain.add()
            V.memset(SCB[:, :, 32, :], NEG)
            V.tensor_scalar(QB[:].rearrange("p a b -> p (a b)"), SQ[:].rearrange("p a b -> p (a b)")[:, 0:448], 0.0,
                            None, ALU.mult).then_inc(S["qrb_ready"], 1)
            qrb = Count(S["qrb_ready"])
            dve.wait_ge(qrb.sem, qrb.after())
            ct_a, s_full, page_hi = Count(S["ct_act"]), Count(S["s_full"]), Count(S["page_hi"])
            bank_free, mxt, mxs = Count(S["s_bank_free"]), Count(S["mx_turned"]), Count(S["mx_spread"])
            exp_s, sums, pv_full = Count(S["exp_s"]), Count(S["sum_spread"]), Count(S["pv_full"])
            p_hi, lat_turned = Count(S["p_hi"]), Count(S["lat_turned"])

            def split_query(b):
                q = QAB[:, :, bass.ds(b, 1), :].rearrange("p a b h -> p a (b h)")
                V.tensor_copy(QB[:, :, 96:96 + HEADS], q).then_inc(chain.sem, 1)
                dve.wait_ge(chain.sem, chain.after())
                V.tensor_tensor(QB[:, :, 96 + HEADS:96 + 2 * HEADS], q, QB[:, :, 96:96 + HEADS].bitcast(F32), ALU.subtract
                                ).then_inc(S["q_parts"], 1)

            def chunk_lo(c):
                dve.wait_ge(ct_a.sem, ct_a.after())
                j = c % 2
                V.tensor_tensor(CTL[:, j].rearrange("p a b -> p (a b)"),
                                PS[:, 2 * j:2 * j + 2, :].rearrange("p a b -> p (a b)"),
                                CTH[:, j].rearrange("p a b -> p (a b)").bitcast(F32), ALU.subtract
                                ).then_inc(S["ct_dve"], 1)

            def page_lo(par, c):
                dve.wait_ge(page_hi.sem, page_hi.after())
                V.tensor_tensor(PLO[c % 4], PGC[:, par, 4 * c:4 * c + 4, :], PHI[c % 4].bitcast(F32),
                                ALU.subtract).then_inc(S["page_split"], 1)

            def probs_lo(par):
                dve.wait_ge(p_hi.sem, p_hi.after())
                V.tensor_tensor(PHL[:, :, HEADS:2 * HEADS], PB[:, par, 0:NPAGES], PHL[:, :, 0:HEADS].bitcast(F32),
                                ALU.subtract).then_inc(S["p_split"], 1)

            def scores_back(par, b):
                dve.wait_ge(s_full.sem, s_full.after())
                V.tensor_copy(SCB[:, par, 0:32, :].rearrange("p k h -> p (k h)"), PS[:, 6, 0:256])
                V.tensor_scalar(SCB[0:DEC, par, 32, :], PS[0:DEC, 6, 256:264], SMALL[0:DEC, bass.ds(b + 16, 1)], None,
                                ALU.add).then_inc(S["s_bank_free"], 1)
                dve.wait_ge(bank_free.sem, bank_free.after())
                V.reduce_max(SSM[:, par, 0:8], SCB[:, par].rearrange("p k h -> p h k"), AX).then_inc(S["mx_ready"], 1)

            def max_rows(par):
                dve.wait_ge(mxt.sem, mxt.after())
                V.reduce_max(SSM[0:8, par, 8:9], PS[0:8, 7, 0:P], AX).then_inc(chain.sem, 1)
                dve.wait_ge(chain.sem, chain.after())
                V.tensor_scalar(SSM[0:8, par, 16:24], IDENT[0:8, 0:8], SSM[0:8, par, 8:9], None, ALU.mult
                                ).then_inc(S["dg_ready"], 1)

            def shift(par):
                dve.wait_ge(mxs.sem, mxs.after())
                V.tensor_tensor(SCB[:, par], SCB[:, par],
                                PS[:, 7, P:P + 8].unsqueeze(1).to_broadcast([P, 33, 8]), ALU.subtract
                                ).then_inc(S["shifted"], 1)

            def sum_rows(par):
                dve.wait_ge(exp_s.sem, exp_s.after())
                V.reduce_sum(SSM[:, par, 24:32], PB[:, par].rearrange("p k h -> p h k"), AX).then_inc(S["sum_ready"], 1)

            def inv_sum(par):
                dve.wait_ge(sums.sem, sums.after())
                V.reciprocal(SSM[:, par, 32:40], PS[:, 7, P + 8:P + 16]).then_inc(S["rs_ready"], 1)
                V.memset(SCB[:, par, 32, :], NEG).then_inc(chain.sem, 1)
                dve.wait_ge(chain.sem, chain.after())

            def latent_out(par, b):
                dve.wait_ge(lat_turned.sem, lat_turned.after())
                V.tensor_tensor(OL[:, :, :, bass.ds(b, 1)].rearrange("p a h b -> p a (h b)"),
                                PS[:, 7, 144:160].rearrange("p (a h) -> p a h", a=2),
                                SSM[:, par, 32:40].unsqueeze(1).to_broadcast([P, 2, 8]), ALU.mult
                                ).then_inc(S["olat_ready"], 1)

            def outputs_back():
                dve.wait_ge(pv_full.sem, pv_full.after())
                V.tensor_copy(OPART[:], PS[0:2 * HEADS, 7, 256:256 + KVL]).then_inc(S["o_parts"], 1)

            def sample_dve(par, b, prev, more=True):
                for c in range(2, NCH):
                    chunk_lo(c)
                    if prev is not None:
                        if c % 2 == 0:
                            page_lo(prev, c // 2 - 1)
                        {3: max_rows, 5: shift, 7: sum_rows}.get(c, lambda q: None)(prev)
                if prev is not None:
                    probs_lo(prev)
                    inv_sum(prev)
                if more:
                    chunk_lo(0)
                if prev is not None:
                    page_lo(prev, 3)
                scores_back(par, b)
                if more:
                    split_query(b + 1)
                if prev is not None:
                    for c in range(4, NCH):
                        if c == 7 and more:
                            chunk_lo(1)
                        page_lo(prev, c)
                    outputs_back()
                    latent_out(prev, b - 1)
                else:
                    chunk_lo(1)

            split_query(0)
            chunk_lo(0)
            chunk_lo(1)
            sample_dve(0, 0, None)
            with loop(dve, 3, {chain: 6, ct_a: 2 * NCH, page_hi: 2 * NCH, mxt: 2, mxs: 2, exp_s: 2, sums: 2, s_full: 2,
                               bank_free: 2, pv_full: 2, p_hi: 2, lat_turned: 2}) as i:
                for par in range(2):
                    sample_dve(1 - par, i * 2 + (1 + par), par)
            sample_dve(1, DEC - 1, 0, False)
            max_rows(1)
            shift(1)
            sum_rows(1)
            probs_lo(1)
            inv_sum(1)
            for c in range(NCH):
                page_lo(1, c)
            outputs_back()
            latent_out(1, DEC - 1)
            a_full = Count(S["a_s_full"])
            dve.wait_ge(a_full.sem, a_full.after())
            for hh in range(2):
                last = V.tensor_copy(AT[64 * hh:64 * hh + 64, :, 0:DEC],
                                     PS[64 * hh:64 * hh + 64, 7, 0:64].rearrange("p (a c) -> p a c", a=4)
                                     [:, :, 8 * hh:8 * hh + 8])
            last.then_inc(S["a_done"], 1)

            ab = Count(S["ab_hi"])
            for hi_, lo_, full in ((AH, AL, AT), (BH, BL, BT)):
                dve.wait_ge(ab.sem, ab.after())
                V.tensor_tensor(lo_[:], full[:], hi_[:].bitcast(F32), ALU.subtract).then_inc(S["ab_split"], 1)
            gates, m_hi, m_added = Count(S["gates_back"], 16), Count(S["m_hi"]), Count(S["m_added"])
            done.n = N_MERGE

            def merge(jj, nk):
                dve.wait_ge(gates.sem, gates.after(2))
                dve.wait_ge(fd[0].sem, fd[0].after())
                V.scalar_tensor_tensor(two(GG[:, 0, 0]), two(GG[:, 0, 0]), 1.0, pair(0), ALU.add, ALU.mult
                                       ).then_inc(s_free[0], 1)
                dve.wait_ge(done.sem, done.after())
                V.scalar_tensor_tensor(two(GG[:, 0, 1]), two(GG[:, 0, 1]), 1.0, pair(1), ALU.add, ALU.mult
                                       ).then_inc(s_free[1], 1)
                lo(N_MERGE + 2, nk)
                dve.wait_ge(fd[2].sem, fd[2].after())
                V.scalar_tensor_tensor(two(GG[:, 1, 0]), two(GG[:, 1, 0]), 1.0, pair(2), ALU.add, ALU.mult
                                       ).then_inc(s_free[2], 1)
                dve.wait_ge(done.sem, done.after())
                V.scalar_tensor_tensor(two(GG[:, 1, 1]), two(GG[:, 1, 1]), 1.0, pair(3), ALU.add,
                                       ALU.mult).then_inc(chain.sem, 1)
                dve.wait_ge(chain.sem, chain.after())
                V.tensor_tensor(GG[:, 0], GG[:, 0], GG[:, 1], ALU.add).then_inc(S["m_added"], 1)
                lo(N_MERGE + 3, nk)
                dve.wait_ge(m_hi.sem, m_hi.after())
                V.scalar_tensor_tensor(ML[:, bass.ds(jj * 2, 2), :], GG[:, 0], 0.5,
                                       MH[:, bass.ds(jj * 2, 2), :].bitcast(F32), ALU.mult, ALU.subtract
                                       ).then_inc(S["m_split"], 1)

            with loop(dve, 3, {gates: 2, fd[0]: 1, fd[2]: 1, done: 2, whi: 2, chain: 1, m_hi: 1}) as jj:
                merge(jj, 4)
            merge(3, 8)

            with loop(dve, 2, {whi: 2}):
                lo(N_O)
                lo(N_O + 1)

            y_back = Count(S["y_back"], 16)
            dve.wait_ge(y_back.sem, y_back.after(2))
            taken = Count(S["back_taken"])

            def residual(t):
                p = t % 2
                r = tile_cols(t)[1]
                dve.wait_ge(fd[p].sem, fd[p].after())
                y = YK[0:r, t, :].rearrange("p (a b) -> p a b", a=2)
                V.scalar_tensor_tensor(y, y, ALPHA, PS[0:r, 2 * p:2 * p + 2, :], ALU.mult, ALU.add
                                       ).then_inc(S["back_taken"], 1)

            for t in range(NT):
                residual(t)
            dve.wait_ge(taken.sem, taken.after(NT))
            norm_tiles(YK)
            split_x(XF1)

            V.memset(AB[:, :, 0:2], 0.0).then_inc(S["rows_zeroed"], 1)
            first, gelu, h_hi = Count(S["conv_first"]), Count(S["gelu_done"]), Count(S["h_hi"])

            def conv(m, f):
                dve.wait_ge(first.sem, first.after())
                V.scalar_tensor_tensor(ACC[:, m, DEC:], AB[:, m, 1:1 + META + SEQ],
                                       CV[:, bass.ds(f + FT, 1)], ACC[:, m, DEC:], ALU.mult, ALU.add).then_inc(chain.sem, 1)
                chain.add()
                V.scalar_tensor_tensor(
                    ACC[:, m, 0:DEC], PV[:, bass.ds(f, 1), 1:2 * DEC:2].rearrange("p a c -> p (a c)"),
                    CV[:, bass.ds(f + FT, 1)], ACC[:, m, 0:DEC], ALU.mult, ALU.add).then_inc(chain.sem, 1)
                dve.wait_ge(chain.sem, chain.after())
                V.scalar_tensor_tensor(ACC[:, m, DEC:], AB[:, m, 2:], CV[:, bass.ds(f + 2 * FT, 1)],
                                       ACC[:, m, DEC:], ALU.mult, ALU.add)
                V.scalar_tensor_tensor(
                    ACC[:, m, 0:DEC].rearrange("p (k r) -> p k r", k=2), css(f), CV[:, bass.ds(f + 2 * FT, 1)],
                    ACC[:, m, 0:DEC].rearrange("p (k r) -> p k r", k=2), ALU.mult, ALU.add).then_inc(S["conv_acc"], 1)

            for part, nf in enumerate(FFN_TILES):
                f0 = sum(FFN_TILES[:part])
                na, no = (N_F1, N_F2)[part], (N_F1O, N_F2O)[part]
                hk = nf // 2
                done.n = na + 1

                def ffn_in_pair(i, next_a, next_b, skip):
                    for m in range(2):
                        conv(m, i * 2 + (f0 + m))
                    next_a()
                    for m in range(2):
                        if m == 0:
                            dve.wait_ge(fd[2].sem, fd[2].after())
                        else:
                            dve.wait_ge(done.sem, done.after())
                        dve.wait_ge(gelu.sem, gelu.after())
                        V.tensor_tensor(two(HF[:, m]), two(GL[:, m]), pair(2 + m), ALU.mult).then_inc(S["h_ready"], 1)
                    for m in range(2):
                        dve.wait_ge(h_hi.sem, h_hi.after())
                        fm = bass.ds(i * 2 + m, 1)
                        V.tensor_tensor(FL[:, fm, :].rearrange("p a c -> p (a c)"), HF[:, m],
                                        FH[:, fm, :].rearrange("p a c -> p (a c)").bitcast(F32), ALU.subtract
                                        ).then_inc(s_free[2 + m], 1)
                    next_b()
                    dve.wait_ge(done.sem, done.after(skip))

                with loop(dve, nf // 2 - 1, {whi: 2, chain: 4, first: 2, gelu: 2, h_hi: 2, fd[2]: 1, done: 2}) as i:
                    ffn_in_pair(i, lambda: lo(na), lambda: lo(na + 1), 1)
                ffn_in_pair(nf // 2 - 1, lambda: lo(no, hk), lambda: lo(no + 1, hk), 0)
                last_part = part == 1

                def out_cols(jj, lo_a, lo_b):
                    lo_a()
                    if last_part:
                        tt = TT[:, bass.ds(jj * 2, 2), :]
                        for m in range(2):
                            if m == 0:
                                dve.wait_ge(fd[0].sem, fd[0].after())
                            else:
                                dve.wait_ge(done.sem, done.after(2))
                            t_ = TT[:, bass.ds(jj * 2 + m, 1), :].rearrange("p a c -> p (a c)")
                            V.tensor_tensor(two(t_), two(t_), pair(m), ALU.add).then_inc(s_free[m], 1)
                    lo_b()

                per = {whi: 2}
                if last_part:
                    per[fd[0]], per[done] = 1, 2
                with loop(dve, 3, per) as jj:
                    out_cols(jj, lambda: lo(no, hk), lambda: lo(no + 1, hk))
                if last_part:
                    out_cols(3, lambda: None, lambda: None)
                else:
                    out_cols(3, lambda: lo(N_F2), lambda: lo(N_F2 + 1))

            dve.wait_ge(fd[3].sem, fd[3].after())
            V.tensor_copy(CST[0:2 * FT, 0, :], PS[0:2 * FT, 6, 0:P]).then_inc(S["cst_ready"], 1)
            for k in range(2):
                V.tensor_copy(CST[0:4 * FT, 1 + k, :], PS[0:4 * FT, 7, k * P:(k + 1) * P]).then_inc(S["cst_ready"], 1)
            tok = Count(S["x_tok_ready"])
            dve.wait_ge(tok.sem, tok.after(NT))
            for t in range(NT):
                residual(t)
            dve.wait_ge(taken.sem, taken.after(NT))
            norm_tiles(YK)
            gb = Count(S["gb_landed"], 16)
            dve.wait_ge(gb.sem, gb.after(4))
            normed = Count(S["x_normed"], start=2 * NT)
            for t in range(NT):
                r = tile_cols(t)[1]
                dve.wait_ge(normed.sem, normed.after())
                V.tensor_tensor(YK[0:r, t, :], YK[0:r, t, :], GB2[0:r, 0, :], ALU.mult).then_inc(S["y_scaled"], 1)

        @block.tensor
        def _(pe):
            T = nc.tensor
            free = [Count(s_free[p]) for p in range(4)]
            split = Count(s_wsplit)

            def tile(par, m, nk, xh, xl, k0, p, done=None, start=True, stop=True, halves=(0, 1), banks=None):
                for k in range(nk):
                    for w, xs in ((WH, (xh, xl)), (WL, (xh,))):
                        for j, x in enumerate(xs):
                            for half in halves:
                                bank = 2 * p + half
                                last = T.matmul(PS[:, bank, 0:HALF], w[:, par, k, m * P:(m + 1) * P],
                                                x[:, k0 + k, half * HALF:(half + 1) * HALF],
                                                start=start and k == 0 and w is WH and j == 0,
                                                stop=stop and k == nk - 1 and w is WL)
                if done is not None:
                    last.then_inc(done, 1)

            def small(p, lhs, rhs, done):
                for half in range(2):
                    for i, (a, b) in enumerate(zip(lhs, rhs)):
                        last = T.matmul(PS[:, 2 * p + half, 0:HALF], a, b[:, half * HALF:(half + 1) * HALF],
                                        start=i == 0, stop=i == len(lhs) - 1)
                last.then_inc(done, 1)

            def forward(x):
                for t in range(NT):
                    if t >= 2:
                        pe.wait_ge(x_split.sem, x_split.after())
                    pe.wait_ge(normed.sem, normed.after())
                    r = tile_cols(t)[1]
                    for k in range(KT):
                        last = T.transpose(PS[:, 4 + 2 * (t % 2) + k // 4, (k % 4) * P:(k % 4) * P + r],
                                           x[0:r, t, k * P:(k + 1) * P], IDENT[0:r, 0:r])
                    last.then_inc(S["ln_turned"], 1)
                pe.wait_ge(x_split.sem, x_split.after(2))

            def backward():
                for t in range(NT):
                    if t >= 2:
                        pe.wait_ge(taken.sem, taken.after())
                    c, r = evac_cols(t)
                    for k in range(KT):
                        last = T.transpose(PS[0:r, 2 * (t % 2) + k // 4, (k % 4) * P:(k % 4 + 1) * P], TT[:, k, c],
                                           IDENT)
                    last.then_inc(s_fd[t % 2], 1)
                pe.wait_ge(taken.sem, taken.after(2))

            pe.sem_inc(s_free[0], 1)
            pe.sem_inc(s_free[1], 1)
            pe.sem_inc(s_free[2], 1)
            pe.sem_inc(s_free[3], 1)
            x_split, normed, taken = Count(S["x_split"]), Count(S["x_normed"]), Count(S["back_taken"])
            c1, c2 = Count(S["consts_landed"], 16), Count(S["consts2_landed"], 16)
            pe.wait_ge(c1.sem, c1.after(12))
            pe.wait_ge(free[0].sem, free[0].after())
            T.transpose(PS[:, 0, 0:41], VR[0:41, 0, :], IDENT[0:41, 0:41])
            T.transpose(PS[:, 1, 0:4 * FT], VR[0:4 * FT, 1, :], IDENT[0:4 * FT, 0:4 * FT]).then_inc(s_fd[0], 1)
            pe.wait_ge(free[2].sem, free[2].after())
            pe.wait_ge(free[3].sem, free[3].after())
            forward(XK)
            pe.sem_inc(s_free[2], 1)
            pe.sem_inc(s_free[3], 1)
            vt = Count(S["vectors_T_ready"])
            pe.wait_ge(vt.sem, vt.after())
            pe.sem_inc(s_free[0], 1)
            pe.wait_ge(c2.sem, c2.after(10))
            pe.wait_ge(free[1].sem, free[1].after())
            rows = CN[:].rearrange("p a b -> p (a b)")
            for f in range(FT):
                last = T.transpose(PS[:, 2, 16 * f:16 * f + 16], rows[:, f * P:(f + 1) * P], IDENT[0:16, 0:16])
            last.then_inc(s_fd[1], 1)

            k_feat, q_feat, g_ready = Count(S["k_feat"]), Count(S["q_feat"]), Count(S["g_ready"])
            inner, sn, ot = Count(S["inner_ready"]), Count(S["sn_ready"]), Count(S["ot_ready"])
            sq, sd, tok = Count(S["sq_ready"]), Count(S["sd_ready"]), Count(S["tok_ready"])

            def outputs():
                pe.wait_ge(inner.sem, inner.after())
                for t in range(1, NT):
                    out = PS[:, 6, P * (t - 1):P * t]
                    T.matmul(out, VTOK[:, t, :], INT[:, t - 1, :], start=True, stop=False)
                    T.matmul(out, RS[:, t - 1, :], RQD[:, t - 1, :], start=False, stop=True)
                T.matmul(PS[:, 7, 0:T0], VTOK[0:T0, 0, :], IN0[0:T0, :], start=True, stop=True).then_inc(s_fd[3], 1)
                for j in range(2):
                    last = T.matmul(PS[:, 4 + j, :], KTOK0[0:DEC, :],
                                    VBLK[0:DEC, 4 * j:4 * j + 4, :].rearrange("p b v -> p (b v)"), start=True, stop=True)
                last.then_inc(s_fd[2], 1)

            def sample_out():
                pe.wait_ge(sn.sem, sn.after())
                for b in range(DEC):
                    last = T.matmul(PS[:, 6, b:b + 1], ST[:, b, :], RQ[:, b:b + 1], start=True, stop=True)
                last.then_inc(s_fd[3], 1)

            def centre():
                pe.wait_ge(ot.sem, ot.after())
                small(2, [CENTRE], [OT], s_fa[2])

            def variance():
                pe.wait_ge(sq.sem, sq.after())
                small(3, [MEAN], [OSQ], s_fa[3])

            def ret_head(prev):
                pe.wait_ge(split.sem, split.after())
                if not prev:
                    pe.wait_ge(free[0].sem, free[0].after())
                tile(0, 0, 8, XH, XL, 0, 0, s_fa[0])
                if prev:
                    outputs()
                    pe.wait_ge(g_ready.sem, g_ready.after())
                else:
                    pe.wait_ge(free[1].sem, free[1].after())
                tile(0, 1, 8, XH, XL, 0, 1, s_done)
                if prev:
                    sample_out()
                    centre()
                pe.wait_ge(split.sem, split.after())
                pe.wait_ge(k_feat.sem, k_feat.after())
                tile(1, 0, 8, XH, XL, 0, 0, s_fa[0])
                if prev:
                    variance()
                else:
                    pe.wait_ge(free[2].sem, free[2].after())
                pe.wait_ge(free[1].sem, free[1].after())
                for t in range(1, NT):
                    c, _ = evac_cols(t)
                    T.transpose(PS[:, 4, P * (t - 1):P * t], RK[:, c], IDENT)
                    last = T.transpose(PS[:, 5, P * (t - 1):P * t], RV[:, c], IDENT)
                last.then_inc(s_fd[2], 1)
                if prev:
                    pe.wait_ge(sd.sem, sd.after())
                else:
                    pe.wait_ge(free[3].sem, free[3].after())
                T.transpose(PS[0:T0, 6, 0:P], RK[:, 0:T0], IDENT)
                T.transpose(PS[0:T0, 6, P:2 * P], RV[:, 0:T0], IDENT).then_inc(s_fd[3], 1)
                tile(1, 1, 8, XH, XL, 0, 1, s_done)
                pe.wait_ge(tok.sem, tok.after())
                pe.wait_ge(q_feat.sem, q_feat.after())
                for t in range(1, NT):
                    c, _ = evac_cols(t)
                    T.matmul(PS[:, 4, P * (t - 1):P * t], RK[:, c], RQ[:, c], start=True, stop=True)
                    last = T.matmul(PS[:, 5, P * (t - 1):P * t], KDEC[:, t, :], VTOK[:, t, :], start=True, stop=True)
                last.then_inc(s_fd[2], 1)
                T.matmul(PS[0:T0, 6, 0:T0], RK[:, 0:T0], RQ[:, 0:T0], start=True, stop=True)
                T.matmul(PS[:, 6, P:2 * P], KDEC[0:T0, 0, :], VTOK[0:T0, 0, :], start=True, stop=True
                         ).then_inc(s_fd[3], 1)

            ret_head(False)
            with loop(pe, RH - 1, {split: 2, k_feat: 1, q_feat: 1, g_ready: 1, inner: 1, sn: 1, ot: 1, sq: 1, sd: 1,
                                   tok: 1, free[1]: 1}):
                ret_head(True)
            outputs()
            sample_out()
            centre()
            variance()
            pe.wait_ge(sd.sem, sd.after())
            pe.wait_ge(g_ready.sem, g_ready.after())

            lat_sq, lat_sd, normed_l = Count(S["lat_sq"]), Count(S["lat_sd"]), Count(S["lat_normed"])
            pe.wait_ge(split.sem, split.after())
            tile(0, 0, 8, XH, XL, 0, 0, s_fa[0])
            tile(0, 1, 8, XH, XL, 0, 1, s_done)
            pe.wait_ge(split.sem, split.after())
            pe.wait_ge(free[0].sem, free[0].after())
            tile(1, 0, 8, XH, XL, 0, 0, s_fa[0])
            pe.wait_ge(free[1].sem, free[1].after())
            tile(1, 1, 8, XH, XL, 0, 1, s_done)
            pe.wait_ge(lat_sq.sem, lat_sq.after())
            small(2, [ONES] * 3, [QSQ[:, j, :] for j in range(3)], s_fa[2])
            pe.wait_ge(split.sem, split.after())
            tile(0, 0, 8, XH, XL, 0, 0, s_fa[0])
            pe.wait_ge(free[1].sem, free[1].after())
            tile(0, 1, 8, XH, XL, 0, 1, s_done)
            pe.wait_ge(lat_sq.sem, lat_sq.after())
            small(3, [ONES] * 2, [QSQ[:, j, :] for j in range(2)], s_fa[3])
            pe.wait_ge(lat_sd.sem, lat_sd.after(2))
            pe.wait_ge(normed_l.sem, normed_l.after(2))
            for t in range(1, NT):
                c, _ = evac_cols(t)
                for j in range(2):
                    at_ = (t - 1) % 2 * KVL + j * P
                    last = T.transpose(PS[:, 4 + (t - 1) // 2, at_:at_ + P], CNT[:, j, c], IDENT)
            last.then_inc(s_fd[2], 1)
            for j in range(2):
                T.transpose(PS[0:T0, 6, j * P:(j + 1) * P], CNT[:, j, 0:T0], IDENT)
            for t in range(1, NT):
                c, _ = evac_cols(t)
                T.transpose(PS[:, 7, ROPE * (t - 1):ROPE * t], KRT[0:ROPE, c], IDENT[0:ROPE, 0:ROPE])
            T.transpose(PS[0:T0, 7, P:P + ROPE], KRT[0:ROPE, 0:T0], IDENT[0:ROPE, 0:ROPE]).then_inc(s_fd[3], 1)
            tok_out = Count(S["tok_out_ready"])

            pe.wait_ge(free[0].sem, free[0].after())
            pe.sem_inc(S["gate_free0"], 1)
            pe.sem_inc(S["gate_free1"], 1)
            gate_free = [Count(S[f"gate_free{j}"]) for j in range(2)]
            head_w, uk_T, q_heads = Count(S["head_w_landed"], 16), Count(S["uk_T_ready"]), Count(S["q_heads_ready"])
            probs, pt_a, pt_d, attn = Count(S["probs_ready"]), Count(S["pt_act"]), Count(S["pt_dve"]), Count(S["attn_done"])

            def gate(g):
                if g % 4 == 0:
                    pe.wait_ge(split.sem, split.after())
                half = g % 2
                pe.wait_ge(gate_free[half].sem, gate_free[half].after())
                par = (N_GATE + g // 4) % 2
                tile(par, (g // 2) % 2, 8, XH, XL, 0, 0, s_done if g % 4 == 3 else S["gate_full"], halves=(half,))

            def scores(t):
                c, r = evac_cols(t)
                n = META + P * (t - 1)
                for hh in range(2):
                    if t:
                        T.matmul(PS[:, 4 + hh, 0:n], QT[0:QD_, hh, c], KTB[0:QD_, hh, DEC:DEC + n], start=True, stop=True)
                        last = T.matmul(PS[:, 6, hh * P:(hh + 1) * P], QT[0:QD_, hh, c], KTB[0:QD_, hh, c],
                                        start=True, stop=True)
                    else:
                        last = T.matmul(PS[0:r, 6, hh * P:hh * P + META], QT[0:QD_, hh, c], KTB[0:QD_, hh, DEC:T0],
                                        start=True, stop=True)
                last.then_inc(S["scores_full"], 1)

            def turn_probs(t):
                pe.wait_ge(probs.sem, probs.after())
                pe.sem_inc(S["go_on"])
                r = tile_cols(t)[1]
                for hh in range(2):
                    for k in range(t + 1):
                        e0_, w = (0, META) if k == 0 else (META + P * (k - 1), P)
                        bank, at_ = (4 + hh, k * P) if k < 4 else (6, hh * P)
                        last = T.transpose(PS[0:w, bank, at_:at_ + r], EX[0:r, hh, e0_:e0_ + w], IDENT[0:r, 0:r])
                last.then_inc(S["probs_turned"], 1)

            def weigh(t):
                pe.wait_ge(pt_a.sem, pt_a.after())
                pe.wait_ge(pt_d.sem, pt_d.after())
                r = tile_cols(t)[1]
                for hh in range(2):
                    rows_ = slice(64 * hh, 64 * hh + 64)
                    out = PS[rows_, 2, P * (t - 1):P * t] if t else PS[rows_, 3, 0:T0]
                    for k in range(t + 1):
                        w = P if k else META
                        last = T.matmul(out, VB[0:w, k, rows_], PTS[0:w, hh, k, 0:r], start=k == 0, stop=k == t)
                return last

            def attn_pair(p):
                pe.wait_ge(head_w.sem, head_w.after(7))
                pe.wait_ge(free[2].sem, free[2].after())
                small(2, [UQ[:, k, 0, :] for k in range(3)], [QN[:, k, :] for k in range(3)], s_fd[2])
                pe.wait_ge(free[3].sem, free[3].after())
                small(3, [UQ[:, k, 1, :] for k in range(3)], [QN[:, k, :] for k in range(3)], s_fd[3])
                small(1, [UK[:, k, :] for k in range(2)], [CNT[:, k, :] for k in range(2)], s_fd[1])
                gate(0)
                pe.wait_ge(free[2].sem, free[2].after())
                pe.wait_ge(free[3].sem, free[3].after())
                for t in range(NT):
                    c, r = evac_cols(t)
                    if t == 0:
                        c, r = slice(DEC, T0), META
                    for k in range(2):
                        out = PS[:, 4, P * (t - 1):P * t] if t else PS[0:META, 5, 0:P]
                        last = T.matmul(out, CNT[:, k, c], UV[:, k, bass.ds(p * P, P)], start=k == 0, stop=k == 1)
                last.then_inc(s_fd[2], 1)
                for hh in range(2):
                    for k in range(2):
                        last = T.transpose(PS[0:NOPE, 6, (2 * hh + k) * P:(2 * hh + k + 1) * P],
                                           UK[:, k, hh * NOPE:(hh + 1) * NOPE], IDENT)
                last.then_inc(S["proj_done"], 1)
                gate(1)
                pe.wait_ge(uk_T.sem, uk_T.after())
                pe.wait_ge(q_heads.sem, q_heads.after())
                for k in range(2):
                    for hh in range(2):
                        last = T.matmul(PS[:, 6, (2 * k + hh) * DEC:(2 * k + hh + 1) * DEC], UKT[0:NOPE, hh, k, :],
                                        QT[0:NOPE, hh, 0:DEC], start=True, stop=True)
                last.then_inc(s_fd[3], 1)
                gate(2)
                pe.wait_ge(free[2].sem, free[2].after())
                pe.wait_ge(free[3].sem, free[3].after())
                for t in range(NT):
                    scores(t)
                    if t:
                        gate(2 + t)
                    turn_probs(t)
                    last = weigh(t)
                last.then_inc(s_fd[1], 1)
                pe.sem_inc(s_free[2], 1)
                pe.sem_inc(s_free[3], 1)
                gate(7)
                pe.wait_ge(attn.sem, attn.after())

            pe.wait_ge(tok_out.sem, tok_out.after())
            pe.sem_inc(s_free[3], 1)
            with loop(pe, 4, {head_w: 7, free[2]: 3, free[3]: 3, split: 2, gate_free[0]: 4, gate_free[1]: 4, uk_T: 1,
                              q_heads: 1, probs: NT, pt_a: NT, pt_d: NT, attn: 1}) as p:
                attn_pair(p)

            pe.wait_ge(free[2].sem, free[2].after())
            pe.wait_ge(free[3].sem, free[3].after())
            pe.wait_ge(gate_free[0].sem, gate_free[0].after())
            pe.wait_ge(gate_free[1].sem, gate_free[1].after())
            pages = [[Count(s_pg[j][c], 16) for c in range(NCH)] for j in range(2)]
            rope_p = [Count(S[f"rope_pages{j}"], 16) for j in range(2)]
            ct_a, ct_d, bank_free = Count(S["ct_act"]), Count(S["ct_dve"]), Count(S["s_bank_free"])
            mx, dg, sums, rs = Count(S["mx_ready"]), Count(S["dg_ready"]), Count(S["sum_ready"]), Count(S["rs_ready"])
            olat = Count(S["olat_ready"])
            qrb = Count(S["qrb_ready"])
            pe.wait_ge(qrb.sem, qrb.after())

            def turn_rope(par):
                pe.wait_ge(rope_p[par].sem, rope_p[par].after())
                for c in range(NCH):
                    last = T.transpose(PS[:, 2 + c // 4, P * (c % 4):P * (c % 4 + 1)],
                                       PGR[:, par, 4 * c:4 * c + 4, :].rearrange("p r d -> p (r d)"), IDENT)
                last.then_inc(S["rope_turned"], 1)

            def turn_chunk(par, c):
                pe.wait_ge(pages[par][c].sem, pages[par][c].after())
                for ct in range(2):
                    for r in range(4):
                        last = T.transpose(PS[:, 2 * (c % 2) + ct, P * r:P * (r + 1)],
                                           PGC[:, par, 4 * c + r, ct * P:(ct + 1) * P], IDENT)
                last.then_inc(S["chunk_turned"], 1)

            def q_of(b, ct, n=P):
                return QAB[0:n, ct, bass.ds(b, 1), :].rearrange("p b h -> p (b h)")

            def score_chunk(c, b, wait_bank):
                pe.wait_ge(ct_a.sem, ct_a.after())
                pe.wait_ge(ct_d.sem, ct_d.after())
                if c == 0 and wait_bank:
                    pe.wait_ge(bank_free.sem, bank_free.after())
                T.matmul(PS[:, 6, 32 * c:32 * c + 32], RTT[:, c, :],
                         QRB[:, bass.ds(b, 1), :, :].rearrange("p b g h -> p (b g h)"), start=c == 0, stop=False,
                         skip_group_check=True)
                g = c % 4
                for ct in range(2):
                    for x in (CTH, CTL):
                        last = T.matmul(PS[:, 4 + c // 4, :], QB[:, ct, 96 - 32 * g:224 - 32 * g],
                                        x[:, c % 2].rearrange("p a b -> p (a b)")[:, 512 * ct:512 * ct + 512],
                                        start=g == 0 and ct == 0 and x is CTH, stop=g == 3 and ct == 1 and x is CTL)
                last.then_inc(S["chunk_scored"], 1)

            def add_parts(a):
                pe.wait_ge(parts.sem, parts.after())
                for r in range(4):
                    out = PS[:, 6, 0:256].rearrange("p (a g r h) -> p a r g h", a=2, g=4, r=4)[:, a, r]
                    last = T.matmul(out, SPART[:, a, P * r:P * (r + 1)], SMALL[:, 26:58], start=False,
                                    stop=a == 1 and r == 3, skip_group_check=True)
                return last

            def score_new(b):
                out = PS[0:DEC, 6, 256:264]
                for ct in range(2):
                    T.matmul(out, CN8[:, ct, :], q_of(b, ct), start=False, stop=False, skip_group_check=True)
                T.matmul(out, KR8[:], QRB[:, bass.ds(b, 1), 0, :].rearrange("p b h -> p (b h)"),
                         start=False, stop=True, skip_group_check=True)

            def max_turn(par):
                pe.wait_ge(mx.sem, mx.after())
                T.transpose(PS[0:8, 7, 0:P], SSM[:, par, 0:8], IDENT).then_inc(S["mx_turned"], 1)

            def max_spread(par):
                pe.wait_ge(dg.sem, dg.after())
                T.matmul(PS[:, 7, P:P + 8], ONES[0:8, :], SSM[0:8, par, 16:24], start=True, stop=True
                         ).then_inc(S["mx_spread"], 1)

            def sum_spread(par):
                pe.wait_ge(sums.sem, sums.after())
                T.matmul(PS[:, 7, P + 8:P + 16], ONES, SSM[:, par, 24:32], start=True, stop=True
                         ).then_inc(S["sum_spread"], 1)

            def latent_turn():
                pe.wait_ge(o_parts.sem, o_parts.after())
                for ct in range(2):
                    last = T.matmul(PS[:, 7, 144 + 8 * ct:152 + 8 * ct], OPART[:, ct * P:(ct + 1) * P],
                                    SMALL[0:2 * HEADS, 26:26 + HEADS], start=True, stop=True)
                last.then_inc(S["lat_turned"], 1)

            def sample_weigh(par, midway=None):
                pe.wait_ge(p_split.sem, p_split.after())
                pe.wait_ge(rs.sem, rs.after())
                out = PS[0:2 * HEADS, 7, 256:256 + KVL]
                for c in range(NCH):
                    if c == 3 and midway:
                        midway()
                    pe.wait_ge(page_split.sem, page_split.after())
                    for r in range(4):
                        for x in (PHI, PLO):
                            last = T.matmul(out, PHL[:, 4 * c + r, :], x[c % 4][:, r, :],
                                            start=c == 0 and r == 0 and x is PHI, stop=False, skip_group_check=True)
                    last.then_inc(S["pv_chunk"], 1)
                T.matmul(PS[0:HEADS, 7, 256:256 + KVL], PB[0:DEC, par, 32, :], CTX[0:DEC, :], start=False, stop=True,
                         skip_group_check=True).then_inc(S["pv_full"], 1)

            def second_turn(par):
                pe.wait_ge(rope_back.sem, rope_back.after())
                turn_chunk(par, 1)

            def first_scores(b, wait_bank):
                pe.wait_ge(q_parts.sem, q_parts.after())
                score_chunk(0, b, wait_bank)

            def sample(par, b, prev, more=True):
                for c in range(1, NCH):
                    if c + 1 < NCH:
                        turn_chunk(par, c + 1)
                    else:
                        add_parts(0)
                    score_chunk(c, b, False)
                    if prev is not None:
                        {2: max_turn, 4: max_spread, 7: sum_spread}.get(c, lambda q: None)(prev)
                score_new(b)
                if more:
                    turn_chunk(1 - par, 0)
                    turn_rope(1 - par)
                add_parts(1).then_inc(S["s_full"], 1)
                if prev is not None:
                    sample_weigh(prev, (lambda: second_turn(1 - par)) if more else None)
                elif more:
                    second_turn(1 - par)
                if more:
                    first_scores(b + 1, True)
                if prev is not None:
                    latent_turn()

            rope_back, q_parts, parts = Count(S["rope_back"]), Count(S["q_parts"]), Count(S["parts_back"])
            o_parts, page_split, p_split = Count(S["o_parts"]), Count(S["page_split"]), Count(S["p_split"])
            turn_chunk(0, 0)
            turn_rope(0)
            second_turn(0)
            first_scores(0, False)
            sample(0, 0, None)
            per = {ct_a: 2 * NCH, ct_d: 2 * NCH, bank_free: 2, mx: 2, dg: 2, sums: 2, rs: 2,
                   rope_p[0]: 1, rope_p[1]: 1, rope_back: 2, q_parts: 2, parts: 4, o_parts: 2, p_split: 2,
                   page_split: 2 * NCH}
            per.update({pages[j][c]: 1 for j in range(2) for c in range(NCH)})
            with loop(pe, 3, per) as i:
                for par in range(2):
                    sample(1 - par, i * 2 + (1 + par), par)
            sample(1, DEC - 1, 0, False)
            pe.wait_ge(olat.sem, olat.after(DEC - 1))
            max_turn(1)
            max_spread(1)
            sum_spread(1)
            sample_weigh(1)
            latent_turn()
            pe.wait_ge(olat.sem, olat.after())
            for p in range(4):
                for ct in range(2):
                    last = T.matmul(PS[:, 7, 16 * p:16 * p + 16], UV[:, ct, p * P:(p + 1) * P],
                                    OL[:, ct, 2 * p:2 * p + 2, :].rearrange("p h b -> p (h b)"),
                                    start=ct == 0, stop=ct == 1)
            last.then_inc(S["a_s_full"], 1)
            ab, m_added, m_split = Count(S["ab_split"]), Count(S["m_added"]), Count(S["m_split"])
            pe.wait_ge(ab.sem, ab.after(2))

            pe.sem_inc(s_free[0], 1)
            pe.sem_inc(s_free[1], 1)
            pe.sem_inc(s_free[2], 1)

            def merge():
                pe.wait_ge(split.sem, split.after())
                pe.wait_ge(free[0].sem, free[0].after())
                tile(N_MERGE % 2, 0, 4, AH, AL, 0, 0, s_fd[0])
                pe.wait_ge(free[1].sem, free[1].after())
                tile(N_MERGE % 2, 1, 4, AH, AL, 0, 1, s_done)
                pe.wait_ge(split.sem, split.after())
                pe.wait_ge(free[2].sem, free[2].after())
                tile((N_MERGE + 1) % 2, 0, 4, BH, BL, 0, 2, s_fd[2])

            def merge_last():
                tile((N_MERGE + 1) % 2, 1, 4, BH, BL, 0, 3, s_done)

            merge()
            merge_last()
            with loop(pe, 3, {split: 2, free[0]: 1, free[1]: 1, free[2]: 1, m_added: 1}):
                merge()
                pe.wait_ge(m_added.sem, m_added.after())
                merge_last()
            pe.wait_ge(m_added.sem, m_added.after())
            pe.sem_inc(s_free[3], 1)
            pe.wait_ge(m_split.sem, m_split.after(4))

            with loop(pe, 2, {split: 2, free[0]: 1, free[1]: 1, free[2]: 1, free[3]: 1}):
                for j in range(2):
                    pe.wait_ge(split.sem, split.after())
                    for m in range(2):
                        pe.wait_ge(free[2 * j + m].sem, free[2 * j + m].after())
                        tile((N_O + j) % 2, m, 8, MH, ML, 0, 2 * j + m, s_done if m else s_fa[2 * j])

            pe.wait_ge(free[0].sem, free[0].after())
            pe.wait_ge(free[1].sem, free[1].after())
            pe.wait_ge(free[2].sem, free[2].after())
            pe.wait_ge(free[3].sem, free[3].after())
            backward()
            forward(YK)
            pe.sem_inc(s_free[0], 1)
            pe.sem_inc(s_free[1], 1)
            pe.sem_inc(s_free[2], 1)
            pe.sem_inc(s_free[3], 1)

            for part, nf in enumerate(FFN_TILES):
                na, no = (N_F1, N_F2)[part], (N_F1O, N_F2O)[part]
                hk = nf // 2
                with loop(pe, nf // 2, {split: 2, free[0]: 1, free[1]: 1, free[2]: 1, free[3]: 1}):
                    for j in range(2):
                        pe.wait_ge(split.sem, split.after())
                        for m in range(2):
                            pe.wait_ge(free[2 * j + m].sem, free[2 * j + m].after())
                            tile((na + j) % 2, m, 8, XH, XL, 0, 2 * j + m, s_done if m else s_fa[0] if j == 0 else s_fd[2])
                pe.wait_ge(free[2].sem, free[2].after())
                pe.wait_ge(free[3].sem, free[3].after())
                with loop(pe, 4, {split: 2, free[0]: 1, free[1]: 1}):
                    pe.wait_ge(split.sem, split.after())
                    pe.wait_ge(free[0].sem, free[0].after())
                    tile(no % 2, 0, hk, FH, FL, 0, 0, None, stop=False)
                    pe.wait_ge(free[1].sem, free[1].after())
                    tile(no % 2, 1, hk, FH, FL, 0, 1, s_done, stop=False)
                    pe.wait_ge(split.sem, split.after())
                    tile((no + 1) % 2, 0, hk, FH, FL, hk, 0, s_fa[0] if part == 0 else s_fd[0], start=False)
                    tile((no + 1) % 2, 1, hk, FH, FL, hk, 1, s_done, start=False)
                if part == 0:
                    pe.sem_inc(s_free[2], 1)
                    pe.sem_inc(s_free[3], 1)
            T.transpose(PS[0:2 * FT, 6, 0:P], CSP[:].rearrange("p f c -> p (f c)"), IDENT)
            for k in range(2):
                last = T.transpose(PS[0:4 * FT, 7, k * P:(k + 1) * P], CSS[:, k, :, :].rearrange("p f r -> p (f r)"), IDENT)
            last.then_inc(s_fd[3], 1)
            pe.wait_ge(free[0].sem, free[0].after())
            pe.wait_ge(free[1].sem, free[1].after())
            backward()


_INS = ["x_prompt", "x_sample", "cache_kv_latent", "cache_k_rope", "state_retention", "state_ffn_conv", "page_table",
        "meta_tokens", "ln0_g", "ln0_b", "w_in", "q_norm_g", "kv_norm_g", "w_uq", "w_uk", "w_uv", "ret_gn_g",
        "w_attn_out", "w_ret_out", "w_o", "ln1_g", "ln1_b", "w_ffn_in", "conv_w", "conv_b", "w_ffn_out", "ln2_g",
        "ln2_b"]
_OUTS = [(1, SEQ, D), (DEC, 1, D), (1, 1, SEQ + META, KVL), (1, 1, SEQ + META, ROPE), (1, 1, RH, RD, RD),
         (1, 1, 2, DFF), (1, DEC, 1, KVL), (1, DEC, 1, ROPE), (1, DEC, RH, RD, RD), (1, DEC, 2, DFF)]


def kernel(**inputs):
    import numpy as _np
    import concourse.bacc as _bacc
    from concourse import mybir as _mybir
    from concourse.bass_utils import run_bass_kernel_spmd as _run

    nc = _bacc.Bacc("TRN2", target_bir_lowering=False, num_devices=1)
    arrays, ins, outs = {}, {}, []
    for name in _INS:
        a = _np.ascontiguousarray(inputs[name])
        arrays[f"in_{name}_dram"] = a
        ins[name] = nc.dram_tensor(f"in_{name}_dram", a.shape, _mybir.dt.from_np(a.dtype), kind="ExternalInput").ap()
    for i, shape in enumerate(_OUTS):
        outs.append(nc.dram_tensor(f"out_{i}_dram", shape, _mybir.dt.float32, kind="ExternalOutput").ap())
    build(nc, ins, outs)
    r = _run(nc, [arrays], core_ids=[0])
    return tuple(r.results[0][f"out_{i}_dram"] for i in range(len(_OUTS)))
```

```python
from contextlib import ExitStack, contextmanager

import numpy as np
import concourse.bass as bass
from concourse import mybir

ALU = mybir.AluOpType
ACT = mybir.ActivationFunctionType
F32 = mybir.dt.float32
F32R = mybir.dt.float32r
I32 = mybir.dt.int32
AX = mybir.AxisListType.X

P = 128
D = 1024
KT = D // P
SEQ, META, DEC = 512, 16, 8
COLS = DEC + META + SEQ
HALF = COLS // 2
T0 = DEC + META
NT = 5
HEADS, NOPE, ROPE, VD = 8, 64, 32, 64
QD_ = NOPE + ROPE
QL, KVL = 384, 256
RH, RD = 4, 128
DFF = 2816
FT = DFF // P
PAGE, NPAGES = 128, 32
PAST = PAGE * NPAGES
NCH = 8
ALPHA = 2.0 ** 0.25
LN_EPS, RMS_EPS = 1e-5, 1e-6
SCALE = float(QD_) ** -0.5
NEG = -1e30
OFF_Q, OFF_C, OFF_KR, OFF_RQ = 0, 384, 640, 672
OFF_RK, OFF_RV, OFF_RG = 1184, 1696, 2208
OFF_GA, OFF_GB = 2720, 3744
SLOT_W = 256
FFN_TILES = (12, 10)


def tile_cols(t):
    return (0, T0) if t == 0 else (T0 + P * (t - 1), P)


def shape_constants():
    f32 = np.float32
    pos = np.concatenate([np.full(DEC, PAST, f32), np.arange(META + SEQ, dtype=f32)])

    def rope_rows(half):
        inv = (10000.0 ** (-np.arange(half, dtype=np.float64) / half)).astype(f32)
        ang = (pos[None, :] * inv[:, None]).astype(f32).astype(np.float64)
        c, s = np.cos(ang), np.sin(ang)
        return np.concatenate([c, c]).astype(f32), np.concatenate([-s, s]).astype(f32)

    rc, rs = rope_rows(RD // 2)
    mc, ms = rope_rows(ROPE // 2)
    c = {"ret_rope": np.stack([rc, rs], 1), "mla_rope": np.concatenate([mc, ms], 0)}
    lg = np.log(1.0 - 2.0 ** (-5.0 - np.arange(RH)))
    i = np.arange(P)
    head = np.zeros((P, RH, 2 * P + T0 + 8), f32)
    for h in range(RH):
        d = i[None, :] - i[:, None]
        head[:, h, 0:P] = np.where(d >= 0, np.exp(np.maximum(d, 0) * lg[h]), 0.0)
        head[:, h, P:2 * P] = np.exp((i[None, :] + 1.0) * lg[h])
        m = head[:, h, 2 * P:2 * P + T0]
        m[DEC:T0, DEC:T0] = head[0:META, h, 0:META]
        head[:, h, 2 * P + T0] = np.exp((P - 1.0 - i) * lg[h])
        head[DEC:T0, h, 2 * P + T0 + 1] = np.exp((META - 1.0 - np.arange(META)) * lg[h])
        head[:, h, 2 * P + T0 + 2] = np.exp(lg[h])
        head[:, h, 2 * P + T0 + 3] = np.exp(P * lg[h])
    c["ret_head"] = head
    sq = np.zeros((P, 5, P), f32)
    sq[:, 0] = np.eye(P)
    sq[:, 1] = 1.0
    sq[:, 2] = 1.0 / P
    sq[:, 3] = np.eye(P) - 1.0 / P
    sq[:, 4] = np.where(i[None, :] <= i[:, None], 0.0, NEG)
    c["square"] = sq
    m = np.zeros((P, 58), f32)
    jj = np.arange(META)
    m[DEC:T0, 0:META] = np.where(jj[None, :] <= jj[:, None], 0.0, NEG)
    m[0:DEC, 16:24] = np.where(np.eye(DEC) > 0, 0.0, NEG)
    m[:, 24] = i % 4
    m[:, 25] = 8 * (i % 4)
    for g in range(4):
        for j in range(2 * HEADS):
            m[32 * g + j, 26 + HEADS * g + j % HEADS] = 1.0
    c["small"] = m
    return c


class Count:

    def __init__(self, sem, step=1, start=0):
        self.sem, self.step, self.n, self.term, self.inside = sem, step, start, 0, False

    def add(self, k=1):
        assert not k or not Count.looping or self.inside, f"not declared in the loop: {self.sem}"
        self.n += k

    def after(self, k=1):
        self.add(k)
        assert self.n > 0, f"a wait against zero: {self.sem}"
        return self.term + self.n * self.step

    looping = False


@contextmanager
def loop(eng, count, per):
    with eng.Fori(0, count) as i:
        begun = {}
        for c, k in per.items():
            begun[c], c.term, c.inside = c.n, i * (k * c.step), True
        Count.looping = True
        yield i
        Count.looping = False
        bad = {str(c.sem): (c.n - begun[c], k) for c, k in per.items() if c.n - begun[c] != k}
        assert not bad, f"counts per iteration differ (found, declared): {bad}"
    for c, k in per.items():
        c.n += (count - 1) * k
        c.term, c.inside = 0, False


def build(nc, ins, outs):
    ctx = ExitStack()
    with ctx:
        consts = {k: nc.inline_tensor(v, name=k + "_const") for k, v in shape_constants().items()}
        sems = {}

        def sem(name):
            sems[name] = ctx.enter_context(nc.semaphore(name))
            return sems[name]

        base = -(-nc.sbuf_base // 32) * 32
        top = [0]

        def fixed(name, shape, dt=F32):
            n = int(np.prod(shape[1:])) * 4
            t = nc.alloc_sbuf_tensor_at(name, shape, dt, offset=base + top[0])
            top[0] += -(-n // 32) * 32
            return t

        XH = fixed("x_hi", [P, KT, COLS], F32R)
        XL = fixed("x_lo", [P, KT, COLS], F32R)
        RAW = fixed("w_raw", [P, 2, 8, SLOT_W])
        WH = fixed("w_hi", [P, 2, 8, SLOT_W], F32R)
        WL = fixed("w_lo", [P, 2, 8, SLOT_W], F32R)
        ab_off = top[0]
        AT = fixed("attn_T", [P, 4, COLS])
        BT = fixed("ret_T", [P, 4, COLS])
        TT = nc.alloc_sbuf_tensor_at("sum_T", [P, KT, COLS], F32, offset=base + ab_off)
        SQ = fixed("square_consts", [P, 5, P])
        SMALL = fixed("small_consts", [P, 58])
        VT = fixed("vectors_T", [P, 9])
        CV = fixed("conv_T", [P, 88])
        PV = fixed("conv_prev_T", [P, FT, 2 * DEC])
        CSP = fixed("conv_last_T", [P, FT, 2])
        CSS = fixed("conv_new_T", [P, 2, FT, 4])
        QS = fixed("q_sample", [P, HEADS, DEC])
        EPS = fixed("eps", [P, 2])
        STAT = fixed("stats", [P, NT, 2, 6])
        MV = fixed("mean_var", [P, NT, 2])
        SDV = fixed("std", [P, NT])
        RSV = fixed("rstd", [P, NT])
        SMX = fixed("softmax_small", [P, 32])
        PTI = fixed("page_table_rows", [P, DEC], I32)
        IDX = fixed("page_rows", [P, DEC, NCH + 1], I32)
        IDB = fixed("page_rows_now", [P, 2, NCH + 1], I32)
        CN8 = fixed("latent_new_T", [P, 2, DEC])
        KR8 = fixed("rope_new_T", [P, DEC])
        arena = top[0]

        def at(name, off, shape, dt=F32):
            n = int(np.prod(shape[1:])) * 4
            assert arena + off + n <= nc.sbuf_usable_end - base, (name, arena + off + n, nc.sbuf_usable_end - base)
            assert off % 32 == 0, name
            return nc.alloc_sbuf_tensor_at(name, shape, dt, offset=base + arena + off)

        def plan(start, *items):
            got, off = [], start
            for name, shape, *dt in items:
                got.append(at(name, off, shape, *dt))
                off += -(-int(np.prod(shape[1:])) * 4 // 32) * 32
            return got, off

        IDENT, ONES, MEAN, CENTRE, CAUSAL = (SQ[:, j, :] for j in range(5))
        (XK, GB0), e0 = plan(0, ("x_tok", [P, NT, D]), ("ln0_gb", [P, 2, D]))
        e0 = max(e0, 32768)
        (VR, CN), _ = plan(e0 + 21760, ("vec_rows", [P, 2, P]), ("conv_rows", [16, 2, 1408]))
        (RR, HC, RQ, RK, RV, RG, SW, TP, RQD, KDEC, VTOK, KTOK0, VBLK, INT, IN0, RS, ST, OT, OC, OSQ,
         ORS), e1 = plan(
            e0, ("ret_rope", [P, 2, COLS]), ("ret_head", [P, RH, 2 * P + T0 + 8]), ("rq", [P, COLS]),
            ("rk", [P, COLS]), ("rv", [P, COLS]), ("rg", [P, COLS]), ("rot_swap", [P, COLS]),
            ("rot_tmp", [P, COLS]), ("rq_dec", [P, 4, P]), ("k_dec", [P, NT, P]), ("v_tok", [P, NT, P]),
            ("k_tok0", [P, P]), ("v_blocks", [P, DEC, P]), ("inner", [P, 4, P]), ("inner0", [P, T0]),
            ("states", [P, NT, P]), ("state_s", [P, DEC, P]), ("o_T", [P, COLS]), ("o_cent", [P, COLS]),
            ("o_sq", [P, COLS]), ("o_rstd", [P, COLS]))
        (CTOK, QN, CNT, MR, KRT, KRO, UQ, UK, TQ, QT, KTB, VB, UKT, SG), e2 = plan(
            32768, ("c_tok", [P, NT, KVL]), ("q_lat", [P, 3, COLS]), ("c_lat", [P, 2, COLS]),
            ("mla_rope", [P, COLS]), ("k_rope_T", [P, COLS]), ("k_rope_tok", [P, NT, ROPE]),
            ("w_uq", [P, 3, 2, P]), ("w_uk", [P, 2, P]), ("rope_tmp", [P, 2, COLS]), ("q_heads", [P, 2, COLS]),
            ("k_heads", [P, 2, COLS]), ("v_pair", [P, NT, P]), ("w_uk_T", [P, 2, 2, P]),
            ("gate_out", [P, 2, 2, COLS]))
        (QSQ, RIN), _ = plan(e2, ("lat_sq", [P, 3, COLS]), ("lat_rms", [P, COLS]))
        (EX, SD, PTS), e3 = plan(e2, ("probs", [P, 2, 528]), ("diag", [P, 2, P]), ("probs_T", [P, 2, NT, P]))
        (PGC,), _ = plan(0, ("pages_c", [P, 2, NPAGES, KVL]))
        (CTX, QAB, UV), _ = plan(e3, ("c_tok0", [T0, KVL]), ("q_abs", [P, 2, DEC, HEADS]), ("w_uv", [P, 2, 512]))
        assert PGC.shape[2] * KVL * 4 == 32768
        (PGR, RTT, SCB, PB, PHL, QRB, SSM, OL, SPART, OPART, QB), e4 = plan(
            65536, ("pages_r", [P, 2, NPAGES, ROPE]), ("rope_T", [P, NCH, P]),
            ("scores", [P, 2, 33, HEADS]), ("p_sample", [P, 2, 33, HEADS]), ("p_parts", [P, 32, 2 * HEADS], F32R),
            ("q_rope_blocks", [P, DEC, 4, HEADS]), ("sm", [P, 2, 40]), ("o_lat", [P, 2, HEADS, DEC]),
            ("score_parts", [P, 2, 512]), ("out_parts", [2 * HEADS, KVL]), ("q_parts", [P, 2, 224], F32R))
        CTH, CTL, PGH, PGL = (nc.alloc_sbuf_tensor_at(name, [P, 2, 4, KVL], F32R, offset=base + j * 2 * 4 * KVL * 4)
                              for j, name in enumerate(("pages_T_hi", "pages_T_lo", "pages_hi", "pages_lo")))
        assert 4 * 2 * 4 * KVL * 4 <= 2 * KT * COLS * 4
        PHI = [PGH[:, 0], PGH[:, 1], WH[:, 0, 4:8, :], WH[:, 1, 4:8, :]]
        PLO = [PGL[:, 0], PGL[:, 1], WL[:, 0, 4:8, :], WL[:, 1, 4:8, :]]
        assert e4 <= e3
        (MH, ML, AH, AL, BH, BL, GW), e5 = plan(
            0, ("m_hi", [P, KT, COLS], F32R), ("m_lo", [P, KT, COLS], F32R), ("attn_hi", [P, 4, COLS], F32R),
            ("attn_lo", [P, 4, COLS], F32R), ("ret_hi", [P, 4, COLS], F32R), ("ret_lo", [P, 4, COLS], F32R),
            ("gated", [P, 2, 2, COLS]))
        GG = nc.alloc_sbuf_tensor_at("gates", [P, 2, 2, 2, COLS], F32, offset=base)
        YK = at("y_tok", 84000, [P, NT, D])
        assert e5 <= 84000
        GB1 = at("ln1_gb", 68608, [P, 2, D])
        NH = FFN_TILES[0]
        (FH, FL, AB, ACC, GL, HF), e6 = plan(
            0, ("ffn_hi", [P, NH, COLS], F32R), ("ffn_lo", [P, NH, COLS], F32R), ("a_rows", [P, 2, 2 + META + SEQ]),
            ("conv_acc", [P, 2, COLS]), ("gelu", [P, 2, COLS]), ("h_f32", [P, 2, COLS]))
        (GB2, CST), e7 = plan(e6, ("ln2_gb", [P, 2, D]), ("conv_out", [P, 3, P]))
        assert e7 <= 84000, e7
        assert KT * COLS * 4 == 2 * 4 * COLS * 4

        PS = ctx.enter_context(nc.psum_tensor("PS", [P, 8, 512], F32))

        def pair(p, lo=0, hi=P):
            return PS[lo:hi, 2 * p:2 * p + 2, 0:HALF]

        def two(ap):
            return ap.rearrange("p (a b) -> p a b", a=2)

        x_scr = nc.dram_tensor("x_tok_scratch", (NT, P, D), F32, kind="Internal").ap()
        g_scr = nc.dram_tensor("gate_scratch", (2, KT, P, COLS), F32, kind="Internal").ap()

        s_free = [sem(f"psum_free{p}") for p in range(4)]
        s_fa = [sem(f"psum_full_for_act{p}") for p in range(4)]
        s_fd = [sem(f"psum_full_for_dve{p}") for p in range(4)]
        s_act, s_dve, s_pool = sem("act_own_order"), sem("dve_own_order"), sem("pool_own_order")
        s_win = [sem(f"weights_landed{j}") for j in range(2)]
        s_whi, s_wsplit, s_done = sem("weights_hi"), sem("weights_split"), sem("slot_done")
        s_x = [sem(f"x_landed{t}") for t in range(NT)]
        names = ("consts_landed consts2_landed vectors_T_ready stats_ready std_ready x_gained x_scaled "
                 "x_normed ln_turned x_hi_ready x_split x_tok_stored swap_ready k_feat q_feat g_ready "
                 "head_done sn_ready state_landed state_stored inner_ready tok_ready ot_ready sq_ready "
                 "sd_ready final_state_stored lat_sq lat_sd lat_normed tok_out_ready out_stored "
                 "head_w_landed proj_done q_heads_ready uk_T_ready scores_full nmax_ready exp_ready "
                 "probs_ready probs_turned pt_act pt_dve attn_done gate_full gate_stored0 gate_stored1 "
                 "kr_landed idx_in gate_free0 gate_free1 idx_ready rope_pages0 rope_pages1 rope_turned "
                 "rope_back chunk_turned ct_act ct_dve chunk_scored q_parts parts_back page_hi page_split "
                 "p_hi p_split o_parts lat_turned s_full s_bank_free mx_ready mx_turned dg_ready "
                 "mx_spread shifted exp_s sum_ready sum_spread rs_ready pv_chunk pv_full olat_ready "
                 "a_s_full a_done ab_hi ab_split gates_back0 gates_back1 m_added m_hi m_split y_back "
                 "back_taken gb_landed gain0_landed bias0_landed conv_first conv_acc gelu_done h_ready "
                 "h_hi cst_ready go_on rows_zeroed qrb_ready").split()
        for n in names:
            sem(n)
        s_pg = [[sem(f"pages_landed{j}_{c}") for c in range(NCH)] for j in range(2)]
        S = sems

        w_in = ins["w_in"][0].rearrange("(k p) n -> p k n", p=P)
        w_ffi = ins["w_ffn_in"][0].rearrange("(k p) n -> p k n", p=P)
        w_ffo = ins["w_ffn_out"][0].rearrange("(k p) n -> p k n", p=P)
        w_ao = ins["w_attn_out"][0].rearrange("(k p) n -> p k n", p=P)
        w_ro = ins["w_ret_out"][0].rearrange("(k p) n -> p k n", p=P)
        w_o = ins["w_o"][0].rearrange("(k p) n -> p k n", p=P)
        w_uq = ins["w_uq"][0].rearrange("(k p) h n -> p k h n", p=P)
        w_uk = ins["w_uk"][0].rearrange("(k p) h n -> p k (h n)", p=P)
        w_uv = ins["w_uv"][0].rearrange("(k p) h n -> p k (h n)", p=P)

        N_RET = 0
        N_LAT = N_RET + 2 * RH
        N_GATE = N_LAT + 3
        N_MERGE = N_GATE + 8
        N_O = N_MERGE + 8
        N_F1 = N_O + 4
        N_F1O = N_F1 + FFN_TILES[0]
        N_F2 = N_F1O + 8
        N_F2O = N_F2 + FFN_TILES[1]
        N_END = N_F2O + 8

        def evac_cols(t):
            c0, r = tile_cols(t)
            return slice(c0, c0 + r), r

        def css(f):
            return CSS[:, :, bass.ds(f, 1), :].rearrange("p k f r -> p k (f r)")

        block = ctx.enter_context(nc.Block())

        @block.sync
        def _(sp):
            raw_free = Count(S["weights_split"])
            state_stored, sn, inner = Count(S["state_stored"], 16), Count(S["sn_ready"]), Count(S["inner_ready"])
            final_stored = Count(S["final_state_stored"], 16)
            out_stored = Count(S["out_stored"], 16)

            def slot(par, parts, first=False):
                if not first:
                    sp.wait_ge(raw_free.sem, raw_free.after())
                for dst, src in parts:
                    sp.dma_start(dst, src).then_inc(s_win[par], 16)

            def cols_slot(n, w, c0, c1, nk=8, k0=0, first=False):
                par = n % 2
                slot(par, [(RAW[:, par, 0:nk, 0:P], w[:, k0:k0 + nk, bass.ds(c0, P)]),
                           (RAW[:, par, 0:nk, P:2 * P], w[:, k0:k0 + nk, bass.ds(c1, P)])], first)

            sp.dma_start(XK[0:DEC, 0, :], ins["x_sample"][:, 0, :]).then_inc(s_x[0], 16)
            sp.dma_start(XK[DEC:T0, 0, :], ins["meta_tokens"]).then_inc(s_x[0], 16)
            sp.dma_start(GB0[:, 0, :], ins["ln0_g"].partition_broadcast(P)).then_inc(S["gain0_landed"], 16)
            for t in range(1, NT):
                sp.dma_start(XK[:, t, :], ins["x_prompt"][0, P * (t - 1):P * t, :]).then_inc(s_x[t], 16)
                if t == 1:
                    sp.dma_start(GB0[:, 1, :], ins["ln0_b"].partition_broadcast(P)).then_inc(S["bias0_landed"], 16)
            sp.dma_start(SQ[:], consts["square"].ap()).then_inc(S["consts_landed"], 16)
            row = 0
            for name, k in (("q_norm_g", 3), ("kv_norm_g", 2), ("ret_gn_g", 4)):
                sp.dma_start(VR[row:row + k, 0, :], ins[name][0].rearrange("(k p) -> k p", p=P)
                             ).then_inc(S["consts_landed"], 16)
                row += k
            for j in range(3):
                sp.dma_start(VR[j * FT:(j + 1) * FT, 1, :],
                             ins["conv_w"][0, j].rearrange("(k p) -> k p", p=P)).then_inc(S["consts_landed"], 16)
            sp.dma_start(VR[3 * FT:4 * FT, 1, :],
                         ins["conv_b"][0].rearrange("(k p) -> k p", p=P)).then_inc(S["consts_landed"], 16)
            cols_slot(0, w_in, OFF_RK, OFF_RV, first=True)
            cols_slot(1, w_in, OFF_RQ, OFF_RG, first=True)
            c2 = S["consts2_landed"]
            sp.dma_start(RR[:], consts["ret_rope"].ap()).then_inc(c2, 16)
            sp.dma_start(HC[:], consts["ret_head"].ap()).then_inc(c2, 16)
            sp.dma_start(SMALL[:], consts["small"].ap()).then_inc(c2, 16)
            sp.dma_start(CN[:].rearrange("p a b -> p (a b)"),
                         ins["state_ffn_conv"][0].rearrange("b j f -> (b j) f")).then_inc(c2, 16)
            for q in range(4):
                sp.dma_start(PTI[q:P:4, :], ins["page_table"].rearrange("b j -> j b"),
                             allow_slow_non_contiguous=True).then_inc(c2, 16)
            st_dram = ins["state_retention"][0].rearrange("b h k v -> k b h v")
            sto_dram = outs[8][0].rearrange("b h k v -> k b h v")

            def state_load(h):
                sp.dma_start(ST[:], st_dram[:, :, bass.ds(h, 1), :].rearrange("k b h v -> k b (h v)")
                             ).then_inc(S["state_landed"], 16)

            def state_store(h):
                sp.wait_ge(inner.sem, inner.after())
                sp.dma_start(outs[4][0, 0, bass.ds(h, 1)].rearrange("h k v -> k (h v)"), RS[:, NT - 1, :]
                             ).then_inc(S["final_state_stored"], 16)
                sp.wait_ge(sn.sem, sn.after())
                sp.dma_start(sto_dram[:, :, bass.ds(h, 1), :].rearrange("k b h v -> k b (h v)"), ST[:]
                             ).then_inc(S["state_stored"], 16)
                sp.wait_ge(state_stored.sem, state_stored.after())

            normed = Count(S["x_normed"])
            for t in range(NT):
                r = tile_cols(t)[1]
                sp.wait_ge(normed.sem, normed.after())
                sp.dma_start(x_scr[t, 0:r, :], XK[0:r, t, :]).then_inc(S["x_tok_stored"], 16)
            state_load(0)
            ot = Count(S["ot_ready"])
            with loop(sp, RH - 1, {raw_free: 2, ot: 1, inner: 1, sn: 1, state_stored: 1}) as i:
                cols_slot(0, w_in, i * P + (OFF_RK + P), i * P + (OFF_RV + P))
                cols_slot(1, w_in, i * P + (OFF_RQ + P), i * P + (OFF_RG + P))
                state_store(i)
                sp.wait_ge(ot.sem, ot.after())
                state_load(i + 1)
            cols_slot(N_LAT, w_in, OFF_Q, OFF_Q + P)
            par = (N_LAT + 1) % 2
            slot(par, [(RAW[:, par, :, 0:P], w_in[:, :, OFF_Q + 2 * P:OFF_Q + 3 * P]),
                       (RAW[:, par, :, P:P + 96], w_in[:, :, OFF_KR - 64:OFF_KR + ROPE])])
            sp.dma_start(RAW[:, par, :, P + 96:P + 112], w_in[:, :, OFF_KR + 16:OFF_KR + 32]).then_inc(S["kr_landed"], 16)
            sp.dma_start(RAW[:, par, :, P + 112:P + 128], w_in[:, :, OFF_KR:OFF_KR + 16]).then_inc(S["kr_landed"], 16)
            state_store(RH - 1)
            sp.wait_ge(final_stored.sem, final_stored.after(RH))
            cols_slot(N_LAT + 2, w_in, OFF_C, OFF_C + P)
            head_done = Count(S["head_done"])
            sp.wait_ge(head_done.sem, head_done.after(RH))
            sp.dma_start(MR[64:P, :], consts["mla_rope"].ap()).then_inc(S["idx_in"], 16)
            sp.dma_start(UV[:], w_uv).then_inc(S["idx_in"], 16)

            def head_weights(p):
                hw = S["head_w_landed"]
                for hh in range(2):
                    src = w_uq[:, :, bass.ds(p * 2 + hh, 1), :].rearrange("p k h n -> p k (h n)")
                    sp.dma_start(UQ[:, :, hh, 0:QD_], src[:, :, 0:QD_]).then_inc(hw, 16)
                    sp.dma_start(UQ[:, :, hh, QD_:QD_ + 16], src[:, :, QD_ - 16:QD_]).then_inc(hw, 16)
                    sp.dma_start(UQ[:, :, hh, QD_ + 16:P], src[:, :, NOPE:NOPE + 16]).then_inc(hw, 16)
                sp.dma_start(UK[:], w_uk[:, :, bass.ds(p * P, P)]).then_inc(hw, 16)

            head_weights(0)
            tok_out = Count(S["tok_out_ready"])

            def store(dst, src):
                sp.dma_start(dst, src).then_inc(S["out_stored"], 16)

            proj_done = Count(S["proj_done"])
            cols_slot(N_GATE, w_in, OFF_GA, OFF_GA + P)
            cols_slot(N_GATE + 1, w_in, OFF_GB, OFF_GB + P)
            sp.wait_ge(tok_out.sem, tok_out.after())
            store(outs[2][0, 0, 0:META, :], CTX[DEC:T0, :])
            store(outs[2][0, 0, META:, :].rearrange("(t p) c -> p t c", p=P), CTOK[:, 1:NT, :])
            store(outs[6][0, :, 0, :], CTX[0:DEC, :])
            store(outs[3][0, 0, 0:META, :], KRO[DEC:T0, 0, :])
            store(outs[3][0, 0, META:, :].rearrange("(t p) c -> p t c", p=P), KRO[:, 1:NT, :])
            store(outs[7][0, :, 0, :], KRO[0:DEC, 0, :])
            store(outs[9][0, :, 0, :], ins["state_ffn_conv"][0, :, 1, :])
            with loop(sp, 3, {raw_free: 2, proj_done: 1}) as i:
                sp.wait_ge(proj_done.sem, proj_done.after())
                head_weights(i + 1)
                cols_slot(N_GATE, w_in, i * 2 * P + (OFF_GA + 2 * P), i * 2 * P + (OFF_GA + 3 * P))
                cols_slot(N_GATE + 1, w_in, i * 2 * P + (OFF_GB + 2 * P), i * 2 * P + (OFF_GB + 3 * P))
            sp.wait_ge(out_stored.sem, out_stored.after(7))
            cols_slot(N_MERGE, w_ao, 0, P, 4)
            cols_slot(N_MERGE + 1, w_ro, 0, P, 4)
            a_done = Count(S["a_done"])
            sp.wait_ge(a_done.sem, a_done.after())
            m_split = Count(S["m_split"])

            def gates_back(jj):
                for s in range(2):
                    sp.dma_start(GG[:, jj % 2, s, :, :], g_scr[s, jj * 2:jj * 2 + 2].rearrange("m p c -> p m c")
                                 ).then_inc(S[f"gates_back{jj % 2}"], 16)

            for j in range(2):
                sp.wait_ge(S[f"gate_stored{j}"], 16 * (1 + 4))
            x_stored = Count(S["x_tok_stored"], 16)
            sp.wait_ge(x_stored.sem, x_stored.after(NT))
            gates_back(0)
            gates_back(1)
            sp.dma_start(YK[:, 1:NT, :], x_scr[1:NT].rearrange("t p d -> p t d")).then_inc(S["y_back"], 16)
            sp.dma_start(YK[0:T0, 0, :], x_scr[0, 0:T0, :]).then_inc(S["y_back"], 16)
            for i in range(3):
                cols_slot(N_MERGE, w_ao, i * 2 * P + 2 * P, i * 2 * P + 3 * P, 4)
                cols_slot(N_MERGE + 1, w_ro, i * 2 * P + 2 * P, i * 2 * P + 3 * P, 4)
                sp.wait_ge(m_split.sem, m_split.after())
                if i < 2:
                    gates_back(i + 2)
            with loop(sp, 2, {raw_free: 2}) as i:
                cols_slot(N_O, w_o, i * 4 * P, i * 4 * P + P)
                cols_slot(N_O + 1, w_o, i * 4 * P + 2 * P, i * 4 * P + 3 * P)
            sp.wait_ge(m_split.sem, m_split.after())
            for j, name in enumerate(("ln1_g", "ln1_b")):
                sp.dma_start(GB1[:, j, :], ins[name][0].partition_broadcast(P)).then_inc(S["gb_landed"], 16)
            f0 = 0
            for part, nf in enumerate(FFN_TILES):
                na = (N_F1, N_F2)[part]
                with loop(sp, nf // 2, {raw_free: 2}) as i:
                    cols_slot(na, w_ffi, i * 2 * P + f0 * P, i * 2 * P + (f0 + 1) * P)
                    cols_slot(na + 1, w_ffi, i * 2 * P + (DFF + f0 * P), i * 2 * P + (DFF + (f0 + 1) * P))
                no = (N_F1O, N_F2O)[part]
                hk = nf // 2
                with loop(sp, 4, {raw_free: 2}) as i:
                    cols_slot(no, w_ffo, i * 2 * P, i * 2 * P + P, hk, f0)
                    cols_slot(no + 1, w_ffo, i * 2 * P, i * 2 * P + P, hk, f0 + hk)
                if part == 0:
                    sp.wait_ge(S["x_normed"], 2 * NT)
                    for j, name in enumerate(("ln2_g", "ln2_b")):
                        sp.dma_start(GB2[:, j, :], ins[name][0].partition_broadcast(P)).then_inc(S["gb_landed"], 16)
                f0 += nf
            cst = Count(S["cst_ready"])
            sp.wait_ge(cst.sem, cst.after(3))
            for j in range(2):
                store(outs[5][0, 0, j].rearrange("(f p) -> f p", p=P), CST[j:2 * FT:2, 0, :])
            for b in range(DEC):
                k, r = divmod(b, 4)
                store(outs[9][0, b, 1].rearrange("(f p) -> f p", p=P), CST[r:4 * FT:4, 1 + k, :])
            y_out = Count(S["x_normed"], start=2 * NT)
            sp.wait_ge(y_out.sem, y_out.after())
            store(outs[1][:, 0, :], YK[0:DEC, 0, :])
            for t in range(1, NT):
                sp.wait_ge(y_out.sem, y_out.after())
                store(outs[0][0, P * (t - 1):P * t, :], YK[:, t, :])
            sp.wait_ge(out_stored.sem, out_stored.after(2 + DEC + NT))
            assert out_stored.n == 7 + 2 + DEC + NT

        @block.gpsimd
        def _(pool):
            chain = Count(S["pool_own_order"])
            turned = Count(S["ln_turned"])
            scaled, gb = Count(S["x_scaled"]), Count(S["gb_landed"], 16)

            def norm_end(x, t, bias):
                r = tile_cols(t)[1]
                pool.wait_ge(scaled.sem, scaled.after())
                nc.gpsimd.tensor_tensor(x[0:r, t, :], x[0:r, t, :], bias[0:r, 1, :], ALU.add
                                        ).then_inc(S["x_normed"], 1)

            pool.wait_ge(S["bias0_landed"], 16)
            for t in range(NT):
                norm_end(XK, t, GB0)
            stored = Count(S["x_tok_stored"], 16)
            pool.wait_ge(stored.sem, stored.after(NT))
            pool.wait_ge(turned.sem, turned.after(NT))
            lat_rows = ins["cache_kv_latent"][0].rearrange("n (q r) c -> (n q) (r c)", q=32)
            rope_rows = ins["cache_k_rope"][0].rearrange("n (q r) c -> (n q) (r c)", q=4)

            def rows_of(par, b):
                nc.gpsimd.tensor_copy(
                    IDB[:, par, :], IDX[:, bass.ds(b, 1), :].rearrange("p b c -> p (b c)")).then_inc(chain.sem, 1)
                pool.wait_ge(chain.sem, chain.after())

            def chunk(par, c):
                nc.gpsimd.indirect_dma_start(
                    out=PGC[:, par, 4 * c:4 * c + 4, :].rearrange("p r c -> p (r c)"), out_offset=None,
                    in_=lat_rows, in_offset=bass.IndirectOffsetOnAxis(ap=IDB[:, par, c:c + 1], axis=0)
                ).then_inc(s_pg[par][c], 16)

            def rope_page(par):
                nc.gpsimd.indirect_dma_start(
                    out=PGR[:, par, :, :].rearrange("p r c -> p (r c)"), out_offset=None, in_=rope_rows,
                    in_offset=bass.IndirectOffsetOnAxis(ap=IDB[:, par, NCH:NCH + 1], axis=0)
                ).then_inc(S[f"rope_pages{par}"], 16)

            idx = Count(S["idx_ready"])
            pool.wait_ge(idx.sem, idx.after())
            rows_of(0, 0)
            for c in range(NCH):
                chunk(0, c)
            attn_done = Count(S["attn_done"])
            pool.wait_ge(attn_done.sem, attn_done.after(4))
            for j in range(2):
                pool.wait_ge(S[f"gate_stored{j}"], 16 * (1 + 4))
            rope_page(0)
            rows_of(1, 1)
            rope_page(1)
            for c in range(NCH):
                chunk(1, c)
            s_full, page_split = Count(S["s_full"]), Count(S["page_split"])
            with loop(pool, 3, {chain: 2, s_full: 2, page_split: 2 * NCH}) as i:
                for par in range(2):
                    pool.wait_ge(s_full.sem, s_full.after())
                    rows_of(par, i * 2 + (2 + par))
                    pool.sem_inc(S["go_on"])
                    rope_page(par)
                    for c in range(NCH):
                        pool.wait_ge(page_split.sem, page_split.after())
                        pool.sem_inc(S["go_on"])
                        chunk(par, c)

            pool.wait_ge(gb.sem, gb.after(2))
            for t in range(NT):
                norm_end(YK, t, GB1)
            pool.wait_ge(gb.sem, gb.after(2))
            for t in range(NT):
                norm_end(YK, t, GB2)

        @block.scalar
        def _(act):
            chain = Count(S["act_own_order"])
            landed = [Count(s_win[j], 16) for j in range(2)]
            reuse = Count(s_done)
            done = Count(s_done)
            fa = [Count(s_fa[p]) for p in range(4)]

            def hi(n, nk=8, first=False):
                par = n % 2
                act.wait_ge(landed[par].sem, landed[par].after(2))
                if not first:
                    act.wait_ge(reuse.sem, reuse.after())
                nc.scalar.activation(WH[:, par, 0:nk], RAW[:, par, 0:nk], ACT.Copy).then_inc(s_whi, 1)

            stats, turned = Count(S["stats_ready"]), Count(S["ln_turned"])

            gained = Count(S["x_gained"])

            def scale_rows(x, t):
                r = tile_cols(t)[1]
                act.wait_ge(stats.sem, stats.after())
                nc.scalar.activation(SDV[0:r, t:t + 1], MV[0:r, t, 1:2], ACT.Sqrt, bias=EPS[0:r, 0:1]
                                     ).then_inc(S["std_ready"], 1)
                act.wait_ge(gained.sem, gained.after())
                nc.scalar.activation(x[0:r, t, :], x[0:r, t, :], ACT.Identity, scale=RSV[0:r, t:t + 1]
                                     ).then_inc(S["x_scaled"], 1)

            def turned_hi(t):
                act.wait_ge(turned.sem, turned.after())
                cols, r = evac_cols(t)
                bank = 4 + 2 * (t % 2)
                nc.scalar.activation(XH[:, :, cols], PS[:, bank:bank + 2, :].rearrange(
                    "p a (k c) -> p (a k) c", c=P)[:, :, 0:r], ACT.Copy).then_inc(S["x_hi_ready"], 1)

            def norm_to_features(x, early_hi=None):
                for t in range(NT):
                    scale_rows(x, t)
                    if t >= 2:
                        turned_hi(t - 2)
                    if t == 3 and early_hi:
                        hi(0, first=True)
                turned_hi(NT - 2)
                if early_hi:
                    hi(1, first=True)
                turned_hi(NT - 1)

            norm_to_features(XK, True)

            k_feat, q_feat, head_done = Count(S["k_feat"]), Count(S["q_feat"]), Count(S["head_done"])

            def swap(scale):
                for lo in (0, 64):
                    ins_ = nc.scalar.activation(two(SW[lo:lo + 64, :]), pair(0, 64 - lo, 128 - lo), ACT.Copy,
                                                scale=scale)
                ins_.then_inc(S["swap_ready"], 1)

            def centred():
                act.wait_ge(fa[2].sem, fa[2].after())
                nc.scalar.activation(two(OC[:]), pair(2), ACT.Copy)
                nc.scalar.activation(two(OSQ[:]), pair(2), ACT.Square).then_inc(S["sq_ready"], 1)

            def deviation():
                act.wait_ge(fa[3].sem, fa[3].after())
                nc.scalar.activation(two(ORS[:]), pair(3), ACT.Sqrt, bias=EPS[:, 0:1]).then_inc(S["sd_ready"], 1)

            def ret_head(prev, n_next):
                if prev:
                    hi(1)
                act.wait_ge(fa[0].sem, fa[0].after())
                if prev:
                    act.wait_ge(q_feat.sem, q_feat.after())
                swap(RD ** -0.5)
                act.wait_ge(done.sem, done.after())
                nc.scalar.activation(two(RV[:]), pair(1), ACT.Copy).then_inc(s_free[1], 1)
                if prev:
                    centred()
                    deviation()
                act.wait_ge(fa[0].sem, fa[0].after())
                act.wait_ge(k_feat.sem, k_feat.after())
                swap(1.0)
                hi(n_next)
                act.wait_ge(done.sem, done.after())
                if prev:
                    act.wait_ge(head_done.sem, head_done.after())
                nc.scalar.activation(two(RG[:]), pair(1), ACT.Silu).then_inc(S["g_ready"], 1)

            ret_head(False, 2)
            with loop(act, RH - 1, {landed[0]: 2, landed[1]: 2, reuse: 2, done: 2, fa[0]: 2, fa[2]: 1, fa[3]: 1,
                                    q_feat: 1, k_feat: 1, head_done: 1}):
                ret_head(True, 2)
            centred()
            deviation()

            kr = Count(S["kr_landed"], 16)
            act.wait_ge(kr.sem, kr.after(2))
            hi(N_LAT + 1)
            act.wait_ge(head_done.sem, head_done.after())
            act.wait_ge(S["x_tok_stored"], 16 * NT)
            act.wait_ge(S["state_stored"], 16 * RH)
            act.wait_ge(S["final_state_stored"], 16 * RH)
            act.wait_ge(fa[0].sem, fa[0].after())
            nc.scalar.activation(two(QN[:, 0, :]), pair(0), ACT.Copy).then_inc(s_free[0], 1)
            act.wait_ge(done.sem, done.after())
            nc.scalar.activation(two(QN[:, 1, :]), pair(1), ACT.Copy).then_inc(s_free[1], 1)
            act.wait_ge(fa[0].sem, fa[0].after())
            nc.scalar.activation(two(QN[:, 2, :]), pair(0), ACT.Copy).then_inc(chain.sem, 1)
            chain.add()
            act.wait_ge(chain.sem, chain.after(0))
            nc.scalar.activation(QSQ[:], QN[:], ACT.Square).then_inc(S["lat_sq"], 1)
            hi(N_LAT + 2)
            act.wait_ge(fa[2].sem, fa[2].after())
            nc.scalar.activation(two(RIN[:]), pair(2), ACT.Sqrt, bias=EPS[:, 1:2], scale=1.0 / QL
                                 ).then_inc(S["lat_sd"], 1)
            act.wait_ge(done.sem, done.after())
            act.wait_ge(fa[0].sem, fa[0].after())
            nc.scalar.activation(two(CNT[:, 0, :]), pair(0), ACT.Copy).then_inc(s_free[0], 1)
            act.wait_ge(done.sem, done.after())
            nc.scalar.activation(two(CNT[:, 1, :]), pair(1), ACT.Copy).then_inc(chain.sem, 1)
            act.wait_ge(chain.sem, chain.after())
            nc.scalar.activation(QSQ[:, 0:2, :], CNT[:], ACT.Square).then_inc(S["lat_sq"], 1)
            hi(N_GATE)
            act.wait_ge(fa[3].sem, fa[3].after())
            nc.scalar.activation(two(QSQ[:, 2, :]), pair(3), ACT.Sqrt, bias=EPS[:, 1:2], scale=1.0 / KVL
                                 ).then_inc(S["lat_sd"], 1)

            gate_full = Count(S["gate_full"])
            stored = [Count(S[f"gate_stored{j}"], 16) for j in range(2)]
            nmax, probs_turned = Count(S["nmax_ready"]), Count(S["probs_turned"])
            act.sem_inc(S["gate_stored0"], 16)
            act.sem_inc(S["gate_stored1"], 16)

            def gate(g, p):
                s, m, half = g // 4, (g // 2) % 2, g % 2
                if g % 4 == 3:
                    act.wait_ge(done.sem, done.after())
                else:
                    act.wait_ge(gate_full.sem, gate_full.after())
                if g % 4 == 0:
                    act.wait_ge(stored[s].sem, stored[s].after())
                ins_ = nc.scalar.activation(SG[:, s, m, half * HALF:(half + 1) * HALF], PS[:, half, 0:HALF],
                                            ACT.Tanh, scale=0.5)
                ins_.then_inc(S[f"gate_free{half}"], 1)
                if g % 4 == 3:
                    act.wait_ge(turn_free.sem, turn_free.after(2))
                    act.dma_start(g_scr[s, bass.ds(p * 2, 2)].rearrange("m p c -> p m c"), SG[:, s]
                                  ).then_inc(S[f"gate_stored{s}"], 16)

            def exps(s):
                t, hh = divmod(s, 2)
                act.wait_ge(nmax.sem, nmax.after())
                r = tile_cols(t)[1]
                n = META + P * (t - 1)
                at_ = 16 * hh
                bias = SMX[0:r, at_ + 3:at_ + 4]
                if t:
                    nc.scalar.activation(EX[:, hh, 0:n], PS[:, 4 + hh, 0:n], ACT.Exp, bias=bias, scale=SCALE,
                                         accum_out=SMX[:, at_ + 4:at_ + 5])
                    ins_ = nc.scalar.activation(EX[:, hh, n:n + P], SD[:, hh, :], ACT.Exp, bias=bias,
                                                scale=SCALE, accum_out=SMX[:, at_ + 5:at_ + 6])
                else:
                    ins_ = nc.scalar.activation(EX[0:r, hh, 0:META], SD[0:r, hh, 0:META], ACT.Exp, bias=bias,
                                                scale=SCALE, accum_out=SMX[0:r, at_ + 4:at_ + 5])
                ins_.then_inc(S["exp_ready"], 1)

            def probs_back(t):
                act.wait_ge(probs_turned.sem, probs_turned.after())
                r = tile_cols(t)[1]
                if t:
                    k = min(t, 3)
                    nc.scalar.activation(PTS[:, 0, 1:k + 1, :], PS[:, 4, P:(k + 1) * P].rearrange(
                        "p (k c) -> p k c", k=k), ACT.Copy)
                if t == NT - 1:
                    nc.scalar.activation(PTS[:, 0, NT - 1, :], PS[:, 6, 0:P], ACT.Copy)
                nc.scalar.activation(PTS[0:META, 0, 0, 0:r], PS[0:META, 4, 0:r], ACT.Copy).then_inc(S["pt_act"], 1)

            turn_free = Count(S["gate_free1"], start=1)

            def gate_pair(p):
                hi(N_GATE + 1)
                for g in range(3):
                    gate(g, p)
                exps(0)
                exps(1)
                for s in range(2 * NT):
                    if s % 2 == 0:
                        probs_back(s // 2)
                    else:
                        probs_turned.add()
                    if s + 2 < 2 * NT:
                        exps(s + 2)
                    if s % 2:
                        gate(3 + s // 2, p)
                    if s == 2:
                        hi(N_GATE)

            with loop(act, 4, {landed[0]: 2, landed[1]: 2, reuse: 2, done: 2, gate_full: 6, stored[0]: 1,
                               stored[1]: 1, nmax: 2 * NT, probs_turned: 2 * NT, turn_free: 4}) as p:
                gate_pair(p)

            for j in range(2):
                act.wait_ge(stored[j].sem, stored[j].after(1))
            hi(N_MERGE + 1, 4)
            ct, scored, shifted = Count(S["chunk_turned"]), Count(S["chunk_scored"]), Count(S["shifted"])
            rope_t, exp_s, pv = Count(S["rope_turned"]), Count(S["exp_s"]), Count(S["pv_chunk"])

            def chunk_hi(c):
                act.wait_ge(ct.sem, ct.after())
                if c >= 2:
                    act.wait_ge(scored.sem, scored.after())
                j = c % 2
                nc.scalar.activation(CTH[:, j].rearrange("p a b -> p (a b)"),
                                     PS[:, 2 * j:2 * j + 2, :].rearrange("p a b -> p (a b)"), ACT.Copy
                                     ).then_inc(S["ct_act"], 1)

            def exp_sample(par):
                act.wait_ge(shifted.sem, shifted.after())
                nc.scalar.activation(PB[:, par], SCB[:, par], ACT.Exp, scale=SCALE).then_inc(S["exp_s"], 1)

            def probs_hi(par):
                act.wait_ge(exp_s.sem, exp_s.after())
                nc.scalar.activation(PHL[:, :, 0:HEADS], PB[:, par, 0:NPAGES], ACT.Copy).then_inc(S["p_hi"], 1)

            def page_hi(par, c):
                if c >= 4:
                    act.wait_ge(pv.sem, pv.after())
                nc.scalar.activation(PHI[c % 4], PGC[:, par, 4 * c:4 * c + 4, :], ACT.Copy
                                     ).then_inc(S["page_hi"], 1)

            def parts_back(a):
                nc.scalar.activation(SPART[:, a, :], PS[:, 4 + a, :], ACT.Copy).then_inc(S["parts_back"], 1)

            def rope_back():
                act.wait_ge(rope_t.sem, rope_t.after())
                nc.scalar.activation(RTT[:].rearrange("p c s -> p (c s)"),
                                     PS[:, 2:4, :].rearrange("p a b -> p (a b)"), ACT.Copy
                                     ).then_inc(S["rope_back"], 1)

            def sample_act(prev, more=True):
                for c in range(2, NCH):
                    chunk_hi(c)
                    if prev is not None:
                        if c % 2 == 0:
                            page_hi(prev, c // 2 - 1)
                        if c == 6:
                            exp_sample(prev)
                    if c == 5:
                        parts_back(0)
                if prev is not None:
                    probs_hi(prev)
                act.wait_ge(scored.sem, scored.after(2))
                parts_back(1)
                if more:
                    chunk_hi(0)
                    rope_back()
                if prev is not None:
                    for c in range(3, NCH):
                        if c == 7 and more:
                            chunk_hi(1)
                        page_hi(prev, c)
                    act.wait_ge(pv.sem, pv.after(4))
                else:
                    chunk_hi(1)

            chunk_hi(0)
            rope_back()
            chunk_hi(1)
            sample_act(None)
            with loop(act, 3, {ct: 2 * NCH, scored: 2 * NCH, shifted: 2, rope_t: 2, exp_s: 2, pv: 2 * NCH}):
                for par in range(2):
                    sample_act(par)
            sample_act(0, False)
            exp_sample(1)
            probs_hi(1)
            for c in range(NCH):
                page_hi(1, c)

            a_done = Count(S["a_done"])
            act.wait_ge(a_done.sem, a_done.after())
            nc.scalar.activation(AH[:], AT[:], ACT.Copy).then_inc(S["ab_hi"], 1)
            nc.scalar.activation(BH[:], BT[:], ACT.Copy).then_inc(S["ab_hi"], 1)
            m_added = Count(S["m_added"])

            def merge(jj, nk_next0, nk_next1):
                act.wait_ge(done.sem, done.after())
                hi(N_MERGE + 2, nk_next0)
                act.wait_ge(done.sem, done.after())
                hi(N_MERGE + 3, nk_next1)
                act.wait_ge(m_added.sem, m_added.after())
                nc.scalar.activation(MH[:, bass.ds(jj * 2, 2), :], GW[:, 0], ACT.Copy, scale=0.5
                                     ).then_inc(S["m_hi"], 1)

            with loop(act, 3, {landed[0]: 2, landed[1]: 2, reuse: 2, done: 2, m_added: 1}) as jj:
                merge(jj, 4, 4)
            merge(3, 8, 8)

            def out_pair(jj):
                act.wait_ge(fa[0].sem, fa[0].after())
                nc.scalar.activation(two(TT[:, bass.ds(jj * 4, 1), :].rearrange("p a c -> p (a c)")), pair(0),
                                     ACT.Copy).then_inc(s_free[0], 1)
                act.wait_ge(done.sem, done.after())
                nc.scalar.activation(two(TT[:, bass.ds(jj * 4 + 1, 1), :].rearrange("p a c -> p (a c)")), pair(1),
                                     ACT.Copy).then_inc(s_free[1], 1)
                hi(N_O)
                act.wait_ge(fa[2].sem, fa[2].after())
                nc.scalar.activation(two(TT[:, bass.ds(jj * 4 + 2, 1), :].rearrange("p a c -> p (a c)")), pair(2),
                                     ACT.Copy).then_inc(s_free[2], 1)
                act.wait_ge(done.sem, done.after())
                nc.scalar.activation(two(TT[:, bass.ds(jj * 4 + 3, 1), :].rearrange("p a c -> p (a c)")), pair(3),
                                     ACT.Copy).then_inc(s_free[3], 1)
                hi(N_O + 1)

            with loop(act, 2, {landed[0]: 2, landed[1]: 2, reuse: 2, done: 2, fa[0]: 1, fa[2]: 1}) as jj:
                out_pair(jj)

            norm_to_features(YK)

            conv_acc, h_ready = Count(S["conv_acc"]), Count(S["h_ready"])
            act.wait_ge(S["rows_zeroed"], 1)

            def conv_start(m, f):
                if m:
                    act.wait_ge(done.sem, done.after())
                else:
                    act.wait_ge(fa[0].sem, fa[0].after())
                nc.scalar.activation(AB[:, m, 2:2 + HALF - DEC], PS[:, 2 * m, DEC:HALF], ACT.Copy)
                nc.scalar.activation(AB[:, m, 2 + HALF - DEC:], PS[:, 2 * m + 1, 0:HALF], ACT.Copy).then_inc(chain.sem, 1)
                chain.add()
                nc.scalar.activation(CSP[:, bass.ds(f, 1), :].rearrange("p a c -> p (a c)"),
                                     PS[:, 2 * m + 1, HALF - 2:HALF], ACT.Copy)
                nc.scalar.activation(css(f), PS[:, 2 * m, 0:DEC].rearrange("p (k r) -> p k r", k=2),
                                     ACT.Copy).then_inc(s_free[m], 1)
                act.wait_ge(chain.sem, chain.after(0))
                nc.scalar.activation(ACC[:, m, DEC:], AB[:, m, 0:META + SEQ], ACT.Identity,
                                     scale=CV[:, bass.ds(f, 1)], bias=CV[:, bass.ds(f + 3 * FT, 1)])
                nc.scalar.activation(ACC[:, m, 0:DEC], PV[:, bass.ds(f, 1), 0:2 * DEC:2].rearrange("p a c -> p (a c)"),
                                     ACT.Identity, scale=CV[:, bass.ds(f, 1)], bias=CV[:, bass.ds(f + 3 * FT, 1)]
                                     ).then_inc(S["conv_first"], 1)

            for part, nf in enumerate(FFN_TILES):
                f0 = sum(FFN_TILES[:part])

                def ffn_in_pair(i, next_a, next_b):
                    for m in range(2):
                        conv_start(m, i * 2 + (f0 + m))
                    next_a()
                    for m in range(2):
                        act.wait_ge(conv_acc.sem, conv_acc.after())
                        nc.scalar.activation(GL[:, m], ACC[:, m], ACT.Gelu_apprx_tanh).then_inc(S["gelu_done"], 1)
                    for m in range(2):
                        act.wait_ge(h_ready.sem, h_ready.after())
                        nc.scalar.activation(FH[:, bass.ds(i * 2 + m, 1), :].rearrange("p a c -> p (a c)"), HF[:, m],
                                             ACT.Copy).then_inc(S["h_hi"], 1)
                    act.wait_ge(done.sem, done.after())
                    next_b()

                na = (N_F1, N_F2)[part]
                no = (N_F1O, N_F2O)[part]
                hk = nf // 2
                with loop(act, nf // 2 - 1, {landed[0]: 2, landed[1]: 2, reuse: 2, done: 2, fa[0]: 1, chain: 2,
                                             conv_acc: 2, h_ready: 2}) as i:
                    ffn_in_pair(i, lambda: hi(na), lambda: hi(na + 1))
                ffn_in_pair(nf // 2 - 1, lambda: hi(no, hk), lambda: hi(no + 1, hk))
                last = part == 1

                def out_cols(jj, hi_a, hi_b):
                    act.wait_ge(done.sem, done.after())
                    hi_a()
                    if not last:
                        act.wait_ge(fa[0].sem, fa[0].after())
                        nc.scalar.activation(two(TT[:, bass.ds(jj * 2, 1), :].rearrange("p a c -> p (a c)")), pair(0),
                                             ACT.Copy).then_inc(s_free[0], 1)
                    act.wait_ge(done.sem, done.after())
                    if not last:
                        nc.scalar.activation(two(TT[:, bass.ds(jj * 2 + 1, 1), :].rearrange("p a c -> p (a c)")),
                                             pair(1), ACT.Copy).then_inc(s_free[1], 1)
                    hi_b()

                per = {landed[0]: 2, landed[1]: 2, reuse: 2, done: 2}
                if not last:
                    per[fa[0]] = 1
                with loop(act, 3, per) as jj:
                    out_cols(jj, lambda: hi(no, hk), lambda: hi(no + 1, hk))
                if last:
                    out_cols(3, lambda: None, lambda: None)
                else:
                    out_cols(3, lambda: hi(N_F2), lambda: hi(N_F2 + 1))

            for t in range(NT):
                scale_rows(YK, t)

        @block.vector
        def _(dve):
            chain = Count(S["dve_own_order"])
            whi = Count(s_whi)
            fd = [Count(s_fd[p]) for p in range(4)]
            done = Count(s_done)
            V = nc.vector

            def lo(n, nk=8):
                par = n % 2
                dve.wait_ge(whi.sem, whi.after())
                V.tensor_tensor(WL[:, par, 0:nk], RAW[:, par, 0:nk], WH[:, par, 0:nk].bitcast(F32), ALU.subtract
                                ).then_inc(s_wsplit, 1)

            def lo_quarter(n, q):
                par, k = n % 2, slice(2 * q, 2 * q + 2)
                if q == 0:
                    dve.wait_ge(whi.sem, whi.after())
                last = V.tensor_tensor(WL[:, par, k], RAW[:, par, k], WH[:, par, k].bitcast(F32), ALU.subtract)
                if q == 3:
                    last.then_inc(s_wsplit, 1)

            std, x_hi = Count(S["std_ready"]), Count(S["x_hi_ready"])

            def norm_begin(x, t, gain):
                r = tile_cols(t)[1]
                for j in range(2):
                    V.bn_stats(STAT[0:r, t, j, :], x[0:r, t, 512 * j:512 * j + 512]).then_inc(chain.sem, 1)
                    chain.add()
                dve.wait_ge(chain.sem, chain.after(0))
                V.bn_aggr(MV[0:r, t, :], STAT[0:r, t, :, :].rearrange("p a b -> p (a b)")).then_inc(S["stats_ready"], 1)
                dve.wait_ge(stats.sem, stats.after())
                V.scalar_tensor_tensor(x[0:r, t, :], x[0:r, t, :], MV[0:r, t, 0:1], gain[0:r, 0, :], ALU.subtract,
                                       ALU.mult).then_inc(chain.sem, 1)
                chain.add()
                dve.wait_ge(std.sem, std.after())
                V.reciprocal(RSV[0:r, t:t + 1], SDV[0:r, t:t + 1]).then_inc(S["x_gained"], 1)

            def turned_lo(t):
                c, r = evac_cols(t)
                bank = 4 + 2 * (t % 2)
                dve.wait_ge(x_hi.sem, x_hi.after())
                V.tensor_tensor(XL[:, :, c], PS[:, bank:bank + 2, :].rearrange(
                    "p a (k c) -> p (a k) c", c=P)[:, :, 0:r], XH[:, :, c].bitcast(F32), ALU.subtract
                                ).then_inc(S["x_split"], 1)

            stats, gb = Count(S["stats_ready"]), Count(S["gb_landed"], 16)
            V.memset(EPS[:, 0:1], LN_EPS)
            V.memset(EPS[:, 1:2], RMS_EPS)
            for t in range(NT):
                dve.wait_ge(s_x[t], 32 if t == 0 else 16)
                if t == 0:
                    dve.wait_ge(S["gain0_landed"], 16)
                norm_begin(XK, t, GB0)
                if t >= 3:
                    turned_lo(t - 3)
            lo(0)
            turned_lo(NT - 3)
            turned_lo(NT - 2)
            dve.wait_ge(fd[0].sem, fd[0].after())
            V.tensor_copy(CV[:], PS[:, 1, 0:4 * FT])
            V.tensor_copy(VT[:], PS[:, 0, 0:9]).then_inc(S["vectors_T_ready"], 1)
            turned_lo(NT - 1)
            lo(1)
            vt = Count(S["vectors_T_ready"])
            dve.wait_ge(vt.sem, vt.after())
            dve.wait_ge(fd[1].sem, fd[1].after())
            V.tensor_copy(PV[:].rearrange("p f c -> p (f c)"), PS[:, 2, 0:2 * DEC * FT]).then_inc(s_free[1], 1)

            swap_ready, q_feat = Count(S["swap_ready"]), Count(S["q_feat"])
            state_landed, sd_ready, g_ready = Count(S["state_landed"], 16), Count(S["sd_ready"]), Count(S["g_ready"])
            final_stored = Count(S["final_state_stored"], 16)
            c2 = Count(S["consts2_landed"], 16)
            dve.wait_ge(c2.sem, c2.after(8))

            def rotate(dst, scale, s_out):
                dve.wait_ge(swap_ready.sem, swap_ready.after())
                V.tensor_tensor(TP[:], SW[:], RR[:, 1, :], ALU.mult)
                V.scalar_tensor_tensor(two(dst), pair(0), scale, two(RR[:, 0, :]), ALU.mult, ALU.mult).then_inc(chain.sem, 1)
                dve.wait_ge(chain.sem, chain.after())
                V.tensor_tensor(dst, dst, TP[:], ALU.add).then_inc(s_out, 1)

            def head_const(h, c0, n):
                return HC[:, bass.ds(h, 1), c0:c0 + n].rearrange("p a c -> p (a c)")

            C_KD, C_KD0, C_G1, C_GP = (2 * P + T0 + j for j in range(4))

            def outputs_back(h):
                dve.wait_ge(fd[3].sem, fd[3].after())
                V.tensor_copy(OT[:, DEC:T0], PS[:, 7, DEC:T0])
                V.tensor_copy(OT[:, T0:], PS[:, 6, :])
                dve.wait_ge(fd[2].sem, fd[2].after())
                dve.wait_ge(state_landed.sem, state_landed.after())
                V.scalar_tensor_tensor(ST[:].rearrange("p (a b) v -> p a (b v)", a=2),
                                       ST[:].rearrange("p (a b) v -> p a (b v)", a=2), head_const(h, C_G1, 1),
                                       PS[:, 4:6, :], ALU.mult, ALU.add).then_inc(S["sn_ready"], 1)

            def sample_back():
                dve.wait_ge(fd[3].sem, fd[3].after())
                V.tensor_copy(OT[:, 0:DEC], PS[:, 6, 0:DEC]).then_inc(S["ot_ready"], 1)

            def readout(h):
                dve.wait_ge(sd_ready.sem, sd_ready.after())
                dve.wait_ge(g_ready.sem, g_ready.after())
                V.reciprocal(ORS[:], ORS[:]).then_inc(chain.sem, 1)
                dve.wait_ge(chain.sem, chain.after())
                V.tensor_tensor(OC[:], OC[:], ORS[:], ALU.mult).then_inc(chain.sem, 1)
                dve.wait_ge(chain.sem, chain.after())
                V.scalar_tensor_tensor(BT[:, bass.ds(h, 1), :].rearrange("p a c -> p (a c)"), OC[:],
                                       VT[:, bass.ds(h + 5, 1)], RG[:], ALU.mult, ALU.mult
                                       ).then_inc(S["head_done"], 1)

            tok = Count(S["tok_ready"])

            def ret_head(h, prev):
                if prev:
                    lo(1)
                rotate(RK[:], RD ** -0.5, S["k_feat"])
                if prev:
                    outputs_back(h - 1)
                    sample_back()
                    readout(h - 1)
                rotate(RQ[:], 1.0, S["q_feat"])
                dve.wait_ge(q_feat.sem, q_feat.after())
                V.tensor_tensor(RQD[:], RQ[:, T0:].rearrange("p (t c) -> p t c", t=4),
                                head_const(h, P, P).unsqueeze(1).to_broadcast([P, 4, P]), ALU.mult)
                dve.wait_ge(fd[2].sem, fd[2].after())
                V.tensor_scalar(KDEC[:, 1:NT, :], PS[:, 4, :].rearrange("p (t c) -> p t c", t=4),
                                head_const(h, C_KD, 1), None, ALU.mult)
                V.tensor_copy(VTOK[:, 1:NT, :], PS[:, 5, :].rearrange("p (t c) -> p t c", t=4))
                dve.wait_ge(fd[3].sem, fd[3].after())
                V.tensor_copy(KTOK0[0:T0, :], PS[0:T0, 6, 0:P])
                V.tensor_scalar(KDEC[0:T0, 0, :], PS[0:T0, 6, 0:P], head_const(h, C_KD0, 1)[0:T0], None, ALU.mult)
                V.tensor_copy(VTOK[0:T0, 0, :], PS[0:T0, 6, P:2 * P]).then_inc(S["tok_ready"], 1)
                lo(0)
                dve.wait_ge(tok.sem, tok.after())
                for b in range(DEC):
                    V.tensor_scalar(VBLK[0:DEC, b, :], VTOK[0:DEC, 0, :], IDENT[0:DEC, b:b + 1], None, ALU.mult)
                dve.wait_ge(fd[2].sem, fd[2].after())
                dve.wait_ge(fd[3].sem, fd[3].after())
                if prev:
                    dve.wait_ge(final_stored.sem, final_stored.after())
                V.tensor_tensor(INT[:], PS[:, 4, :].rearrange("p (t c) -> p t c", t=4),
                                head_const(h, 0, P).unsqueeze(1).to_broadcast([P, 4, P]), ALU.mult)
                V.tensor_tensor(IN0[0:T0, :], PS[0:T0, 6, 0:T0], head_const(h, 2 * P, T0)[0:T0], ALU.mult)
                V.tensor_copy(RS[:, 0, :], PS[:, 6, P:2 * P]).then_inc(chain.sem, 1)
                dve.wait_ge(chain.sem, chain.after())
                for t in range(1, NT):
                    ins_ = V.scalar_tensor_tensor(RS[:, t, :], RS[:, t - 1, :], head_const(h, C_GP, 1),
                                                  PS[:, 5, P * (t - 1):P * t], ALU.mult, ALU.add)
                    if t < NT - 1:
                        ins_.then_inc(chain.sem, 1)
                        dve.wait_ge(chain.sem, chain.after())
                ins_.then_inc(S["inner_ready"], 1)

            ret_head(0, False)
            with loop(dve, RH - 1, {whi: 2, chain: 8, tok: 1, swap_ready: 2, q_feat: 1, fd[2]: 3, fd[3]: 4, state_landed: 1,
                                    sd_ready: 1, g_ready: 1, final_stored: 1}) as i:
                ret_head(i + 1, True)
            outputs_back(RH - 1)
            sample_back()
            for c in range(NCH):
                V.tensor_scalar(IDX[:, :, c], PTI[:], 32.0, SMALL[:, 25:26], ALU.mult, ALU.add)
            V.tensor_scalar(IDX[:, :, NCH], PTI[:], 4.0, SMALL[:, 24:25], ALU.mult, ALU.add).then_inc(chain.sem, 1)
            dve.wait_ge(chain.sem, chain.after())
            for c in range(1, NCH):
                last = V.tensor_scalar(IDX[:, :, c], IDX[:, :, c], float(c), None, ALU.add)
            last.then_inc(S["idx_ready"], 1)
            readout(RH - 1)

            lo(N_LAT + 1)
            dve.wait_ge(done.sem, done.after(N_LAT + 2))
            mr = Count(S["idx_in"], 16)
            dve.wait_ge(mr.sem, mr.after(2))
            hd = Count(S["head_done"])
            dve.wait_ge(hd.sem, hd.after(RH))
            R0, R1 = slice(64, 96), slice(96, 128)

            def rotated(p, j):
                dve.wait_ge(chain.sem, chain.after(0))
                V.tensor_tensor(two(TQ[R0, 0, :]), pair(p, 96, 128), two(MR[R1, :]), ALU.mult)
                V.tensor_tensor(two(TQ[R0, 1, :]), pair(p, 64, 96), two(MR[R0, :]), ALU.mult).then_inc(chain.sem, 1)
                dve.wait_ge(chain.sem, chain.after())

            rotated(1, 0)
            for j in range(2):
                V.tensor_tensor(KTB[R0, j, :], TQ[R0, 0, :], TQ[R0, 1, :], ALU.add)
            V.tensor_tensor(KRT[0:32, :], TQ[R0, 0, :], TQ[R0, 1, :], ALU.add).then_inc(s_free[1], 1)
            lo(N_LAT + 2)
            lat_sd = Count(S["lat_sd"])
            dve.wait_ge(lat_sd.sem, lat_sd.after())
            V.reciprocal(RIN[:], RIN[:]).then_inc(chain.sem, 1)
            dve.wait_ge(chain.sem, chain.after())
            for j in range(3):
                last = V.scalar_tensor_tensor(QN[:, j, :], QN[:, j, :], VT[:, j:1 + j], RIN[:], ALU.mult, ALU.mult)
            last.then_inc(S["lat_normed"], 1)
            lo(N_GATE)
            dve.wait_ge(lat_sd.sem, lat_sd.after())
            V.reciprocal(QSQ[:, 2, :], QSQ[:, 2, :]).then_inc(chain.sem, 1)
            dve.wait_ge(chain.sem, chain.after())
            for j in range(2):
                last = V.scalar_tensor_tensor(CNT[:, j, :], CNT[:, j, :], VT[:, 3 + j:4 + j], QSQ[:, 2, :],
                                              ALU.mult, ALU.mult)
            V.memset(KR8[:], 0.0).then_inc(chain.sem, 1)
            dve.wait_ge(chain.sem, chain.after())
            last2 = V.tensor_copy(KR8[0:32, :], KRT[0:32, 0:DEC])
            last2.then_inc(chain.sem, 1)
            dve.wait_ge(chain.sem, chain.after())
            V.tensor_copy(CN8[:], CNT[:, :, 0:DEC]).then_inc(S["lat_normed"], 1)
            dve.wait_ge(fd[2].sem, fd[2].after())
            V.tensor_copy(CTOK[:, 1:NT, :].rearrange("p (a b) c -> p a (b c)", a=2), PS[:, 4:6, :]
                          ).then_inc(s_free[2], 1)
            dve.wait_ge(fd[3].sem, fd[3].after())
            V.tensor_copy(CTX[:], PS[0:T0, 6, 0:KVL])
            V.tensor_copy(KRO[0:T0, 0, :], PS[0:T0, 7, P:P + ROPE])
            V.tensor_copy(KRO[:, 1:NT, :], PS[:, 7, 0:P].rearrange("p (t c) -> p t c", t=4)
                          ).then_inc(S["tok_out_ready"], 1)

            proj, scores = Count(S["proj_done"]), Count(S["scores_full"])
            expd, turned = Count(S["exp_ready"]), Count(S["probs_turned"])

            def maxima(s):
                t, hh = divmod(s, 2)
                dve.wait_ge(scores.sem, scores.after())
                r = tile_cols(t)[1]
                n = META + P * (t - 1)
                at_ = 16 * hh
                top = SMX[0:r, at_:at_ + 1]
                if t:
                    V.tensor_tensor(SD[:, hh, :], PS[:, 6 + hh, 0:P], CAUSAL, ALU.add).then_inc(chain.sem, 1)
                    chain.add()
                    V.reduce_max(top, PS[:, 4 + hh, 0:n], AX).then_inc(chain.sem, 1)
                    dve.wait_ge(chain.sem, chain.after())
                    V.reduce_max(SMX[:, at_ + 1:at_ + 2], SD[:, hh, :], AX).then_inc(chain.sem, 1)
                    dve.wait_ge(chain.sem, chain.after())
                    V.tensor_scalar(SMX[:, at_ + 3:at_ + 4], top, SMX[:, at_ + 1:at_ + 2], -SCALE, ALU.max, ALU.mult
                                    ).then_inc(S["nmax_ready"], 1)
                else:
                    V.tensor_tensor(SD[0:r, hh, 0:META], PS[0:r, 6 + hh, 0:META], SMALL[0:r, 0:META], ALU.add
                                    ).then_inc(chain.sem, 1)
                    dve.wait_ge(chain.sem, chain.after())
                    V.reduce_max(top, SD[0:r, hh, 0:META], AX).then_inc(chain.sem, 1)
                    dve.wait_ge(chain.sem, chain.after())
                    V.tensor_scalar(SMX[0:r, at_ + 3:at_ + 4], top, -SCALE, None, ALU.mult).then_inc(S["nmax_ready"], 1)

            def normalise(s):
                t, hh = divmod(s, 2)
                dve.wait_ge(expd.sem, expd.after())
                r = tile_cols(t)[1]
                at_ = 16 * hh
                total = SMX[0:r, at_ + 4:at_ + 5]
                if t:
                    total = SMX[:, at_ + 6:at_ + 7]
                    V.tensor_tensor(total, SMX[:, at_ + 4:at_ + 5], SMX[:, at_ + 5:at_ + 6], ALU.add
                                    ).then_inc(chain.sem, 1)
                    dve.wait_ge(chain.sem, chain.after())
                V.reciprocal(SMX[0:r, at_ + 7:at_ + 8], total).then_inc(chain.sem, 1)
                dve.wait_ge(chain.sem, chain.after())
                w = META + P * t if t else META
                V.tensor_scalar(EX[0:r, hh, 0:w], EX[0:r, hh, 0:w], SMX[0:r, at_ + 7:at_ + 8], None, ALU.mult
                                ).then_inc(S["probs_ready"], 1)

            def probs_back(t):
                dve.wait_ge(turned.sem, turned.after())
                r = tile_cols(t)[1]
                if t:
                    k = min(t, 3)
                    V.tensor_copy(PTS[:, 1, 1:k + 1, :], PS[:, 5, P:(k + 1) * P].rearrange("p (k c) -> p k c", k=k))
                if t == NT - 1:
                    V.tensor_copy(PTS[:, 1, NT - 1, :], PS[:, 7, 0:P])
                V.tensor_copy(PTS[0:META, 1, 0, 0:r], PS[0:META, 5, 0:r]).then_inc(S["pt_dve"], 1)

            def attn_pair(p):
                lo(N_GATE + 1)
                for hh in range(2):
                    dve.wait_ge(fd[2 + hh].sem, fd[2 + hh].after())
                    rotated(2 + hh, hh)
                    V.tensor_copy(two(QT[0:64, hh, :]), pair(2 + hh, 0, 64)).then_inc(s_free[2 + hh], 1)
                    V.tensor_tensor(QT[R0, hh, :], TQ[R0, 0, :], TQ[R0, 1, :], ALU.add).then_inc(chain.sem, 1)
                    chain.add()
                dve.wait_ge(fd[1].sem, fd[1].after())
                V.tensor_copy(two(KTB[0:64, 0, :]), pair(1, 0, 64))
                V.tensor_copy(two(KTB[0:64, 1, :]), pair(1, 64, 128))
                dve.wait_ge(chain.sem, chain.after(0))
                V.tensor_copy(QS[R0, bass.ds(p * 2, 2), :], QT[R0, :, 0:DEC]).then_inc(S["q_heads_ready"], 1)
                dve.wait_ge(fd[2].sem, fd[2].after())
                V.tensor_copy(VB[0:META, 0, :], PS[0:META, 5, 0:P])
                V.tensor_copy(VB[:, 1:NT, :], PS[:, 4, :].rearrange("p (t c) -> p t c", t=4)).then_inc(s_free[2], 1)
                dve.wait_ge(proj.sem, proj.after())
                V.tensor_copy(UKT[0:64].rearrange("p a b c -> p (a b c)"), PS[0:64, 6, :]).then_inc(S["uk_T_ready"], 1)
                dve.wait_ge(fd[3].sem, fd[3].after())
                for ct in range(2):
                    last = V.tensor_copy(QAB[:, ct, :, bass.ds(p * 2, 2)].rearrange("p b h -> p h b"),
                                         PS[:, 6, 16 * ct:16 * ct + 16].rearrange("p (h b) -> p h b", h=2))
                last.then_inc(s_free[3], 1)
                maxima(0)
                maxima(1)
                normalise(0)
                for s in range(2 * NT):
                    if s % 2:
                        probs_back(s // 2)
                    else:
                        turned.add()
                    if s + 1 < 2 * NT:
                        normalise(s + 1)
                    if s + 2 < 2 * NT:
                        maxima(s + 2)
                    if s in (4, 5, 6, 7):
                        lo_quarter(N_GATE, s - 4)
                dve.wait_ge(fd[1].sem, fd[1].after())
                at_p = AT[:, bass.ds(p, 1), :].rearrange("p a c -> p (a c)")
                V.tensor_copy(at_p[:, DEC:T0], PS[:, 3, DEC:T0])
                V.tensor_copy(at_p[:, T0:], PS[:, 2, :]).then_inc(S["attn_done"], 1)

            with loop(dve, 4, {whi: 2, chain: 4 + 2 * (3 + 4 * 5), fd[1]: 2, fd[2]: 2, fd[3]: 2, proj: 1,
                               scores: 2 * NT, expd: 2 * NT, turned: 2 * NT}) as p:
                attn_pair(p)

            lo(N_MERGE + 1, 4)
            attn_done = Count(S["attn_done"])
            dve.wait_ge(attn_done.sem, attn_done.after(4))
            V.memset(QRB[:], 0.0).then_inc(chain.sem, 1)
            dve.wait_ge(chain.sem, chain.after())
            for g in range(4):
                V.tensor_copy(QRB[32 * g:32 * g + 32, :, g, :],
                              QS[R0, :, :].rearrange("p h b -> p b h")).then_inc(chain.sem, 1)
                chain.add()
            V.memset(SCB[:, :, 32, :], NEG)
            V.tensor_scalar(QB[:].rearrange("p a b -> p (a b)"), SQ[:].rearrange("p a b -> p (a b)")[:, 0:448], 0.0,
                            None, ALU.mult).then_inc(S["qrb_ready"], 1)
            qrb = Count(S["qrb_ready"])
            dve.wait_ge(qrb.sem, qrb.after())
            ct_a, s_full, page_hi = Count(S["ct_act"]), Count(S["s_full"]), Count(S["page_hi"])
            bank_free, mxt, mxs = Count(S["s_bank_free"]), Count(S["mx_turned"]), Count(S["mx_spread"])
            exp_s, sums, pv_full = Count(S["exp_s"]), Count(S["sum_spread"]), Count(S["pv_full"])
            p_hi, lat_turned = Count(S["p_hi"]), Count(S["lat_turned"])

            def split_query(b):
                q = QAB[:, :, bass.ds(b, 1), :].rearrange("p a b h -> p a (b h)")
                V.tensor_copy(QB[:, :, 96:96 + HEADS], q).then_inc(chain.sem, 1)
                dve.wait_ge(chain.sem, chain.after())
                V.tensor_tensor(QB[:, :, 96 + HEADS:96 + 2 * HEADS], q, QB[:, :, 96:96 + HEADS].bitcast(F32), ALU.subtract
                                ).then_inc(S["q_parts"], 1)

            def chunk_lo(c):
                dve.wait_ge(ct_a.sem, ct_a.after())
                j = c % 2
                V.tensor_tensor(CTL[:, j].rearrange("p a b -> p (a b)"),
                                PS[:, 2 * j:2 * j + 2, :].rearrange("p a b -> p (a b)"),
                                CTH[:, j].rearrange("p a b -> p (a b)").bitcast(F32), ALU.subtract
                                ).then_inc(S["ct_dve"], 1)

            def page_lo(par, c):
                dve.wait_ge(page_hi.sem, page_hi.after())
                V.tensor_tensor(PLO[c % 4], PGC[:, par, 4 * c:4 * c + 4, :], PHI[c % 4].bitcast(F32),
                                ALU.subtract).then_inc(S["page_split"], 1)

            def probs_lo(par):
                dve.wait_ge(p_hi.sem, p_hi.after())
                V.tensor_tensor(PHL[:, :, HEADS:2 * HEADS], PB[:, par, 0:NPAGES], PHL[:, :, 0:HEADS].bitcast(F32),
                                ALU.subtract).then_inc(S["p_split"], 1)

            def scores_back(par, b):
                dve.wait_ge(s_full.sem, s_full.after())
                V.tensor_copy(SCB[:, par, 0:32, :].rearrange("p k h -> p (k h)"), PS[:, 6, 0:256])
                V.tensor_scalar(SCB[0:DEC, par, 32, :], PS[0:DEC, 6, 256:264], SMALL[0:DEC, bass.ds(b + 16, 1)], None,
                                ALU.add).then_inc(S["s_bank_free"], 1)
                dve.wait_ge(bank_free.sem, bank_free.after())
                V.reduce_max(SSM[:, par, 0:8], SCB[:, par].rearrange("p k h -> p h k"), AX).then_inc(S["mx_ready"], 1)

            def max_rows(par):
                dve.wait_ge(mxt.sem, mxt.after())
                V.reduce_max(SSM[0:8, par, 8:9], PS[0:8, 7, 0:P], AX).then_inc(chain.sem, 1)
                dve.wait_ge(chain.sem, chain.after())
                V.tensor_scalar(SSM[0:8, par, 16:24], IDENT[0:8, 0:8], SSM[0:8, par, 8:9], None, ALU.mult
                                ).then_inc(S["dg_ready"], 1)

            def shift(par):
                dve.wait_ge(mxs.sem, mxs.after())
                V.tensor_tensor(SCB[:, par], SCB[:, par],
                                PS[:, 7, P:P + 8].unsqueeze(1).to_broadcast([P, 33, 8]), ALU.subtract
                                ).then_inc(S["shifted"], 1)

            def sum_rows(par):
                dve.wait_ge(exp_s.sem, exp_s.after())
                V.reduce_sum(SSM[:, par, 24:32], PB[:, par].rearrange("p k h -> p h k"), AX).then_inc(S["sum_ready"], 1)

            def inv_sum(par):
                dve.wait_ge(sums.sem, sums.after())
                V.reciprocal(SSM[:, par, 32:40], PS[:, 7, P + 8:P + 16]).then_inc(S["rs_ready"], 1)
                V.memset(SCB[:, par, 32, :], NEG).then_inc(chain.sem, 1)
                dve.wait_ge(chain.sem, chain.after())

            def latent_out(par, b):
                dve.wait_ge(lat_turned.sem, lat_turned.after())
                V.tensor_tensor(OL[:, :, :, bass.ds(b, 1)].rearrange("p a h b -> p a (h b)"),
                                PS[:, 7, 144:160].rearrange("p (a h) -> p a h", a=2),
                                SSM[:, par, 32:40].unsqueeze(1).to_broadcast([P, 2, 8]), ALU.mult
                                ).then_inc(S["olat_ready"], 1)

            def outputs_back():
                dve.wait_ge(pv_full.sem, pv_full.after())
                V.tensor_copy(OPART[:], PS[0:2 * HEADS, 7, 256:256 + KVL]).then_inc(S["o_parts"], 1)

            def sample_dve(par, b, prev, more=True):
                for c in range(2, NCH):
                    chunk_lo(c)
                    if prev is not None:
                        if c % 2 == 0:
                            page_lo(prev, c // 2 - 1)
                        {3: max_rows, 5: shift, 7: sum_rows}.get(c, lambda q: None)(prev)
                if prev is not None:
                    probs_lo(prev)
                    inv_sum(prev)
                if more:
                    chunk_lo(0)
                if prev is not None:
                    page_lo(prev, 3)
                scores_back(par, b)
                if more:
                    split_query(b + 1)
                if prev is not None:
                    for c in range(4, NCH):
                        if c == 7 and more:
                            chunk_lo(1)
                        page_lo(prev, c)
                    outputs_back()
                    latent_out(prev, b - 1)
                else:
                    chunk_lo(1)

            split_query(0)
            chunk_lo(0)
            chunk_lo(1)
            sample_dve(0, 0, None)
            with loop(dve, 3, {chain: 6, ct_a: 2 * NCH, page_hi: 2 * NCH, mxt: 2, mxs: 2, exp_s: 2, sums: 2, s_full: 2,
                               bank_free: 2, pv_full: 2, p_hi: 2, lat_turned: 2}) as i:
                for par in range(2):
                    sample_dve(1 - par, i * 2 + (1 + par), par)
            sample_dve(1, DEC - 1, 0, False)
            max_rows(1)
            shift(1)
            sum_rows(1)
            probs_lo(1)
            inv_sum(1)
            for c in range(NCH):
                page_lo(1, c)
            outputs_back()
            latent_out(1, DEC - 1)
            a_full = Count(S["a_s_full"])
            dve.wait_ge(a_full.sem, a_full.after())
            for hh in range(2):
                last = V.tensor_copy(AT[64 * hh:64 * hh + 64, :, 0:DEC],
                                     PS[64 * hh:64 * hh + 64, 7, 0:64].rearrange("p (a c) -> p a c", a=4)
                                     [:, :, 8 * hh:8 * hh + 8])
            last.then_inc(S["a_done"], 1)

            ab = Count(S["ab_hi"])
            for hi_, lo_, full in ((AH, AL, AT), (BH, BL, BT)):
                dve.wait_ge(ab.sem, ab.after())
                V.tensor_tensor(lo_[:], full[:], hi_[:].bitcast(F32), ALU.subtract).then_inc(S["ab_split"], 1)
            gates, m_hi, m_added = [Count(S[f"gates_back{j}"], 16) for j in range(2)], Count(S["m_hi"]), Count(S["m_added"])
            done.n = N_MERGE

            def merge(jj, nk):
                if jj:
                    dve.wait_ge(S["m_split"], jj)
                dve.wait_ge(gates[jj % 2].sem, gates[jj % 2].after(2))
                dve.wait_ge(fd[0].sem, fd[0].after())
                V.scalar_tensor_tensor(two(GW[:, 0, 0]), two(GG[:, jj % 2, 0, 0]), 1.0, pair(0), ALU.add, ALU.mult
                                       ).then_inc(s_free[0], 1)
                dve.wait_ge(done.sem, done.after())
                V.scalar_tensor_tensor(two(GW[:, 0, 1]), two(GG[:, jj % 2, 0, 1]), 1.0, pair(1), ALU.add, ALU.mult
                                       ).then_inc(s_free[1], 1)
                lo(N_MERGE + 2, nk)
                dve.wait_ge(fd[2].sem, fd[2].after())
                V.scalar_tensor_tensor(two(GW[:, 1, 0]), two(GG[:, jj % 2, 1, 0]), 1.0, pair(2), ALU.add, ALU.mult
                                       ).then_inc(s_free[2], 1)
                dve.wait_ge(done.sem, done.after())
                V.scalar_tensor_tensor(two(GW[:, 1, 1]), two(GG[:, jj % 2, 1, 1]), 1.0, pair(3), ALU.add,
                                       ALU.mult).then_inc(chain.sem, 1)
                dve.wait_ge(chain.sem, chain.after())
                V.tensor_tensor(GW[:, 0], GW[:, 0], GW[:, 1], ALU.add).then_inc(S["m_added"], 1)
                lo(N_MERGE + 3, nk)
                dve.wait_ge(m_hi.sem, m_hi.after())
                V.scalar_tensor_tensor(ML[:, bass.ds(jj * 2, 2), :], GW[:, 0], 0.5,
                                       MH[:, bass.ds(jj * 2, 2), :].bitcast(F32), ALU.mult, ALU.subtract
                                       ).then_inc(S["m_split"], 1)

            for jj in range(4):
                merge(jj, 4 if jj < 3 else 8)

            for n in (N_O, N_O + 1, N_O):
                lo(n)

            y_back = Count(S["y_back"], 16)
            dve.wait_ge(y_back.sem, y_back.after(2))
            taken = Count(S["back_taken"])

            def residual(t):
                p = t % 2
                r = tile_cols(t)[1]
                dve.wait_ge(fd[p].sem, fd[p].after())
                y = YK[0:r, t, :].rearrange("p (a b) -> p a b", a=2)
                V.scalar_tensor_tensor(y, y, ALPHA, PS[0:r, 2 * p:2 * p + 2, :], ALU.mult, ALU.add
                                       ).then_inc(S["back_taken"], 1)

            dve.wait_ge(gb.sem, gb.after(2))
            for t in range(NT):
                residual(t)
                dve.wait_ge(taken.sem, taken.after())
                norm_begin(YK, t, GB1)
                if t >= 3:
                    turned_lo(t - 3)
            turned_lo(NT - 3)
            turned_lo(NT - 2)
            turned_lo(NT - 1)
            lo(N_O + 1)

            V.memset(AB[:, :, 0:2], 0.0).then_inc(S["rows_zeroed"], 1)
            first, gelu, h_hi = Count(S["conv_first"]), Count(S["gelu_done"]), Count(S["h_hi"])

            def conv(m, f):
                dve.wait_ge(first.sem, first.after())
                V.scalar_tensor_tensor(ACC[:, m, DEC:], AB[:, m, 1:1 + META + SEQ],
                                       CV[:, bass.ds(f + FT, 1)], ACC[:, m, DEC:], ALU.mult, ALU.add).then_inc(chain.sem, 1)
                chain.add()
                V.scalar_tensor_tensor(
                    ACC[:, m, 0:DEC], PV[:, bass.ds(f, 1), 1:2 * DEC:2].rearrange("p a c -> p (a c)"),
                    CV[:, bass.ds(f + FT, 1)], ACC[:, m, 0:DEC], ALU.mult, ALU.add).then_inc(chain.sem, 1)
                dve.wait_ge(chain.sem, chain.after())
                V.scalar_tensor_tensor(ACC[:, m, DEC:], AB[:, m, 2:], CV[:, bass.ds(f + 2 * FT, 1)],
                                       ACC[:, m, DEC:], ALU.mult, ALU.add)
                V.scalar_tensor_tensor(
                    ACC[:, m, 0:DEC].rearrange("p (k r) -> p k r", k=2), css(f), CV[:, bass.ds(f + 2 * FT, 1)],
                    ACC[:, m, 0:DEC].rearrange("p (k r) -> p k r", k=2), ALU.mult, ALU.add).then_inc(S["conv_acc"], 1)

            for part, nf in enumerate(FFN_TILES):
                f0 = sum(FFN_TILES[:part])
                na, no = (N_F1, N_F2)[part], (N_F1O, N_F2O)[part]
                hk = nf // 2
                done.n = na + 1

                def ffn_in_pair(i, next_a, next_b, skip):
                    for m in range(2):
                        conv(m, i * 2 + (f0 + m))
                    next_a()
                    for m in range(2):
                        if m == 0:
                            dve.wait_ge(fd[2].sem, fd[2].after())
                        else:
                            dve.wait_ge(done.sem, done.after())
                        dve.wait_ge(gelu.sem, gelu.after())
                        V.tensor_tensor(two(HF[:, m]), two(GL[:, m]), pair(2 + m), ALU.mult).then_inc(S["h_ready"], 1)
                    for m in range(2):
                        dve.wait_ge(h_hi.sem, h_hi.after())
                        fm = bass.ds(i * 2 + m, 1)
                        V.tensor_tensor(FL[:, fm, :].rearrange("p a c -> p (a c)"), HF[:, m],
                                        FH[:, fm, :].rearrange("p a c -> p (a c)").bitcast(F32), ALU.subtract
                                        ).then_inc(s_free[2 + m], 1)
                    next_b()
                    dve.wait_ge(done.sem, done.after(skip))

                with loop(dve, nf // 2 - 1, {whi: 2, chain: 4, first: 2, gelu: 2, h_hi: 2, fd[2]: 1, done: 2}) as i:
                    ffn_in_pair(i, lambda: lo(na), lambda: lo(na + 1), 1)
                ffn_in_pair(nf // 2 - 1, lambda: lo(no, hk), lambda: lo(no + 1, hk), 0)
                last_part = part == 1

                def out_cols(jj, lo_a, lo_b):
                    lo_a()
                    if last_part:
                        tt = TT[:, bass.ds(jj * 2, 2), :]
                        for m in range(2):
                            if m == 0:
                                dve.wait_ge(fd[0].sem, fd[0].after())
                            else:
                                dve.wait_ge(done.sem, done.after(2))
                            t_ = TT[:, bass.ds(jj * 2 + m, 1), :].rearrange("p a c -> p (a c)")
                            V.tensor_tensor(two(t_), two(t_), pair(m), ALU.add).then_inc(s_free[m], 1)
                    lo_b()

                per = {whi: 2}
                if last_part:
                    per[fd[0]], per[done] = 1, 2
                with loop(dve, 3, per) as jj:
                    out_cols(jj, lambda: lo(no, hk), lambda: lo(no + 1, hk))
                if last_part:
                    out_cols(3, lambda: None, lambda: None)
                else:
                    out_cols(3, lambda: lo(N_F2), lambda: lo(N_F2 + 1))

            dve.wait_ge(fd[3].sem, fd[3].after())
            V.tensor_copy(CST[0:2 * FT, 0, :], PS[0:2 * FT, 6, 0:P]).then_inc(S["cst_ready"], 1)
            for k in range(2):
                V.tensor_copy(CST[0:4 * FT, 1 + k, :], PS[0:4 * FT, 7, k * P:(k + 1) * P]).then_inc(S["cst_ready"], 1)
            dve.wait_ge(S["x_normed"], 2 * NT)
            dve.wait_ge(gb.sem, gb.after(2))
            for t in range(NT):
                residual(t)
                dve.wait_ge(taken.sem, taken.after())
                norm_begin(YK, t, GB2)

        @block.tensor
        def _(pe):
            T = nc.tensor
            free = [Count(s_free[p]) for p in range(4)]
            split = Count(s_wsplit)

            def tile(par, m, nk, xh, xl, k0, p, done=None, start=True, stop=True, halves=(0, 1), ks=None):
                for k in ks or range(nk):
                    for w, xs in ((WH, (xh, xl)), (WL, (xh,))):
                        for j, x in enumerate(xs):
                            for half in halves:
                                bank = 2 * p + half
                                last = T.matmul(PS[:, bank, 0:HALF], w[:, par, k, m * P:(m + 1) * P],
                                                x[:, k0 + k, half * HALF:(half + 1) * HALF],
                                                start=start and k == 0 and w is WH and j == 0,
                                                stop=stop and k == nk - 1 and w is WL)
                if done is not None:
                    last.then_inc(done, 1)

            def small(p, lhs, rhs, done):
                for half in range(2):
                    for i, (a, b) in enumerate(zip(lhs, rhs)):
                        last = T.matmul(PS[:, 2 * p + half, 0:HALF], a, b[:, half * HALF:(half + 1) * HALF],
                                        start=i == 0, stop=i == len(lhs) - 1)
                last.then_inc(done, 1)

            def forward(x, t):
                if t >= 2:
                    pe.wait_ge(x_split.sem, x_split.after())
                pe.wait_ge(normed.sem, normed.after())
                r = tile_cols(t)[1]
                for k in range(KT):
                    last = T.transpose(PS[:, 4 + 2 * (t % 2) + k // 4, (k % 4) * P:(k % 4) * P + r],
                                       x[0:r, t, k * P:(k + 1) * P], IDENT[0:r, 0:r])
                last.then_inc(S["ln_turned"], 1)

            def backward(t):
                if t >= 2:
                    pe.wait_ge(taken.sem, taken.after())
                c, r = evac_cols(t)
                for k in range(KT):
                    last = T.transpose(PS[0:r, 2 * (t % 2) + k // 4, (k % 4) * P:(k % 4 + 1) * P], TT[:, k, c],
                                       IDENT)
                last.then_inc(s_fd[t % 2], 1)

            pe.sem_inc(s_free[0], 1)
            pe.sem_inc(s_free[1], 1)
            pe.sem_inc(s_free[2], 1)
            pe.sem_inc(s_free[3], 1)
            x_split, normed, taken = Count(S["x_split"]), Count(S["x_normed"]), Count(S["back_taken"])
            c1, c2 = Count(S["consts_landed"], 16), Count(S["consts2_landed"], 16)
            pe.wait_ge(c1.sem, c1.after(8))
            pe.wait_ge(free[0].sem, free[0].after())
            T.transpose(PS[:, 0, 0:9], VR[0:9, 0, :], IDENT[0:9, 0:9])
            T.transpose(PS[:, 1, 0:4 * FT], VR[0:4 * FT, 1, :], IDENT[0:4 * FT, 0:4 * FT]).then_inc(s_fd[0], 1)
            pe.wait_ge(free[2].sem, free[2].after())
            pe.wait_ge(free[3].sem, free[3].after())
            for t in range(NT):
                forward(XK, t)
            pe.wait_ge(x_split.sem, x_split.after(2))
            pe.sem_inc(s_free[2], 1)
            pe.sem_inc(s_free[3], 1)
            vt = Count(S["vectors_T_ready"])
            pe.wait_ge(vt.sem, vt.after())
            pe.sem_inc(s_free[0], 1)
            pe.wait_ge(c2.sem, c2.after(8))
            pe.wait_ge(free[1].sem, free[1].after())
            rows = CN[:].rearrange("p a b -> p (a b)")
            for f in range(FT):
                last = T.transpose(PS[:, 2, 16 * f:16 * f + 16], rows[:, f * P:(f + 1) * P], IDENT[0:16, 0:16])
            last.then_inc(s_fd[1], 1)

            k_feat, q_feat, g_ready = Count(S["k_feat"]), Count(S["q_feat"]), Count(S["g_ready"])
            inner, sn, ot = Count(S["inner_ready"]), Count(S["sn_ready"]), Count(S["ot_ready"])
            sq, sd, tok = Count(S["sq_ready"]), Count(S["sd_ready"]), Count(S["tok_ready"])

            def outputs():
                pe.wait_ge(inner.sem, inner.after())
                for t in range(1, NT):
                    out = PS[:, 6, P * (t - 1):P * t]
                    T.matmul(out, VTOK[:, t, :], INT[:, t - 1, :], start=True, stop=False)
                    T.matmul(out, RS[:, t - 1, :], RQD[:, t - 1, :], start=False, stop=True)
                T.matmul(PS[:, 7, 0:T0], VTOK[0:T0, 0, :], IN0[0:T0, :], start=True, stop=True).then_inc(s_fd[3], 1)
                for j in range(2):
                    last = T.matmul(PS[:, 4 + j, :], KTOK0[0:DEC, :],
                                    VBLK[0:DEC, 4 * j:4 * j + 4, :].rearrange("p b v -> p (b v)"), start=True, stop=True)
                last.then_inc(s_fd[2], 1)

            def sample_out():
                pe.wait_ge(sn.sem, sn.after())
                for b in range(DEC):
                    last = T.matmul(PS[:, 6, b:b + 1], ST[:, b, :], RQ[:, b:b + 1], start=True, stop=True)
                last.then_inc(s_fd[3], 1)

            def centre():
                pe.wait_ge(ot.sem, ot.after())
                small(2, [CENTRE], [OT], s_fa[2])

            def variance():
                pe.wait_ge(sq.sem, sq.after())
                small(3, [MEAN], [OSQ], s_fa[3])

            def ret_head(prev):
                pe.wait_ge(split.sem, split.after())
                if not prev:
                    pe.wait_ge(free[0].sem, free[0].after())
                tile(0, 0, 8, XH, XL, 0, 0, s_fa[0])
                if prev:
                    outputs()
                    pe.wait_ge(g_ready.sem, g_ready.after())
                else:
                    pe.wait_ge(free[1].sem, free[1].after())
                tile(0, 1, 8, XH, XL, 0, 1, s_done)
                if prev:
                    sample_out()
                    centre()
                pe.wait_ge(split.sem, split.after())
                pe.wait_ge(k_feat.sem, k_feat.after())
                tile(1, 0, 8, XH, XL, 0, 0, ks=range(4))
                if prev:
                    variance()
                tile(1, 0, 8, XH, XL, 0, 0, s_fa[0], ks=range(4, 8))
                if not prev:
                    pe.wait_ge(free[2].sem, free[2].after())
                pe.wait_ge(free[1].sem, free[1].after())
                for t in range(1, NT):
                    c, _ = evac_cols(t)
                    T.transpose(PS[:, 4, P * (t - 1):P * t], RK[:, c], IDENT)
                    last = T.transpose(PS[:, 5, P * (t - 1):P * t], RV[:, c], IDENT)
                last.then_inc(s_fd[2], 1)
                if prev:
                    pe.wait_ge(sd.sem, sd.after())
                else:
                    pe.wait_ge(free[3].sem, free[3].after())
                T.transpose(PS[0:T0, 6, 0:P], RK[:, 0:T0], IDENT)
                T.transpose(PS[0:T0, 6, P:2 * P], RV[:, 0:T0], IDENT).then_inc(s_fd[3], 1)
                tile(1, 1, 8, XH, XL, 0, 1, s_done)
                pe.wait_ge(tok.sem, tok.after())
                pe.wait_ge(q_feat.sem, q_feat.after())
                for t in range(1, NT):
                    c, _ = evac_cols(t)
                    T.matmul(PS[:, 4, P * (t - 1):P * t], RK[:, c], RQ[:, c], start=True, stop=True)
                    last = T.matmul(PS[:, 5, P * (t - 1):P * t], KDEC[:, t, :], VTOK[:, t, :], start=True, stop=True)
                last.then_inc(s_fd[2], 1)
                T.matmul(PS[0:T0, 6, 0:T0], RK[:, 0:T0], RQ[:, 0:T0], start=True, stop=True)
                T.matmul(PS[:, 6, P:2 * P], KDEC[0:T0, 0, :], VTOK[0:T0, 0, :], start=True, stop=True
                         ).then_inc(s_fd[3], 1)

            ret_head(False)
            with loop(pe, RH - 1, {split: 2, k_feat: 1, q_feat: 1, g_ready: 1, inner: 1, sn: 1, ot: 1, sq: 1, sd: 1,
                                   tok: 1, free[1]: 1}):
                ret_head(True)
            outputs()
            sample_out()
            centre()
            variance()
            pe.wait_ge(sd.sem, sd.after())
            pe.wait_ge(g_ready.sem, g_ready.after())

            lat_sq, lat_sd, normed_l = Count(S["lat_sq"]), Count(S["lat_sd"]), Count(S["lat_normed"])
            pe.wait_ge(split.sem, split.after())
            tile(0, 0, 8, XH, XL, 0, 0, s_fa[0])
            tile(0, 1, 8, XH, XL, 0, 1, s_done)
            pe.wait_ge(split.sem, split.after())
            pe.wait_ge(free[0].sem, free[0].after())
            tile(1, 0, 8, XH, XL, 0, 0, s_fa[0])
            pe.wait_ge(free[1].sem, free[1].after())
            tile(1, 1, 8, XH, XL, 0, 1, s_done)
            pe.wait_ge(lat_sq.sem, lat_sq.after())
            small(2, [ONES] * 3, [QSQ[:, j, :] for j in range(3)], s_fa[2])
            pe.wait_ge(split.sem, split.after())
            tile(0, 0, 8, XH, XL, 0, 0, s_fa[0])
            pe.wait_ge(free[1].sem, free[1].after())
            tile(0, 1, 8, XH, XL, 0, 1, s_done)
            pe.wait_ge(lat_sq.sem, lat_sq.after())
            small(3, [ONES] * 2, [QSQ[:, j, :] for j in range(2)], s_fa[3])
            pe.wait_ge(lat_sd.sem, lat_sd.after(2))
            pe.wait_ge(normed_l.sem, normed_l.after(2))
            for t in range(1, NT):
                c, _ = evac_cols(t)
                for j in range(2):
                    at_ = (t - 1) % 2 * KVL + j * P
                    last = T.transpose(PS[:, 4 + (t - 1) // 2, at_:at_ + P], CNT[:, j, c], IDENT)
            last.then_inc(s_fd[2], 1)
            for j in range(2):
                T.transpose(PS[0:T0, 6, j * P:(j + 1) * P], CNT[:, j, 0:T0], IDENT)
            for t in range(1, NT):
                c, _ = evac_cols(t)
                T.transpose(PS[:, 7, ROPE * (t - 1):ROPE * t], KRT[0:ROPE, c], IDENT[0:ROPE, 0:ROPE])
            T.transpose(PS[0:T0, 7, P:P + ROPE], KRT[0:ROPE, 0:T0], IDENT[0:ROPE, 0:ROPE]).then_inc(s_fd[3], 1)
            tok_out = Count(S["tok_out_ready"])

            pe.wait_ge(free[0].sem, free[0].after())
            pe.sem_inc(S["gate_free0"], 1)
            pe.sem_inc(S["gate_free1"], 1)
            gate_free = [Count(S[f"gate_free{j}"]) for j in range(2)]
            head_w, uk_T, q_heads = Count(S["head_w_landed"], 16), Count(S["uk_T_ready"]), Count(S["q_heads_ready"])
            probs, pt_a, pt_d, attn = Count(S["probs_ready"]), Count(S["pt_act"]), Count(S["pt_dve"]), Count(S["attn_done"])

            def gate(g, k_range=range(8)):
                half = g % 2
                if 0 in k_range:
                    if g % 4 == 0:
                        pe.wait_ge(split.sem, split.after())
                    pe.wait_ge(gate_free[half].sem, gate_free[half].after())
                par, m = (N_GATE + g // 4) % 2, (g // 2) % 2
                for k in k_range:
                    for w, xs in ((WH, (XH, XL)), (WL, (XH,))):
                        for j, x in enumerate(xs):
                            last = T.matmul(PS[:, half, 0:HALF], w[:, par, k, m * P:(m + 1) * P],
                                            x[:, k, half * HALF:(half + 1) * HALF],
                                            start=k == 0 and w is WH and j == 0, stop=k == 7 and w is WL)
                if 7 in k_range:
                    last.then_inc(s_done if g % 4 == 3 else S["gate_full"], 1)

            def scores(s):
                t, hh = divmod(s, 2)
                c, r = evac_cols(t)
                n = META + P * (t - 1)
                if t:
                    T.matmul(PS[:, 4 + hh, 0:n], QT[0:QD_, hh, c], KTB[0:QD_, hh, DEC:DEC + n], start=True, stop=True)
                    last = T.matmul(PS[:, 6 + hh, 0:P], QT[0:QD_, hh, c], KTB[0:QD_, hh, c], start=True, stop=True)
                else:
                    last = T.matmul(PS[0:r, 6 + hh, 0:META], QT[0:QD_, hh, c], KTB[0:QD_, hh, DEC:T0],
                                    start=True, stop=True)
                last.then_inc(S["scores_full"], 1)

            def turn_probs(s):
                t, hh = divmod(s, 2)
                pe.wait_ge(probs.sem, probs.after())
                pe.sem_inc(S["go_on"])
                r = tile_cols(t)[1]
                for k in range(t + 1):
                    e0_, w = (0, META) if k == 0 else (META + P * (k - 1), P)
                    bank, at_ = (4 + hh, k * P) if k < 4 else (6 + hh, 0)
                    last = T.transpose(PS[0:w, bank, at_:at_ + r], EX[0:r, hh, e0_:e0_ + w], IDENT[0:r, 0:r])
                last.then_inc(S["probs_turned"], 1)

            def weigh(s):
                t, hh = divmod(s, 2)
                if hh:
                    pe.wait_ge(pt_d.sem, pt_d.after())
                else:
                    pe.wait_ge(pt_a.sem, pt_a.after())
                r = tile_cols(t)[1]
                rows_ = slice(64 * hh, 64 * hh + 64)
                out = PS[rows_, 2, P * (t - 1):P * t] if t else PS[rows_, 3, 0:T0]
                for k in range(t + 1):
                    w = P if k else META
                    last = T.matmul(out, VB[0:w, k, rows_], PTS[0:w, hh, k, 0:r], start=k == 0, stop=k == t)
                return last

            def attn_pair(p):
                pe.wait_ge(head_w.sem, head_w.after(7))
                pe.wait_ge(free[2].sem, free[2].after())
                small(2, [UQ[:, k, 0, :] for k in range(3)], [QN[:, k, :] for k in range(3)], s_fd[2])
                pe.wait_ge(free[3].sem, free[3].after())
                small(3, [UQ[:, k, 1, :] for k in range(3)], [QN[:, k, :] for k in range(3)], s_fd[3])
                small(1, [UK[:, k, :] for k in range(2)], [CNT[:, k, :] for k in range(2)], s_fd[1])
                gate(0)
                pe.wait_ge(free[2].sem, free[2].after())
                pe.wait_ge(free[3].sem, free[3].after())
                for t in range(NT):
                    c, r = evac_cols(t)
                    if t == 0:
                        c, r = slice(DEC, T0), META
                    for k in range(2):
                        out = PS[:, 4, P * (t - 1):P * t] if t else PS[0:META, 5, 0:P]
                        last = T.matmul(out, CNT[:, k, c], UV[:, k, bass.ds(p * P, P)], start=k == 0, stop=k == 1)
                last.then_inc(s_fd[2], 1)
                for hh in range(2):
                    for k in range(2):
                        last = T.transpose(PS[0:NOPE, 6, (2 * hh + k) * P:(2 * hh + k + 1) * P],
                                           UK[:, k, hh * NOPE:(hh + 1) * NOPE], IDENT)
                last.then_inc(S["proj_done"], 1)
                gate(1)
                pe.wait_ge(uk_T.sem, uk_T.after())
                pe.wait_ge(q_heads.sem, q_heads.after())
                for k in range(2):
                    for hh in range(2):
                        last = T.matmul(PS[:, 6, (2 * k + hh) * DEC:(2 * k + hh + 1) * DEC], UKT[0:NOPE, hh, k, :],
                                        QT[0:NOPE, hh, 0:DEC], start=True, stop=True)
                last.then_inc(s_fd[3], 1)
                gate(2)
                pe.wait_ge(free[2].sem, free[2].after())
                pe.wait_ge(free[3].sem, free[3].after())
                scores(0)
                scores(1)
                for s in range(2 * NT):
                    turn_probs(s)
                    gate(3 + s // 2, range(4 * (s % 2), 4 * (s % 2) + 4))
                    last = weigh(s)
                    if s + 2 < 2 * NT:
                        scores(s + 2)
                last.then_inc(s_fd[1], 1)
                pe.sem_inc(s_free[2], 1)
                pe.sem_inc(s_free[3], 1)
                pe.wait_ge(attn.sem, attn.after())

            pe.wait_ge(tok_out.sem, tok_out.after())
            pe.sem_inc(s_free[3], 1)
            with loop(pe, 4, {head_w: 7, free[2]: 3, free[3]: 3, split: 2, gate_free[0]: 4, gate_free[1]: 4, uk_T: 1,
                              q_heads: 1, probs: 2 * NT, pt_a: NT, pt_d: NT, attn: 1}) as p:
                attn_pair(p)

            pe.wait_ge(free[2].sem, free[2].after())
            pe.wait_ge(free[3].sem, free[3].after())
            pe.wait_ge(gate_free[0].sem, gate_free[0].after())
            pe.wait_ge(gate_free[1].sem, gate_free[1].after())
            pages = [[Count(s_pg[j][c], 16) for c in range(NCH)] for j in range(2)]
            rope_p = [Count(S[f"rope_pages{j}"], 16) for j in range(2)]
            ct_a, ct_d, bank_free = Count(S["ct_act"]), Count(S["ct_dve"]), Count(S["s_bank_free"])
            mx, dg, sums, rs = Count(S["mx_ready"]), Count(S["dg_ready"]), Count(S["sum_ready"]), Count(S["rs_ready"])
            olat = Count(S["olat_ready"])
            qrb = Count(S["qrb_ready"])
            pe.wait_ge(qrb.sem, qrb.after())

            def turn_rope(par):
                pe.wait_ge(rope_p[par].sem, rope_p[par].after())
                for c in range(NCH):
                    last = T.transpose(PS[:, 2 + c // 4, P * (c % 4):P * (c % 4 + 1)],
                                       PGR[:, par, 4 * c:4 * c + 4, :].rearrange("p r d -> p (r d)"), IDENT)
                last.then_inc(S["rope_turned"], 1)

            def turn_chunk(par, c):
                pe.wait_ge(pages[par][c].sem, pages[par][c].after())
                for ct in range(2):
                    for r in range(4):
                        last = T.transpose(PS[:, 2 * (c % 2) + ct, P * r:P * (r + 1)],
                                           PGC[:, par, 4 * c + r, ct * P:(ct + 1) * P], IDENT)
                last.then_inc(S["chunk_turned"], 1)

            def q_of(b, ct, n=P):
                return QAB[0:n, ct, bass.ds(b, 1), :].rearrange("p b h -> p (b h)")

            def score_chunk(c, b, wait_bank):
                pe.wait_ge(ct_a.sem, ct_a.after())
                pe.wait_ge(ct_d.sem, ct_d.after())
                if c == 0 and wait_bank:
                    pe.wait_ge(bank_free.sem, bank_free.after())
                T.matmul(PS[:, 6, 32 * c:32 * c + 32], RTT[:, c, :],
                         QRB[:, bass.ds(b, 1), :, :].rearrange("p b g h -> p (b g h)"), start=c == 0, stop=False,
                         skip_group_check=True)
                g = c % 4
                for ct in range(2):
                    for x in (CTH, CTL):
                        last = T.matmul(PS[:, 4 + c // 4, :], QB[:, ct, 96 - 32 * g:224 - 32 * g],
                                        x[:, c % 2].rearrange("p a b -> p (a b)")[:, 512 * ct:512 * ct + 512],
                                        start=g == 0 and ct == 0 and x is CTH, stop=g == 3 and ct == 1 and x is CTL)
                last.then_inc(S["chunk_scored"], 1)

            def add_parts(a):
                pe.wait_ge(parts.sem, parts.after())
                for r in range(4):
                    out = PS[:, 6, 0:256].rearrange("p (a g r h) -> p a r g h", a=2, g=4, r=4)[:, a, r]
                    last = T.matmul(out, SPART[:, a, P * r:P * (r + 1)], SMALL[:, 26:58], start=False,
                                    stop=a == 1 and r == 3, skip_group_check=True)
                return last

            def score_new(b):
                out = PS[0:DEC, 6, 256:264]
                for ct in range(2):
                    T.matmul(out, CN8[:, ct, :], q_of(b, ct), start=False, stop=False, skip_group_check=True)
                T.matmul(out, KR8[:], QRB[:, bass.ds(b, 1), 0, :].rearrange("p b h -> p (b h)"),
                         start=False, stop=True, skip_group_check=True)

            def max_turn(par):
                pe.wait_ge(mx.sem, mx.after())
                T.transpose(PS[0:8, 7, 0:P], SSM[:, par, 0:8], IDENT).then_inc(S["mx_turned"], 1)

            def max_spread(par):
                pe.wait_ge(dg.sem, dg.after())
                T.matmul(PS[:, 7, P:P + 8], ONES[0:8, :], SSM[0:8, par, 16:24], start=True, stop=True
                         ).then_inc(S["mx_spread"], 1)

            def sum_spread(par):
                pe.wait_ge(sums.sem, sums.after())
                T.matmul(PS[:, 7, P + 8:P + 16], ONES, SSM[:, par, 24:32], start=True, stop=True
                         ).then_inc(S["sum_spread"], 1)

            def latent_turn():
                pe.wait_ge(o_parts.sem, o_parts.after())
                for ct in range(2):
                    last = T.matmul(PS[:, 7, 144 + 8 * ct:152 + 8 * ct], OPART[:, ct * P:(ct + 1) * P],
                                    SMALL[0:2 * HEADS, 26:26 + HEADS], start=True, stop=True)
                last.then_inc(S["lat_turned"], 1)

            def sample_weigh(par, midway=None):
                pe.wait_ge(p_split.sem, p_split.after())
                pe.wait_ge(rs.sem, rs.after())
                out = PS[0:2 * HEADS, 7, 256:256 + KVL]
                for c in range(NCH):
                    if c == 3 and midway:
                        midway()
                    pe.wait_ge(page_split.sem, page_split.after())
                    for r in range(4):
                        for x in (PHI, PLO):
                            last = T.matmul(out, PHL[:, 4 * c + r, :], x[c % 4][:, r, :],
                                            start=c == 0 and r == 0 and x is PHI, stop=False, skip_group_check=True)
                    last.then_inc(S["pv_chunk"], 1)
                T.matmul(PS[0:HEADS, 7, 256:256 + KVL], PB[0:DEC, par, 32, :], CTX[0:DEC, :], start=False, stop=True,
                         skip_group_check=True).then_inc(S["pv_full"], 1)

            def second_turn(par):
                pe.wait_ge(rope_back.sem, rope_back.after())
                turn_chunk(par, 1)

            def first_scores(b, wait_bank):
                pe.wait_ge(q_parts.sem, q_parts.after())
                score_chunk(0, b, wait_bank)

            def sample(par, b, prev, more=True):
                for c in range(1, NCH):
                    if c + 1 < NCH:
                        turn_chunk(par, c + 1)
                    else:
                        add_parts(0)
                    score_chunk(c, b, False)
                    if prev is not None:
                        {2: max_turn, 4: max_spread, 7: sum_spread}.get(c, lambda q: None)(prev)
                score_new(b)
                if more:
                    turn_chunk(1 - par, 0)
                    turn_rope(1 - par)
                add_parts(1).then_inc(S["s_full"], 1)
                if prev is not None:
                    sample_weigh(prev, (lambda: second_turn(1 - par)) if more else None)
                elif more:
                    second_turn(1 - par)
                if more:
                    first_scores(b + 1, True)
                if prev is not None:
                    latent_turn()

            rope_back, q_parts, parts = Count(S["rope_back"]), Count(S["q_parts"]), Count(S["parts_back"])
            o_parts, page_split, p_split = Count(S["o_parts"]), Count(S["page_split"]), Count(S["p_split"])
            turn_chunk(0, 0)
            turn_rope(0)
            second_turn(0)
            first_scores(0, False)
            sample(0, 0, None)
            per = {ct_a: 2 * NCH, ct_d: 2 * NCH, bank_free: 2, mx: 2, dg: 2, sums: 2, rs: 2,
                   rope_p[0]: 1, rope_p[1]: 1, rope_back: 2, q_parts: 2, parts: 4, o_parts: 2, p_split: 2,
                   page_split: 2 * NCH}
            per.update({pages[j][c]: 1 for j in range(2) for c in range(NCH)})
            with loop(pe, 3, per) as i:
                for par in range(2):
                    sample(1 - par, i * 2 + (1 + par), par)
            sample(1, DEC - 1, 0, False)
            pe.wait_ge(olat.sem, olat.after(DEC - 1))
            max_turn(1)
            max_spread(1)
            sum_spread(1)
            sample_weigh(1)
            latent_turn()
            pe.wait_ge(olat.sem, olat.after())
            for p in range(4):
                for ct in range(2):
                    last = T.matmul(PS[:, 7, 16 * p:16 * p + 16], UV[:, ct, p * P:(p + 1) * P],
                                    OL[:, ct, 2 * p:2 * p + 2, :].rearrange("p h b -> p (h b)"),
                                    start=ct == 0, stop=ct == 1)
            last.then_inc(S["a_s_full"], 1)
            ab, m_added, m_split = Count(S["ab_split"]), Count(S["m_added"]), Count(S["m_split"])
            pe.wait_ge(ab.sem, ab.after())

            pe.sem_inc(s_free[0], 1)
            pe.sem_inc(s_free[1], 1)
            pe.sem_inc(s_free[2], 1)

            def merge(first=False):
                pe.wait_ge(split.sem, split.after())
                pe.wait_ge(free[0].sem, free[0].after())
                tile(N_MERGE % 2, 0, 4, AH, AL, 0, 0, s_fd[0])
                pe.wait_ge(free[1].sem, free[1].after())
                tile(N_MERGE % 2, 1, 4, AH, AL, 0, 1, s_done)
                pe.wait_ge(split.sem, split.after())
                pe.wait_ge(free[2].sem, free[2].after())
                if first:
                    pe.wait_ge(ab.sem, ab.after())
                tile((N_MERGE + 1) % 2, 0, 4, BH, BL, 0, 2, s_fd[2])

            def merge_last():
                tile((N_MERGE + 1) % 2, 1, 4, BH, BL, 0, 3, s_done)

            merge(True)
            merge_last()
            with loop(pe, 3, {split: 2, free[0]: 1, free[1]: 1, free[2]: 1, m_added: 1}):
                merge()
                pe.wait_ge(m_added.sem, m_added.after())
                merge_last()

            pe.wait_ge(m_split.sem, m_split.after(3))
            for j in range(2):
                pe.wait_ge(split.sem, split.after())
                for m in range(2):
                    if 2 * j + m < 3:
                        pe.wait_ge(free[2 * j + m].sem, free[2 * j + m].after())
                    else:
                        pe.wait_ge(m_added.sem, m_added.after())
                    tile((N_O + j) % 2, m, 8, MH, ML, 0, 2 * j + m, ks=range(6))
            pe.wait_ge(m_split.sem, m_split.after())
            for j in range(2):
                for m in range(2):
                    tile((N_O + j) % 2, m, 8, MH, ML, 0, 2 * j + m, s_done if m else s_fa[2 * j], ks=range(6, 8))
            for j in range(2):
                pe.wait_ge(split.sem, split.after())
                for m in range(2):
                    pe.wait_ge(free[2 * j + m].sem, free[2 * j + m].after())
                    tile((N_O + j) % 2, m, 8, MH, ML, 0, 2 * j + m, s_done if m else s_fa[2 * j])

            pe.wait_ge(free[0].sem, free[0].after())
            pe.wait_ge(free[1].sem, free[1].after())
            pe.wait_ge(free[2].sem, free[2].after())
            pe.wait_ge(free[3].sem, free[3].after())
            backward(0)
            backward(1)
            backward(2)
            for t in range(NT):
                forward(YK, t)
                if t + 3 < NT:
                    backward(t + 3)
            pe.wait_ge(x_split.sem, x_split.after(2))
            pe.wait_ge(taken.sem, taken.after(2))
            pe.sem_inc(s_free[0], 1)
            pe.sem_inc(s_free[1], 1)
            pe.sem_inc(s_free[2], 1)
            pe.sem_inc(s_free[3], 1)

            for part, nf in enumerate(FFN_TILES):
                na, no = (N_F1, N_F2)[part], (N_F1O, N_F2O)[part]
                hk = nf // 2
                with loop(pe, nf // 2, {split: 2, free[0]: 1, free[1]: 1, free[2]: 1, free[3]: 1}):
                    for j in range(2):
                        pe.wait_ge(split.sem, split.after())
                        for m in range(2):
                            pe.wait_ge(free[2 * j + m].sem, free[2 * j + m].after())
                            tile((na + j) % 2, m, 8, XH, XL, 0, 2 * j + m, s_done if m else s_fa[0] if j == 0 else s_fd[2])
                pe.wait_ge(free[2].sem, free[2].after())
                pe.wait_ge(free[3].sem, free[3].after())
                with loop(pe, 4, {split: 2, free[0]: 1, free[1]: 1}):
                    pe.wait_ge(split.sem, split.after())
                    pe.wait_ge(free[0].sem, free[0].after())
                    tile(no % 2, 0, hk, FH, FL, 0, 0, None, stop=False)
                    pe.wait_ge(free[1].sem, free[1].after())
                    tile(no % 2, 1, hk, FH, FL, 0, 1, s_done, stop=False)
                    pe.wait_ge(split.sem, split.after())
                    tile((no + 1) % 2, 0, hk, FH, FL, hk, 0, s_fa[0] if part == 0 else s_fd[0], start=False)
                    tile((no + 1) % 2, 1, hk, FH, FL, hk, 1, s_done, start=False)
                if part == 0:
                    pe.sem_inc(s_free[2], 1)
                    pe.sem_inc(s_free[3], 1)
            T.transpose(PS[0:2 * FT, 6, 0:P], CSP[:].rearrange("p f c -> p (f c)"), IDENT)
            for k in range(2):
                last = T.transpose(PS[0:4 * FT, 7, k * P:(k + 1) * P], CSS[:, k, :, :].rearrange("p f r -> p (f r)"), IDENT)
            last.then_inc(s_fd[3], 1)
            pe.wait_ge(free[0].sem, free[0].after())
            pe.wait_ge(free[1].sem, free[1].after())
            for t in range(NT):
                backward(t)


_INS = ["x_prompt", "x_sample", "cache_kv_latent", "cache_k_rope", "state_retention", "state_ffn_conv", "page_table",
        "meta_tokens", "ln0_g", "ln0_b", "w_in", "q_norm_g", "kv_norm_g", "w_uq", "w_uk", "w_uv", "ret_gn_g",
        "w_attn_out", "w_ret_out", "w_o", "ln1_g", "ln1_b", "w_ffn_in", "conv_w", "conv_b", "w_ffn_out", "ln2_g",
        "ln2_b"]
_OUTS = [(1, SEQ, D), (DEC, 1, D), (1, 1, SEQ + META, KVL), (1, 1, SEQ + META, ROPE), (1, 1, RH, RD, RD),
         (1, 1, 2, DFF), (1, DEC, 1, KVL), (1, DEC, 1, ROPE), (1, DEC, RH, RD, RD), (1, DEC, 2, DFF)]


def kernel(**inputs):
    import numpy as _np
    import concourse.bacc as _bacc
    from concourse import mybir as _mybir
    from concourse.bass_utils import run_bass_kernel_spmd as _run

    nc = _bacc.Bacc("TRN2", target_bir_lowering=False, num_devices=1)
    arrays, ins, outs = {}, {}, []
    for name in _INS:
        a = _np.ascontiguousarray(inputs[name])
        arrays[f"in_{name}_dram"] = a
        ins[name] = nc.dram_tensor(f"in_{name}_dram", a.shape, _mybir.dt.from_np(a.dtype), kind="ExternalInput").ap()
    for i, shape in enumerate(_OUTS):
        outs.append(nc.dram_tensor(f"out_{i}_dram", shape, _mybir.dt.float32, kind="ExternalOutput").ap())
    build(nc, ins, outs)
    r = _run(nc, [arrays], core_ids=[0])
    return tuple(r.results[0][f"out_{i}_dram"] for i in range(len(_OUTS)))
```
